# Optimizing a Trainium2 kernel written in Bass

```python
import math
import jax, jax.numpy as jnp
from jax import lax
import numpy as np

D_MODEL = 2048
BATCH = 1
SEQ = 256
DEPTH = 1

DN_HEADS = 8
DN_DK = 128
DN_DV = 128
CONV_W = 4
RET_HEADS = 8
RET_DK = 64
RET_DV = 128
CHUNK = 64
ROPE_BASE = 10000.0
N_KEYS = 128
N_EXPERTS = N_KEYS * N_KEYS
PK_HEADS = 8
PK_DQ = 256
PK_TOPK = 16
TOK_BLOCK = 128
PLE_DIM = 256
EPS = 1e-6

DN_QK = DN_HEADS * DN_DK
DN_V = DN_HEADS * DN_DV
CONV_CH = 2 * DN_QK + DN_V
RET_QK = RET_HEADS * RET_DK
RET_V = RET_HEADS * RET_DV
D_MIX = DN_V + RET_V
SPLIT_SIZES = (CONV_CH, DN_V, DN_HEADS, DN_HEADS, RET_QK, RET_QK, RET_V, RET_V)
IN_COLS = CONV_CH + DN_V + 2 * DN_HEADS + 2 * RET_QK + 2 * RET_V

kernel_name = "hybrid_deltanet_retention_peer_block"

def rms_norm(x, w):
    xf = x.astype(jnp.float32)
    y = xf * lax.rsqrt(jnp.mean(xf * xf, axis=-1, keepdims=True) + EPS)
    return (y * w.astype(jnp.float32)).astype(x.dtype)

def l2norm(x):
    return x * lax.rsqrt(jnp.sum(x * x, axis=-1, keepdims=True) + EPS)

def causal_conv_silu(x, w):
    s = x.shape[1]
    xp = jnp.pad(x, ((0, 0), (CONV_W - 1, 0), (0, 0)))
    y = sum(xp[:, j:j + s, :] * w[:, j] for j in range(CONV_W))
    return jax.nn.silu(y)

def rotary(x, positions):
    half = x.shape[-1] // 2
    inv_freq = ROPE_BASE ** (-jnp.arange(half, dtype=jnp.float32) / half)
    ang = positions.astype(jnp.float32)[..., None] * inv_freq
    cos = jnp.cos(ang)[:, :, None, :]
    sin = jnp.sin(ang)[:, :, None, :]
    x1, x2 = x[..., :half], x[..., half:]
    return jnp.concatenate([x1 * cos - x2 * sin, x1 * sin + x2 * cos], axis=-1)

def _chunks(t, n):
    b, _, h = t.shape[:3]
    t = t.reshape((b, n, CHUNK, h) + t.shape[3:])
    return jnp.moveaxis(t, 3, 1)

def _unchunk(t):
    b, h, n, c = t.shape[:4]
    return jnp.moveaxis(t, 1, 3).reshape((b, n * c, h) + t.shape[4:])

def gated_delta_rule(q, k, v, g, beta):
    b, s, h, dk = q.shape
    dv = v.shape[-1]
    n = s // CHUNK
    q, k, v, g, beta = (_chunks(t, n) for t in (q, k, v, g, beta))
    g = jnp.cumsum(g, axis=-1)
    causal = jnp.tril(jnp.ones((CHUNK, CHUNK), dtype=bool))
    strict = jnp.tril(jnp.ones((CHUNK, CHUNK), dtype=bool), -1)
    decay = jnp.exp(jnp.where(causal, g[..., :, None] - g[..., None, :], -jnp.inf))
    k_beta = k * beta[..., None]
    kk = jnp.einsum('bhncd,bhnmd->bhncm', k_beta, k) * decay
    a_mat = jnp.where(strict, kk, 0.0) + jnp.eye(CHUNK, dtype=q.dtype)
    rhs = jnp.concatenate([v * beta[..., None], k_beta * jnp.exp(g)[..., None]], axis=-1)
    sol = lax.linalg.triangular_solve(a_mat, rhs, left_side=True, lower=True, unit_diagonal=True)
    u, w = sol[..., :dv], sol[..., dv:]
    attn = jnp.einsum('bhncd,bhnmd->bhncm', q, k) * decay

    def step(state, xs):
        q_c, k_c, u_c, w_c, g_c, attn_c = xs
        v_new = u_c - jnp.einsum('bhck,bhkv->bhcv', w_c, state)
        o_c = (jnp.einsum('bhck,bhkv->bhcv', q_c * jnp.exp(g_c)[..., None], state)
               + jnp.einsum('bhcm,bhmv->bhcv', attn_c, v_new))
        g_end = g_c[..., -1:]
        state = (state * jnp.exp(g_end)[..., None]
                 + jnp.einsum('bhck,bhcv->bhkv', k_c * jnp.exp(g_end - g_c)[..., None], v_new))
        return state, o_c

    state0 = jnp.zeros((b, h, dk, dv), q.dtype)
    xs = tuple(jnp.moveaxis(t, 2, 0) for t in (q, k, u, w, g, attn))
    _, out = lax.scan(step, state0, xs)
    return _unchunk(jnp.moveaxis(out, 0, 2))

def retention_chunked(q, k, v):
    b, s, h, dk = q.shape
    dv = v.shape[-1]
    n = s // CHUNK
    q, k, v = (_chunks(t, n) for t in (q, k, v))
    log_gamma = jnp.log1p(-jnp.exp2(-5.0 - jnp.arange(RET_HEADS, dtype=jnp.float32)))
    pos = jnp.arange(CHUNK, dtype=jnp.float32)
    rel = pos[:, None] - pos[None, :]
    d_mat = jnp.exp(jnp.where(rel >= 0, rel * log_gamma[:, None, None], -jnp.inf))
    attn = jnp.einsum('bhncd,bhnmd->bhncm', q, k) * d_mat[None, :, None]
    inner = jnp.einsum('bhncm,bhnmv->bhncv', attn, v)
    xi = jnp.exp((pos + 1.0) * log_gamma[:, None])[None, :, :, None]
    zeta = jnp.exp((CHUNK - 1.0 - pos) * log_gamma[:, None])[None, :, :, None]
    chunk_decay = jnp.exp(CHUNK * log_gamma)[None, :, None, None]

    def step(state, xs):
        q_c, k_c, v_c = xs
        cross = jnp.einsum('bhck,bhkv->bhcv', q_c, state) * xi
        state = state * chunk_decay + jnp.einsum('bhck,bhcv->bhkv', k_c * zeta, v_c)
        return state, cross

    state0 = jnp.zeros((b, h, dk, dv), q.dtype)
    xs = tuple(jnp.moveaxis(t, 2, 0) for t in (q, k, v))
    _, cross = lax.scan(step, state0, xs)
    return _unchunk(inner + jnp.moveaxis(cross, 0, 2))

def peer(xn, w_pq, sub_keys, expert_u, expert_v):
    b, s, d = xn.shape
    t = b * s
    xt = xn.reshape(t, d)
    q = (xt @ w_pq).reshape(t, PK_HEADS, 2, PK_DQ // 2)
    scores = jnp.einsum('thpc,hpnc->thpn', q, sub_keys).astype(jnp.float32)
    s1, i1 = lax.top_k(scores[:, :, 0], PK_TOPK)
    s2, i2 = lax.top_k(scores[:, :, 1], PK_TOPK)
    cand_s = (s1[..., :, None] + s2[..., None, :]).reshape(t, PK_HEADS, PK_TOPK * PK_TOPK)
    cand_i = (i1[..., :, None] * N_KEYS + i2[..., None, :]).reshape(t, PK_HEADS, PK_TOPK * PK_TOPK)
    top_s, sel = lax.top_k(cand_s, PK_TOPK)
    idx = jnp.take_along_axis(cand_i, sel, axis=-1)
    gates = jax.nn.softmax(top_s, axis=-1)
    nb = t // TOK_BLOCK
    idx = idx.reshape(nb, TOK_BLOCK, PK_HEADS * PK_TOPK)
    gates = gates.reshape(nb, TOK_BLOCK, PK_HEADS * PK_TOPK)
    xb = xt.reshape(nb, TOK_BLOCK, d)

    def block(args):
        x_blk, i_blk, g_blk = args
        pre = jnp.einsum('tkd,td->tk', expert_u[i_blk], x_blk).astype(jnp.float32)
        act = jax.nn.gelu(pre, approximate=False) * g_blk
        return jnp.einsum('tk,tkd->td', act.astype(x_blk.dtype), expert_v[i_blk])

    out = lax.map(block, (xb, idx, gates))
    return out.reshape(b, s, d)

def setup_inputs(seed: int = 0) -> dict:
    key = jax.random.key(seed)
    ks = jax.random.split(key, 24)
    f32 = jnp.float32

    def nrm(k, shape, scale):
        return jax.random.normal(k, shape, f32) * scale

    def gain(k, shape):
        return 1.0 + 0.02 * jax.random.normal(k, shape, f32)

    L = DEPTH
    x = nrm(ks[0], (BATCH, SEQ, D_MODEL), 1.0)
    p = nrm(ks[1], (L, BATCH, SEQ, PLE_DIM), 1.0)
    positions = (jax.random.randint(ks[2], (BATCH, 1), 0, 1024, dtype=jnp.int32)
                 + jnp.arange(SEQ, dtype=jnp.int32)[None, :])
    norm_mix = gain(ks[3], (L, D_MODEL))
    w_in = nrm(ks[4], (L, D_MODEL, IN_COLS), D_MODEL ** -0.5)
    conv_w = nrm(ks[5], (L, CONV_CH, CONV_W), CONV_W ** -0.5)
    a_log = jnp.log(jax.random.uniform(ks[6], (L, DN_HEADS), f32, 1.0, 16.0))
    dt = jnp.exp(jax.random.uniform(ks[7], (L, DN_HEADS), f32, math.log(1e-3), math.log(1e-1)))
    dt_bias = dt + jnp.log(-jnp.expm1(-dt))
    dn_norm = gain(ks[8], (L, DN_DV))
    ret_gn_w = gain(ks[9], (L, RET_V))
    ret_gn_b = nrm(ks[10], (L, RET_V), 0.02)
    w_out = nrm(ks[11], (L, D_MIX, D_MODEL), D_MIX ** -0.5)
    norm_ffn = gain(ks[12], (L, D_MODEL))
    w_pq = nrm(ks[13], (L, D_MODEL, PK_HEADS * PK_DQ), D_MODEL ** -0.5)
    sub_keys = nrm(ks[14], (L, PK_HEADS, 2, N_KEYS, PK_DQ // 2), (PK_DQ // 2) ** -0.5)
    expert_u = nrm(ks[15], (L, N_EXPERTS, D_MODEL), D_MODEL ** -0.5)
    expert_v = nrm(ks[16], (L, N_EXPERTS, D_MODEL), PK_HEADS ** -0.5)
    norm_ple = gain(ks[17], (L, D_MODEL))
    w_ple_gate = nrm(ks[18], (L, D_MODEL, D_MODEL), D_MODEL ** -0.5)
    w_ple_proj = nrm(ks[19], (L, PLE_DIM, D_MODEL), PLE_DIM ** -0.5)
    norm_final = gain(ks[20], (D_MODEL,))
    return {"x": x, "p": p, "positions": positions, "norm_mix": norm_mix, "w_in": w_in,
            "conv_w": conv_w, "a_log": a_log, "dt_bias": dt_bias, "dn_norm": dn_norm,
            "ret_gn_w": ret_gn_w, "ret_gn_b": ret_gn_b, "w_out": w_out, "norm_ffn": norm_ffn,
            "w_pq": w_pq, "sub_keys": sub_keys, "expert_u": expert_u, "expert_v": expert_v,
            "norm_ple": norm_ple, "w_ple_gate": w_ple_gate, "w_ple_proj": w_ple_proj,
            "norm_final": norm_final}

def reference(x, p, positions, norm_mix, w_in, conv_w, a_log, dt_bias, dn_norm, ret_gn_w, ret_gn_b,
              w_out, norm_ffn, w_pq, sub_keys, expert_u, expert_v, norm_ple, w_ple_gate, w_ple_proj,
              norm_final):
    f32 = jnp.float32
    b, s, _ = x.shape
    splits = [int(c) for c in np.cumsum(SPLIT_SIZES)[:-1]]
    h = x
    for i in range(DEPTH):
        hn = rms_norm(h, norm_mix[i])
        proj = jnp.einsum('bsd,dc->bsc', hn, w_in[i]).astype(f32)
        conv_in, dn_z, dn_a, dn_b, r_q, r_k, r_v, r_g = jnp.split(proj, splits, axis=-1)

        qkv = causal_conv_silu(conv_in, conv_w[i].astype(f32))
        dq, dk, dv = jnp.split(qkv, [DN_QK, 2 * DN_QK], axis=-1)
        dq = l2norm(dq.reshape(b, s, DN_HEADS, DN_DK)) * (DN_DK ** -0.5)
        dk = l2norm(dk.reshape(b, s, DN_HEADS, DN_DK))
        dv = dv.reshape(b, s, DN_HEADS, DN_DV)
        beta = jax.nn.sigmoid(dn_b)
        g = -jnp.exp(a_log[i].astype(f32)) * jax.nn.softplus(dn_a + dt_bias[i].astype(f32))
        o_dn = gated_delta_rule(dq, dk, dv, g, beta)
        o_dn = rms_norm(o_dn, dn_norm[i]) * jax.nn.silu(dn_z.reshape(b, s, DN_HEADS, DN_DV))
        o_dn = o_dn.reshape(b, s, DN_V)

        rq = rotary(r_q.reshape(b, s, RET_HEADS, RET_DK), positions)
        rk = rotary(r_k.reshape(b, s, RET_HEADS, RET_DK), positions) * (RET_DK ** -0.5)
        rv = r_v.reshape(b, s, RET_HEADS, RET_DV)
        o_r = retention_chunked(rq, rk, rv)
        mu = jnp.mean(o_r, axis=-1, keepdims=True)
        var = jnp.mean(jnp.square(o_r - mu), axis=-1, keepdims=True)
        o_r = ((o_r - mu) * lax.rsqrt(var + EPS)).reshape(b, s, RET_V)
        o_r = (o_r * ret_gn_w[i].astype(f32) + ret_gn_b[i].astype(f32)) * jax.nn.silu(r_g)

        mixed = jnp.concatenate([o_dn, o_r], axis=-1).astype(h.dtype)
        h = h + jnp.einsum('bsc,cd->bsd', mixed, w_out[i])

        hn = rms_norm(h, norm_ffn[i])
        h = h + peer(hn, w_pq[i], sub_keys[i], expert_u[i], expert_v[i])

        gate = jax.nn.sigmoid((rms_norm(h, norm_ple[i]) @ w_ple_gate[i]).astype(f32))
        ple = (p[i] @ w_ple_proj[i]).astype(f32)
        h = h + (gate * ple).astype(h.dtype)
    return rms_norm(h, norm_final)


_drawn_inputs = setup_inputs


def setup_inputs(seed=0):
    import zlib

    import numpy as np

    out = dict(_drawn_inputs(seed))
    spreads = {}
    factors = {'dn_norm': 11.183,
     'ret_gn_w': 11.174,
     'ret_gn_b': 11.436,
     'norm_ffn': 7.489,
     'norm_ple': 64.0,
     'norm_final': 8.27}
    for name, (base, spread) in spreads.items():
        noise = np.random.default_rng([zlib.crc32(name.encode()), seed]).standard_normal(out[name].shape)
        drawn = base * np.exp(spread * noise) if base else spread * noise
        out[name] = __import__('jax').numpy.asarray(drawn.astype(out[name].dtype))
    for name, factor in factors.items():
        out[name] = (out[name] * factor).astype(out[name].dtype)
    return out
```

```python
from contextlib import ExitStack

import numpy as np

import concourse.bass as bass
from concourse import mybir

F32 = mybir.dt.float32
F32R = mybir.dt.float32r
BF16 = mybir.dt.bfloat16
I32 = mybir.dt.int32
U32 = mybir.dt.uint32
ALU = mybir.AluOpType
ACT = mybir.ActivationFunctionType
AX_X = mybir.AxisListType.X
ds = bass.ds

P = 128
SEQ = 256
TB = SEQ // P
D = 2048
DC = D // P
DN_HEADS, DK = 8, 128
RET_HEADS, RET_DK, RET_DV = 8, 64, 128
HALF = RET_DK // 2
CONV_CH = 3 * DN_HEADS * DK
CONV_W = 4
N_KEYS = 128
PK_HEADS = 8
TOPK = 16
PLE = 256
ALL_CONSTS = 16 * 10
EPS = 1e-6
MASKED = -1e30
LOWEST = -3.0e38
TOPK_CHUNKS = 48
GROUPS = SEQ // 4
HALF_KEYS = N_KEYS // 2
TWO_PI = 6.283185307179586
TWO_PI_PARTS = (6.28125, 0.001934051513671875, 1.2556659146142806e-06)
PI_BELOW = 3.1415925
ROUNDER = 12582912.0
LEVELS = 7

TILE = 1024
RAW = 4
SPLIT = 2
CONV_CHUNKS = CONV_CH // P
RQK_CHUNKS = 2 * RET_HEADS * RET_DK // P
IN_CHUNKS = CONV_CHUNKS + RQK_CHUNKS
ROW_GROUPS = 6
T_ROW = 2 * IN_CHUNKS
T_OUT = T_ROW + 8 * ROW_GROUPS
T_PQ = T_OUT + 8 * D // 512
PQ_CHUNKS = PK_HEADS * 2
T_U = T_PQ + 2 * PQ_CHUNKS
CHUNKS = N_KEYS
T_V = T_U + 2 * CHUNKS
T_PLE = T_V + 2 * CHUNKS
T_GATE = T_PLE + 4
T_END = T_GATE + 8 * D // 512

TAKEN_OUT = IN_CHUNKS + ROW_GROUPS + D // 512
TAKEN_H = TAKEN_OUT + PQ_CHUNKS + 2 * TB
TAKEN_PLE = TAKEN_H + 4

C_IDENT, C_IOTA, C_INVF = 0, 128, 256
C_KEEP = 257
C_LEVEL = 0
C_NEGA = C_LEVEL + LEVELS * P
C_NEGD = C_NEGA + P
C_RETD = C_NEGD + P
C_MIX = C_RETD + RET_HEADS * 3 * P


def shape_consts():
    i = np.arange(P)
    keep = np.zeros((P, C_KEEP), np.float32)
    keep[:, C_IDENT:C_IDENT + P] = np.eye(P)
    keep[:, C_IOTA:C_IOTA + P] = i[None, :]
    half = np.arange(HALF, dtype=np.float32)
    inv_freq = np.float32(10000.0) ** (-half / np.float32(HALF))
    keep[:, C_INVF] = inv_freq[i % HALF]
    mix = np.zeros((P, C_MIX), np.float32)
    for level in range(LEVELS):
        a, b = i[:, None] >> level, i[None, :] >> level
        mix[:, C_LEVEL + level * P:C_LEVEL + (level + 1) * P] = (a == b + 1) & (b % 2 == 0)
    mix[:, C_NEGA:C_NEGA + P] = np.where(i[:, None] > i[None, :], 0.0, MASKED)
    mix[:, C_NEGD:C_NEGD + P] = np.where(i[None, :] >= i[:, None], 0.0, MASKED)
    log_gamma = np.log1p(-np.exp2(-5.0 - np.arange(RET_HEADS)))
    rel = (i[None, :] - i[:, None]).astype(np.float64)
    for h in range(RET_HEADS):
        near = np.where(rel >= 0, np.exp(np.maximum(rel, 0) * log_gamma[h]), 0.0)
        far = np.exp((rel + P) * log_gamma[h])
        d = np.concatenate([near, far, near], axis=1) * RET_DK ** -0.5
        mix[:, C_RETD + h * 3 * P:C_RETD + (h + 1) * 3 * P] = d
    return keep, mix


def build(nc, x, w_in_cols, w_in_rows, w_ab, w_out, w_pq, expert_u, expert_v, w_gate, w_ple, p_t,
          positions, keep_c, mix_c, norm_cols, conv_cols, sub_keys_t, ab_cols, dn_norm, ret_gn_w,
          ret_gn_b, norm_final, out, h_spill):
    with ExitStack() as ctx:
        def sb(name, shape, dt=F32):
            return ctx.enter_context(nc.sbuf_tensor(name, shape, dt))

        def sem(name):
            return ctx.enter_context(nc.semaphore(name))

        arena = sb("arena", [P, CHUNKS * SEQ])
        raw = sb("raw", [P, RAW, TILE])
        hi = sb("hi", [P, SPLIT, TILE], F32R)
        lo = sb("lo", [P, SPLIT, TILE], F32R)
        act_hi = sb("act_hi", [P, DC, SEQ], F32R)
        act_lo = sb("act_lo", [P, DC, SEQ], F32R)
        stage_hi = sb("stage_hi", [P, 2, SEQ], F32R)
        stage_lo = sb("stage_lo", [P, 2, SEQ], F32R)
        keep = sb("keep", [P, C_KEEP])
        ncol = sb("ncol", [P, 3, DC])
        sel1_t = sb("sel1_t", [P, SEQ])
        sel2_t = sb("sel2_t", [P, SEQ])
        gate_t = sb("gate_t", [P, SEQ])
        ab_col = sb("ab_col", [8, 4])
        gate_parts = sb("gate_parts", [P, 3, SEQ], BF16)
        onehot1 = sb("onehot1", [P, 2, 4, N_KEYS], BF16)
        onehot2 = sb("onehot2", [P, 2, 4, 3, HALF_KEYS], BF16)
        equal2_t = sb("equal2", [P, 4 * HALF_KEYS], BF16)
        sel4 = sb("sel4", [P, 2, 4])
        stat = sb("stat", [P, 16])
        one = sb("one", [P, 2])
        ps = ctx.enter_context(nc.psum_tensor("ps", [P, 8, 512], F32))
        ident = keep[:, C_IDENT:C_IDENT + P]
        iota = keep[:, C_IOTA:C_IOTA + P]

        mixer_small = onehot1[:].rearrange("p a b c -> p (a b c)").bitcast(F32)
        dn_w, ones_m = mixer_small[:, 0:P], mixer_small[:, P:2 * P]

        def region(start, *shape):
            n = int(np.prod(shape))
            v = arena[:, start:start + n]
            if len(shape) == 1:
                return v
            names = "abcd"[:len(shape)]
            return v.rearrange("p (" + " ".join(names) + ") -> p " + " ".join(names),
                               **dict(zip(names[1:], shape[1:])))

        xh = region(0, TB, D)
        xn = region(4096, TB, D)
        qkv = region(8192, 24, SEQ)
        rqk = region(14336, 8, SEQ)
        rows = region(16384, ROW_GROUPS, TB, 512)
        conv_y = region(22528, 2, SEQ)
        squares = region(22528, 2, 512)
        roots = region(23552, 512)
        ab_w = region(23040, DC, 64)
        conv_w = region(24064, CONV_CHUNKS * CONV_W)
        pos_i = region(24160, SEQ).bitcast(I32)
        mixc = region(24448, C_MIX)
        mixed = region(28672, TB, D)

        weights_landed = [sem(f"weights_landed{i}") for i in range(RAW)]
        hi_ready, lo_ready = sem("hi_ready"), sem("lo_ready")
        hi_used, lo_used = sem("hi_used"), sem("lo_used")
        held = {e: sem(f"held_{e}") for e in ("act", "dve", "pool")}
        x_landed, consts_landed = sem("x_landed"), sem("consts_landed")
        ones_ready = sem("ones_ready")

        def hold(eng, name, s, value):
            eng.wait_ge(s, value)
            eng.sem_inc(held[name], 1)

        def load_tile(sp, n, slot, src, first=False):
            if not first:
                sp.wait_ge(lo_ready, n - RAW + 1)
            sp.dma_start(raw[:, slot, :], src).then_inc(weights_landed[slot], 16)

        def round_tile(act, n, slot, use, turn, first=False):
            act.wait_ge(weights_landed[slot], 16 * turn + 16)
            if not first:
                act.wait_ge(hi_used, n - SPLIT + 1)
                act.wait_ge(lo_ready, n - SPLIT + 1)
            act.activation(hi[:, use, :], raw[:, slot, :], ACT.Copy).then_inc(hi_ready, 1)

        def rest_tile(dve, n, slot, use, first=False):
            dve.wait_ge(hi_ready, n + 1)
            if not first:
                dve.wait_ge(lo_used, n - SPLIT + 1)
            dve.tensor_tensor(lo[:, use, :], raw[:, slot, :], hi[:, use, :].bitcast(F32),
                              ALU.subtract).then_inc(lo_ready, 1)

        def tile_at(base, i, per, k):
            assert base % RAW == 0 and per % RAW == 0
            return (base + k + per * i, (base + k) % RAW, (base + k) % SPLIT,
                    (base + k) // RAW + (per // RAW) * i)

        def column_tile(pe, n, use, k, out_ap):
            pe.wait_ge(hi_ready, n + 1)
            for d8 in range(8):
                w, d = hi[:, use, d8 * P:(d8 + 1) * P], 8 * k + d8
                pe.matmul(out_ap, w, act_hi[:, d, :], start=(d == 0), stop=False)
                mm = pe.matmul(out_ap, w, act_lo[:, d, :], start=False, stop=False)
            mm.then_inc(hi_used, 1)
            pe.wait_ge(lo_ready, n + 1)
            for d8 in range(8):
                mm = pe.matmul(out_ap, lo[:, use, d8 * P:(d8 + 1) * P], act_hi[:, 8 * k + d8, :],
                               start=False, stop=(k == 1 and d8 == 7))
            mm.then_inc(lo_used, 1)

        def row_tile(pe, n, use, k, outs, a_hi=None, a_lo=None, last=7):
            a_hi = act_hi if a_hi is None else a_hi
            a_lo = act_lo if a_lo is None else a_lo
            pe.wait_ge(hi_ready, n + 1)
            for tb in range(TB):
                for k2 in range(2):
                    w, d, t = hi[:, use, k2 * 512:(k2 + 1) * 512], 2 * k + k2, slice(tb * P, tb * P + P)
                    pe.matmul(outs[tb], a_hi[:, d, t], w, start=(d == 0), stop=False)
                    mm = pe.matmul(outs[tb], a_lo[:, d, t], w, start=False, stop=False)
            mm.then_inc(hi_used, 1)
            pe.wait_ge(lo_ready, n + 1)
            for tb in range(TB):
                for k2 in range(2):
                    mm = pe.matmul(outs[tb], a_hi[:, 2 * k + k2, tb * P:tb * P + P],
                                   lo[:, use, k2 * 512:(k2 + 1) * 512], start=False,
                                   stop=(k == last and k2 == 1))
            mm.then_inc(lo_used, 1)

        met = [sem(f"phase_done{i}") for i in range(12)]

        def meet(eng, i):
            eng.drain().then_inc(met[i], 1)
            eng.wait_ge(met[i], 4)

        squares_summed, mean_ready, root_ready = sem("squares_summed"), sem("mean_ready"), sem("root_ready")
        scale_ready, normed, turned, act_hi_ready = (sem("scale_ready"), sem("normed"), sem("turned"),
                                                     sem("act_hi_ready"))

        def act_norm(act, n, h):
            for tb in range(TB):
                act.activation(xn_of[n][:, tb, :], h[:, tb, :], ACT.Square,
                               accum_out=stat[:, tb:tb + 1]).then_inc(squares_summed, 1)
            act.wait_ge(mean_ready, n + 1)
            act.activation(stat[:, 4:6], stat[:, 2:4], ACT.Sqrt).then_inc(root_ready, 1)
            act.wait_ge(scale_ready, n + 1)
            act.activation(xn_of[n][:, 0, :], h[:, 0, :], ACT.Copy, scale=stat[:, 6:7]).then_inc(normed, 1)

        def dve_norm(dve, n, h):
            dve.wait_ge(squares_summed, 2 * n + 2)
            dve.tensor_scalar(stat[:, 2:4], stat[:, 0:2], 1.0 / D, EPS, ALU.mult, ALU.add).then_inc(mean_ready, 1)
            dve.wait_ge(root_ready, n + 1)
            dve.reciprocal(stat[:, 6:8], stat[:, 4:6]).then_inc(scale_ready, 1)
            dve.wait_ge(scale_ready, n + 1)
            dve.tensor_scalar(xn_of[n][:, 1, :], h[:, 1, :], stat[:, 7:8], None, ALU.mult).then_inc(normed, 1)

        def pe_turn(pe, rows_ap):
            for b in range(8):
                for k in range(4):
                    d, tb = 2 * b + k // 2, k % 2
                    mm = pe.transpose(ps[:, b, k * P:(k + 1) * P], rows_ap[:, tb, d * P:(d + 1) * P], ident)
                mm.then_inc(turned, 1)

        def act_turn(act, turn, w):
            for d in range(DC):
                act.wait_ge(turned, 8 * turn + d // 2 + 1)
                src = ps[:, d // 2, (d % 2) * SEQ:(d % 2 + 1) * SEQ]
                act.activation(act_hi[:, d, :], src, ACT.Copy,
                               scale=1.0 if w is None else ncol[:, w, d:d + 1]).then_inc(act_hi_ready, 1)

        def dve_turn(dve, turn, w):
            for d in range(DC):
                dve.wait_ge(act_hi_ready, DC * turn + 2 * (d // 2) + 2)
                src = ps[:, d // 2, (d % 2) * SEQ:(d % 2 + 1) * SEQ]
                dve.scalar_tensor_tensor(act_lo[:, d, :], src, 1.0 if w is None else ncol[:, w, d:d + 1],
                                         act_hi[:, d, :].bitcast(F32), ALU.mult, ALU.subtract)

        xn_of = {0: xn, 1: region(8192, TB, D), 2: region(8192, TB, D)}


        taken, ab_copied, selector_ready = sem("taken"), sem("ab_copied"), sem("selector_ready")
        conv_done, silu_done, ab_done = sem("conv_done"), sem("silu_done"), sem("ab_done")
        angles_ready, rows_out, rows_silu = sem("angles_ready"), sem("rows_out"), sem("rows_silu")
        trig_ready, q_rotated, k_rotated = sem("trig_ready"), sem("q_rotated"), sem("k_rotated")
        ret_scores, ret_masked, ret_out = sem("ret_scores"), sem("ret_masked"), sem("ret_out")
        ret_copied, ret_centered, ret_squared = sem("ret_copied"), sem("ret_centered"), sem("ret_squared")
        ret_var, ret_root, ret_scaled = sem("ret_var"), sem("ret_root"), sem("ret_scaled")
        ret_done = sem("ret_done")
        qk_squared, qk_summed, qk_root, qk_normed = (sem("qk_squared"), sem("qk_summed"), sem("qk_root"),
                                                     sem("qk_normed"))
        gate_in, gate_exp, gate_ln_in, gate_ln = sem("gate_in"), sem("gate_exp"), sem("gate_ln_in"), sem("gate_ln")
        decay_row, decay_col, decay_cols_ready = sem("decay_row"), sem("decay_col"), sem("decay_cols_ready")
        decay_exp = sem("decay_exp")
        decay_spread, expo_ready, decays_ready = sem("decay_spread"), sem("expo_ready"), sem("decays_ready")
        kv_turned, k_rows, v_rows = sem("kv_turned"), sem("k_rows"), sem("v_rows")
        kk_done, kk_used, att_done, att_used = sem("kk_done"), sem("kk_used"), sem("att_done"), sem("att_used")
        inv_init, blocks_ready = sem("inv_init"), sem("blocks_ready")
        inner_done, inner_copied, outer_done, inv_updated = (sem("inner_done"), sem("inner_copied"),
                                                             sem("outer_done"), sem("inv_updated"))
        rhs_ready, new_done, new_copied = sem("rhs_ready"), sem("new_done"), sem("new_copied")
        kd_ready, state_done, state_copied = sem("kd_ready"), sem("state_done"), sem("state_copied")
        from_state, q_state, q_state_copied = sem("from_state"), sem("q_state"), sem("q_state_copied")
        o_done, o_copied, o_squared, o_mean, o_root = (sem("o_done"), sem("o_copied"), sem("o_squared"),
                                                       sem("o_mean"), sem("o_root"))
        z_weighted = sem("z_weighted")
        mixed_ready, x_again, h_ready, h_spilled = sem("mixed_ready"), sem("x_again"), sem("h_ready"), sem("h_spilled")

        att_ret = region(0, RET_HEADS, 3 * P)
        sin_t, cos_t = region(3072, SEQ), region(3328, SEQ)
        angle, turns = region(3584, SEQ), region(3840, SEQ)
        rot = region(4096, 4, 2, SEQ)
        rot_tmp = region(6144, 4, 2, SEQ)
        ret_sq = region(0, TB, 1024)
        a_mat = region(0, 4, 4, P)
        inv = region(2048, 4, 4, P)
        inv_t = region(4096, 4, 4, P)
        blocks = region(6144, 4, 4, P)
        expo_a = region(6144, 4, 4, P)
        expo_d = region(18432, 4, 4, P)
        inner = region(18432, 4, 4, P)
        att = region(20480, 4, 4, P)
        k_row = region(14336, 4, 4, P)
        v_row = region(12288, 4, 4, P)
        rhs = region(6144, 4, 4, P)
        v_new = region(18432, 4, 4, P)
        state = region(0, 2, 4, P)
        k_dec = region(1024, 2, 4, P)
        q_out = region(2048, 2, 4, P)
        o_sq = region(4096, 4, 4, P)
        selector = region(22528, DN_HEADS, P)[0:8]
        gb = sel1_t
        tmp8 = sel2_t
        gcol = gate_t[:, 0:80].rearrange("p (b c) -> p b c", b=2)
        neg_g = gate_t[:, 80:96].rearrange("p (b c) -> p b c", b=2)
        exp_g = gate_t[:, 96:112].rearrange("p (b c) -> p b c", b=2)
        neg_beta_exp = gate_t[:, 112:120]
        end_dec = gate_t[:, 120:128]
        o_stat = gate_t[:, 128:176].rearrange("p (s g) -> p s g", s=3)
        ret_stat = gate_t[:, 176:176 + 64].rearrange("p (s b h) -> p s b h", s=4, b=2)
        g_end = gate_t[:, 240:248]

        query_t = region(12288, PQ_CHUNKS, SEQ)
        keys_t = region(26624 - 2048, PQ_CHUNKS, P)
        scores = region(28672, 16, 2, P)
        scores4 = region(28672, 8, 512)
        key_in, key_work = region(20480, 2, P), region(20736, 2, P)
        cand, cand_work = region(20992, TOPK, TOPK), region(21248, TOPK * TOPK)
        picked = region(21504, 2, TOPK, TOPK)
        key_top, key_index = region(22016, 2, TOPK), region(22048, 2, TOPK).bitcast(U32)
        key_index_f = region(22080, 2, TOPK)
        best, best_index = region(22112, TOPK), region(22128, TOPK).bitcast(U32)
        ranks, ranks_f = region(22144, 2, TOPK).bitcast(U32), region(22176, 2, TOPK)
        best_all = region(22528, 16, TOPK)
        picks_all = region(22784, 2, 16, TOPK)
        gates3, gates_all = region(23296, 16, TOPK), region(23296, 16 * TOPK)
        gate_sum = region(23552, 16)
        experts = region(0, CHUNKS, SEQ)
        equal2 = equal2_t[:].rearrange("p (t c) -> p t c", t=4)
        ple = region(12288, TB, D)
        p_rows = region(4096, 2, SEQ)
        gate_sig = region(17408, 2, TB, 512)
        final_w = region(20480, D)
        final = region(24576, TB, D)
        keys_landed, scores_done, scores_ready = sem("keys_landed"), sem("scores_done"), sem("scores_ready")
        expert_bank, gates_in, gates_exp, gates_ready = (sem("expert_bank"), sem("gates_in"), sem("gates_exp"),
                                                         sem("gates_ready"))
        sel_turned, sel_ready = sem("sel_turned"), sem("sel_ready")
        onehot1_ready, onehot2_ready = sem("onehot1_ready"), sem("onehot2_ready")
        gates_summed, gates_applied = sem("gates_summed"), sem("gates_applied")
        stage_hi_ready, stage_lo_ready = sem("stage_hi_ready"), sem("stage_lo_ready")
        h_back, p_landed, final_landed = sem("h_back"), sem("p_landed"), sem("final_landed")
        sigmoid_ready, out_ready, out_stored = (sem("sigmoid_ready"), sem("out_ready"), sem("out_stored"))

        psg = ps[:].rearrange("p b (j n) -> p b j n", j=4)
        ps2 = ps[:, 0:4, :].rearrange("p (b c) n -> p b (c n)", b=2)
        spread = ps[:, 4:8, :].rearrange("p b (c t) -> p (b c) t", c=2)
        qkv2 = region(8192, 8, 512)
        neg_a = mixc[:, C_NEGA:C_NEGA + P].unsqueeze(1)
        neg_d = mixc[:, C_NEGD:C_NEGD + P].unsqueeze(1)
        level_mask = mixc[:, 0:LEVELS * P].rearrange("p (l n) -> p l n", l=LEVELS)
        ret_decay = mixc[:, C_RETD:].rearrange("p (h n) -> p h n", h=RET_HEADS)
        eps_c = one[:, 1:2]
        trig_k, trig_p = region(6144, SEQ), region(6400, SEQ)

        def channel(what, g, j):
            b = g // 2
            return qkv[:, 8 * what + 4 * (g % 2) + j, b * P:(b + 1) * P]

        def o_rows(g):
            return mixed[:, g // 2, (g % 2) * 512:(g % 2 + 1) * 512].rearrange("p (j n) -> p j n", j=4)

        def rotate(eng, at):
            x1, x2 = rqk[:, 2 * at:2 * at + 2], rqk[:, 2 * at + 2:2 * at + 4]
            sin_b, cos_b = (t.unsqueeze(1).broadcast_to([P, 2, SEQ]) for t in (sin_t, cos_t))
            t1, t2 = rot_tmp[:, at], rot_tmp[:, at + 1]
            for out_ap, f1, f2, op in ((rot[:, at], cos_b, sin_b, ALU.subtract), (rot[:, at + 1], sin_b, cos_b, ALU.add)):
                eng.tensor_tensor(t1, x1, f1, ALU.mult)
                eng.tensor_tensor(t2, x2, f2, ALU.mult)
                eng.drain()
                e = eng.tensor_tensor(out_ap, t1, t2, op)
                eng.drain()
            return eng.drain()

        def take_ple(dve, g):
            dve.wait_ge(lo_used, T_PLE + g + 1)
            dve.tensor_copy(ple[:, :, 512 * g:512 * (g + 1)],
                            ps[:, 2 - 2 * (g % 2):4 - 2 * (g % 2), :]).then_inc(taken, 1)

        def start_of_stream(base, i, c):
            return base == 0 and isinstance(i, int) and i == 0 and c == 0

        block = ctx.enter_context(nc.Block())

        @block.sync
        def _(sp):
            sp.dma_start(xh, x.rearrange("(b p) d -> p b d", p=P)).then_inc(x_landed, 16)
            sp.dma_start(keep[:], keep_c).then_inc(consts_landed, 16)
            sp.dma_start(ncol[:], norm_cols).then_inc(consts_landed, 16)
            for k in range(RAW):
                load_tile(sp, k, k, w_in_cols[k], first=True)
            sp.dma_start(conv_w, conv_cols).then_inc(consts_landed, 16)
            sp.dma_start(ab_w, w_ab).then_inc(consts_landed, 16)
            sp.dma_start(mixc, mix_c).then_inc(consts_landed, 16)
            sp.dma_start(ab_col[:, 0:2], ab_cols).then_inc(consts_landed, 16)
            sp.dma_start(dn_w, dn_norm.partition_broadcast(P)).then_inc(consts_landed, 16)
            sp.dma_start(mixed[:, 0, 0:1024], ret_gn_w.partition_broadcast(P)).then_inc(consts_landed, 16)
            sp.dma_start(mixed[:, 1, 0:1024], ret_gn_b.partition_broadcast(P)).then_inc(consts_landed, 16)
            sp.dma_start(pos_i, positions.partition_broadcast(P)).then_inc(consts_landed, 16)

            def stream(base, source, start, stop):
                with sp.Fori(start, stop) as i:
                    for k in range(RAW):
                        n, slot, _, _ = tile_at(base, i, RAW, k)
                        load_tile(sp, n, slot, source[ds(i * RAW + k, 1)].rearrange("a p f -> (a p) f"))

            stream(0, w_in_cols, 1, T_ROW // RAW)
            stream(T_ROW, w_in_rows, 0, (T_OUT - T_ROW) // RAW)
            stream(T_OUT, w_out, 0, (T_PQ - T_OUT) // RAW)
            stream(T_PQ, w_pq, 0, (T_U - T_PQ) // RAW)
            stream(T_U, expert_u, 0, (T_V - T_U) // RAW)
            stream(T_V, expert_v, 0, (T_PLE - T_V) // RAW)
            stream(T_PLE, w_ple, 0, 1)
            stream(T_GATE, w_gate, 0, (T_END - T_GATE) // RAW)
            for tb in range(TB):
                sp.wait_ge(out_ready, tb + 1)
                sp.dma_start(out[tb * P:(tb + 1) * P, :], final[:, tb]).then_inc(out_stored, 16)
            sp.wait_ge(out_stored, 16 * TB)

        @block.scalar
        def _(act):
            act.wait_ge(x_landed, 16)
            act_norm(act, 0, xh)
            act.wait_ge(consts_landed, ALL_CONSTS)
            act_turn(act, 0, 0)
            meet(act, 0)

            def silu_chunk(c, parity):
                hold(act, "act", taken, c + 1)
                act.activation(qkv[:, ds(c, 1), :], conv_y[:, parity:parity + 1, :], ACT.Silu).then_inc(silu_done, 1)

            def chunk_round(base, i, after):
                for c in range(2):
                    for k in range(2):
                        round_tile(act, *tile_at(base, i, 4, 2 * c + k), first=start_of_stream(base, i, c))
                    after(i, c)

            chunk_round(0, 0, lambda i, c: c and silu_chunk(0, 0))
            with act.Fori(1, CONV_CHUNKS // 2) as i:
                chunk_round(0, i, lambda i, c: silu_chunk(2 * i + c - 1, 1 - c))
            chunk_round(0, CONV_CHUNKS // 2, lambda i, c: c or silu_chunk(CONV_CHUNKS - 1, 1))
            with act.Fori(CONV_CHUNKS // 2 + 1, IN_CHUNKS // 2) as i:
                chunk_round(0, i, lambda i, c: None)
            with act.Fori(0, 2 * ROW_GROUPS) as i:
                for k in range(4):
                    round_tile(act, *tile_at(T_ROW, i, 4, k))
            meet(act, 1)

            act.activation(rows[:, 0:2], rows[:, 0:2], ACT.Silu).then_inc(rows_silu, 1)
            act.activation(rows[:, 4:6], rows[:, 4:6], ACT.Silu).then_inc(rows_silu, 1)
            act.wait_ge(angles_ready, 2)
            act.activation(sin_t, angle, ACT.Sin).then_inc(trig_ready, 1)
            act.activation(cos_t, turns, ACT.Sin).then_inc(trig_ready, 1)

            def l2_root(p):
                act.wait_ge(qk_summed, p + 1)
                if p >= 1:
                    act.wait_ge(qk_normed, p)
                act.activation(roots, ps[:, p % 2, :], ACT.Sqrt, bias=eps_c).then_inc(qk_root, 1)

            for p in range(8):
                if p >= 2:
                    act.wait_ge(qk_summed, p - 1)
                act.activation(squares[:, p % 2], qkv2[:, p], ACT.Square).then_inc(qk_squared, 1)
                if p >= 1:
                    l2_root(p - 1)
            l2_root(7)
            for tb in range(TB):
                act.wait_ge(ret_out, tb + 1)
                act.activation(mixed[:, tb, 1024:2048], ps2[:, tb], ACT.Copy).then_inc(ret_copied, 1)
            act.wait_ge(gate_in, 1)
            act.activation(tmp8[0:8, :], tmp8[0:8, :], ACT.Exp).then_inc(gate_exp, 1)
            act.activation(tmp8[32:40, :], tmp8[32:40, :], ACT.Exp, scale=-1.0).then_inc(gate_exp, 1)
            act.activation(ab_col[:, 2:3], ab_col[:, 0:1], ACT.Exp).then_inc(gate_exp, 1)
            act.wait_ge(gate_ln_in, 1)
            act.activation(tmp8[0:8, :], tmp8[0:8, :], ACT.Ln).then_inc(gate_ln, 1)
            for tb in range(TB):
                act.wait_ge(ret_centered, tb + 1)
                act.activation(ret_sq[:, tb], mixed[:, tb, 1024:2048], ACT.Square).then_inc(ret_squared, 1)
            act.wait_ge(decay_cols_ready, 1)
            act.activation(exp_g, gcol[:, :, 0:8], ACT.Exp).then_inc(decay_exp, 1)
            act.wait_ge(decay_cols_ready, 2)
            act.activation(end_dec, end_dec, ACT.Exp).then_inc(decay_exp, 1)
            act.wait_ge(ret_var, 1)
            act.activation(ret_stat[:, 2], ret_stat[:, 1], ACT.Sqrt).then_inc(ret_root, 1)
            for g in range(4):
                act.wait_ge(expo_ready, 2 * g + 2)
                for j in range(4):
                    h = 4 * (g % 2) + j
                    act.activation(expo_a[:, g, j], expo_a[:, g, j], ACT.Exp, bias=gcol[:, g // 2, h:h + 1])
                    e = act.activation(expo_d[:, g, j], expo_d[:, g, j], ACT.Exp, bias=neg_g[:, g // 2, h:h + 1])
                e.then_inc(decays_ready, 1)
            for g in range(4):
                act.wait_ge(kv_turned, 2 * g + 1)
                act.activation(k_row[:, g], psg[:, 2 * g], ACT.Copy).then_inc(k_rows, 1)
            with act.Fori(0, LEVELS) as level:
                for g in range(4):
                    act.wait_ge(inner_done, 4 * level + g + 1)
                    act.activation(inner[:, g], psg[:, g], ACT.Copy).then_inc(inner_copied, 1)
            act.wait_ge(inv_updated, 4 * LEVELS + 4)
            for j in range(8):
                e = act.activation(k_dec[:, j // 4, j % 4], k_row[:, j // 4, j % 4], ACT.Copy, scale=end_dec[:, j:j + 1])
            e.then_inc(kd_ready, 1)
            for g in range(2):
                act.wait_ge(state_done, g + 1)
                act.activation(state[:, g], psg[:, 4 + g], ACT.Copy).then_inc(state_copied, 1)
            for g in range(2):
                act.wait_ge(q_state, g + 1)
                for j in range(4):
                    h = 4 * g + j
                    e = act.activation(q_out[:, g, j], psg[:, 2 + g, j], ACT.Copy, scale=exp_g[:, 1, h:h + 1])
                e.then_inc(q_state_copied, 1)
            act.wait_ge(o_mean, 1)
            act.activation(o_stat[:, 2], o_stat[:, 1], ACT.Sqrt).then_inc(o_root, 1)
            meet(act, 2)
            act.dma_start(xn, x.rearrange("(b p) d -> p b d", p=P)).then_inc(x_again, 16)
            act_turn(act, 1, None)
            meet(act, 3)
            act.dma_start(keys_t, sub_keys_t).then_inc(keys_landed, 16)
            with act.Fori(0, (T_PQ - T_OUT) // RAW) as i:
                for k in range(4):
                    round_tile(act, *tile_at(T_OUT, i, 4, k))
            act.wait_ge(h_ready, 1)
            act.dma_start(h_spill.rearrange("(b p) d -> p b d", p=P), xh).then_inc(h_spilled, 16)
            act_norm(act, 1, xh)
            act_turn(act, 2, 1)
            meet(act, 4)
            with act.Fori(0, PQ_CHUNKS // 2) as i:
                for k in range(4):
                    round_tile(act, *tile_at(T_PQ, i, 4, k))
            for b in range(8):
                act.wait_ge(scores_done, b + 1)
                e = act.activation(scores4[:, b], ps[:, b, :], ACT.Copy).then_inc(scores_ready, 1)
            act.wait_ge(h_spilled, 16)
            act.wait_ge(scores_ready, 8)
            act.sem_inc(expert_bank, 2)

            def gelu_chunk(c, parity):
                hold(act, "act", lo_used, T_U + 2 * c + 2)
                act.activation(experts[:, ds(c, 1), :], ps[:, parity:parity + 1, 0:SEQ], ACT.Gelu).then_inc(expert_bank, 1)

            def expert_round(i, first=False):
                for c in range(2):
                    for k in range(2):
                        round_tile(act, *tile_at(T_U, i, 4, 2 * c + k))
                    if not (first and c == 0):
                        gelu_chunk(2 * i + c - 1, 1 - c)

            expert_round(0, first=True)
            with act.Fori(1, TOPK_CHUNKS // 2) as i:
                expert_round(i)
            act.wait_ge(gates_in, 1)
            act.activation(gates_all, gates_all, ACT.Exp).then_inc(gates_exp, 1)
            with act.Fori(TOPK_CHUNKS // 2, CHUNKS // 2) as i:
                expert_round(i)
            gelu_chunk(CHUNKS - 1, 1)

            def value_round(half, i):
                for c in range(4):
                    v = CHUNKS * half + 4 * i + c
                    hold(act, "act", lo_used, T_V + v - 1)
                    act.activation(stage_hi[:, c % 2:c % 2 + 1, :], experts[:, ds(4 * i + c, 1), :],
                                   ACT.Copy).then_inc(stage_hi_ready, 1)
                    round_tile(act, T_V + v, c % RAW, c % SPLIT, T_V // RAW + CHUNKS // RAW * half + i)

            act.wait_ge(gates_applied, GROUPS + 2)
            with act.Fori(0, CHUNKS // 8) as i:
                value_round(0, i)
            act.wait_ge(gates_applied, 2 * GROUPS + 2)
            with act.Fori(CHUNKS // 8, CHUNKS // 4) as i:
                value_round(0, i)
            with act.Fori(0, CHUNKS // 8) as i:
                value_round(1, i)
            act.wait_ge(stage_lo_ready, CHUNKS + CHUNKS // 2)
            act.dma_start(xh, h_spill.rearrange("(b p) d -> p b d", p=P)).then_inc(h_back, 16)
            act.dma_start(p_rows, p_t).then_inc(p_landed, 16)
            with act.Fori(CHUNKS // 8, CHUNKS // 4) as i:
                value_round(1, i)
            act.wait_ge(stage_lo_ready, 2 * CHUNKS)
            act.dma_start(final_w, norm_final.partition_broadcast(P)).then_inc(final_landed, 16)
            act.wait_ge(p_landed, 16)
            act.wait_ge(lo_used, T_PLE)
            act.activation(stage_hi[:], p_rows, ACT.Copy).then_inc(stage_hi_ready, 1)
            for k in range(4):
                round_tile(act, *tile_at(T_PLE, 0, 4, k))
            act.wait_ge(taken, TAKEN_H)
            act_norm(act, 2, xh)
            act_turn(act, 3, 2)
            meet(act, 5)

            def sigmoid_group(g, parity):
                hold(act, "act", lo_used, T_GATE + 8 * g + 8)
                hold(act, "act", taken, TAKEN_PLE + g - 1)
                act.activation(gate_sig[:, parity], ps[:, 2 - 2 * parity:4 - 2 * parity, :],
                               ACT.Sigmoid).then_inc(sigmoid_ready, 1)

            for i in range(2):
                for g in range(2):
                    for k in range(8):
                        round_tile(act, *tile_at(T_GATE, i, 16, 8 * g + k))
                        if k == 1 and (i, g) != (0, 0):
                            sigmoid_group(2 * i + g - 1, 1 - g)
            sigmoid_group(3, 1)
            for tb in range(TB):
                act.wait_ge(taken, TAKEN_PLE + 4)
                act.activation(xn_of[2][:, tb, :], xh[:, tb, :], ACT.Square,
                               accum_out=stat[:, tb:tb + 1]).then_inc(squares_summed, 1)
            act.wait_ge(mean_ready, 4)
            act.activation(stat[:, 4:6], stat[:, 2:4], ACT.Sqrt).then_inc(root_ready, 1)

        @block.vector
        def _(dve):
            dve.memset(ones_m, 1.0)
            dve.memset(eps_c, EPS)
            dve.wait_ge(x_landed, 16)
            dve_norm(dve, 0, xh)
            dve.wait_ge(consts_landed, ALL_CONSTS)
            dve_turn(dve, 0, 0)
            meet(dve, 0)

            def convolve(c, parity):
                if not (isinstance(c, int) and c < 2):
                    dve.wait_ge(silu_done, c - 1)
                dve.wait_ge(lo_used, 2 * c + 2)
                y, src = conv_y[:, parity, :], ps[:, parity, 0:SEQ]
                dve.tensor_scalar(y, src, conv_w[:, ds(4 * c + 3, 1)], None, ALU.mult)
                for s in range(1, CONV_W):
                    dve.drain()
                    e = dve.scalar_tensor_tensor(y[:, s:], src[:, 0:SEQ - s], conv_w[:, ds(4 * c + 3 - s, 1)],
                                                 y[:, s:], ALU.mult, ALU.add)
                e.then_inc(taken, 1)

            def copy_rqk(c, parity):
                dve.wait_ge(lo_used, 2 * c + 2)
                dve.tensor_scalar(rqk[:, ds(c - CONV_CHUNKS, 1), :], ps[:, parity:parity + 1, 0:SEQ], 1.0, None,
                                  ALU.mult).then_inc(taken, 1)

            def chunk_round(base, i, after):
                for c in range(2):
                    for k in range(2):
                        rest_tile(dve, *tile_at(base, i, 4, 2 * c + k)[:3], first=start_of_stream(base, i, c))
                    after(i, c)

            chunk_round(0, 0, lambda i, c: c and convolve(0, 0))
            chunk_round(0, 1, lambda i, c: convolve(2 * i + c - 1, 1 - c))
            with dve.Fori(2, CONV_CHUNKS // 2) as i:
                chunk_round(0, i, lambda i, c: convolve(2 * i + c - 1, 1 - c))
            chunk_round(0, CONV_CHUNKS // 2,
                        lambda i, c: copy_rqk(CONV_CHUNKS, 0) if c else convolve(CONV_CHUNKS - 1, 1))
            with dve.Fori(CONV_CHUNKS // 2 + 1, IN_CHUNKS // 2) as i:
                chunk_round(0, i, lambda i, c: copy_rqk(2 * i + c - 1, 1 - c))
            copy_rqk(IN_CHUNKS - 1, 1)

            def take_rows(g, parity):
                dve.wait_ge(lo_used, T_ROW + 8 * g + 8)
                dve.tensor_scalar(rows[:, ds(g, 1)].rearrange("p a b c -> p (a b) c"),
                                  ps[:, 2 - 2 * parity:4 - 2 * parity, :], 1.0, None, ALU.mult).then_inc(taken, 1)

            def group_round(base, i, take, first=False):
                for g in range(2):
                    for k in range(8):
                        rest_tile(dve, *tile_at(base, i, 16, 8 * g + k)[:3])
                        if k == 1 and not (first and g == 0):
                            take(2 * i + g - 1, 1 - g)

            group_round(T_ROW, 0, take_rows, first=True)
            with dve.Fori(1, ROW_GROUPS // 2) as i:
                group_round(T_ROW, i, take_rows)
            take_rows(ROW_GROUPS - 1, 1)
            meet(dve, 1)

            dve.tensor_copy(tmp8[0:64, :], ps[0:64, 4, 0:SEQ]).then_inc(ab_copied, 1)
            for p in range(8):
                dve.wait_ge(qk_root, p + 1)
                dve.reciprocal(roots, roots)
                dve.drain()
                dve.scalar_tensor_tensor(qkv2[:, p], qkv2[:, p], DK ** -0.5 if p < 4 else 1.0, roots,
                                         ALU.mult, ALU.mult).then_inc(qk_normed, 1)
            dve.wait_ge(qk_summed, 8)
            dve.drain()
            dve.tensor_copy(selector, ident[0:8, 0:8].unsqueeze(2).broadcast_to([8, 8, P])).then_inc(selector_ready, 1)
            dve.wait_ge(trig_ready, 2)
            rotate(dve, 0).then_inc(q_rotated, 1)
            for h in range(RET_HEADS):
                dve.wait_ge(ret_scores, h + 1)
                dve.tensor_tensor(att_ret[:, h], ps[:, h, 0:3 * P], ret_decay[:, h], ALU.mult).then_inc(ret_masked, 1)
            x8, m8 = tmp8[0:8, :], gb[0:8, :]
            dve.memset(gb[0:64, :], 0.0)
            dve.drain()
            dve.tensor_scalar(x8, x8, ab_col[:, 1:2], None, ALU.add)
            dve.drain()
            dve.tensor_scalar(m8, x8, 0.0, None, ALU.max)
            dve.drain()
            dve.scalar_tensor_tensor(x8, m8, -2.0, x8, ALU.mult, ALU.add).then_inc(gate_in, 1)
            dve.wait_ge(gate_exp, 3)
            dve.tensor_scalar(x8, x8, 1.0, None, ALU.add).then_inc(gate_ln_in, 1)
            dve.tensor_scalar(tmp8[32:40, :], tmp8[32:40, :], 1.0, None, ALU.add)
            dve.tensor_scalar(ab_col[:, 3:4], ab_col[:, 2:3], -1.0, None, ALU.mult)
            dve.drain()
            dve.reciprocal(gb[32:40, :], tmp8[32:40, :])
            dve.wait_ge(gate_ln, 1)
            dve.tensor_tensor(x8, x8, m8, ALU.add)
            dve.drain()
            dve.tensor_scalar(x8, x8, ab_col[:, 3:4], None, ALU.mult)
            dve.drain()
            for b in range(TB):
                e = dve.tensor_tensor_scan(gb[0:8, b * P:(b + 1) * P], ones_m[0:8, :], x8[:, b * P:(b + 1) * P], 0.0,
                                           ALU.mult, ALU.add)
            e.then_inc(decay_row, 1)
            r4 = [mixed[:, tb, 1024:2048].rearrange("p (h d) -> p h d", h=RET_HEADS) for tb in range(TB)]
            s4 = [ret_sq[:, tb].rearrange("p (h d) -> p h d", h=RET_HEADS) for tb in range(TB)]

            def over_head(s, tb):
                return ret_stat[:, s, tb].unsqueeze(2).broadcast_to([P, RET_HEADS, RET_DV])

            for tb in range(TB):
                dve.wait_ge(ret_copied, tb + 1)
                dve.tensor_reduce(ret_stat[:, 0, tb], r4[tb], AX_X, ALU.add)
                dve.drain()
                dve.tensor_scalar(ret_stat[:, 0, tb], ret_stat[:, 0, tb], 1.0 / RET_DV, None, ALU.mult)
                dve.drain()
                dve.tensor_tensor(r4[tb], r4[tb], over_head(0, tb), ALU.subtract).then_inc(ret_centered, 1)
            dve.wait_ge(decay_col, 1)
            dve.tensor_copy(gcol, ps[:, 0, 0:80].rearrange("p (b c) -> p b c", b=2)).then_inc(decay_cols_ready, 1)
            dve.drain()
            dve.tensor_scalar(neg_g, gcol[:, :, 0:8], -1.0, None, ALU.mult)
            dve.wait_ge(decay_spread, 1)
            dve.tensor_copy(g_end, spread[:, :, P - 1])
            dve.drain()
            dve.tensor_tensor(end_dec, g_end, gcol[:, 0, 0:8], ALU.subtract).then_inc(decay_cols_ready, 1)
            for g in range(4):
                src = spread[:, 4 * (g % 2):4 * (g % 2) + 4, (g // 2) * P:(g // 2 + 1) * P]
                dve.scalar_tensor_tensor(expo_a[:, g], src, -1.0, neg_a.broadcast_to([P, 4, P]), ALU.mult,
                                         ALU.add).then_inc(expo_ready, 1)
                dve.tensor_tensor(expo_d[:, g], src, neg_d.broadcast_to([P, 4, P]), ALU.add).then_inc(expo_ready, 1)
            dve.wait_ge(decay_exp, 1)
            dve.scalar_tensor_tensor(neg_beta_exp, exp_g[:, 1], -1.0, gcol[:, 1, 32:40], ALU.mult, ALU.mult)
            for tb in range(TB):
                dve.wait_ge(ret_squared, tb + 1)
                dve.tensor_reduce(ret_stat[:, 1, tb], s4[tb], AX_X, ALU.add)
            dve.drain()
            dve.tensor_scalar(ret_stat[:, 1], ret_stat[:, 1], 1.0 / RET_DV, EPS, ALU.mult, ALU.add).then_inc(ret_var, 1)
            dve.wait_ge(ret_root, 1)
            dve.reciprocal(ret_stat[:, 3], ret_stat[:, 2])
            dve.drain()
            for tb in range(TB):
                dve.tensor_tensor(r4[tb], r4[tb], over_head(3, tb), ALU.mult).then_inc(ret_scaled, 1)
            dve.wait_ge(ret_out, 2)
            for t in (inv, inv_t):
                e = dve.tensor_copy(t.rearrange("p g j n -> p (g j) n"), ident.unsqueeze(1).broadcast_to([P, 16, P]))
            e.then_inc(inv_updated, 4)
            dve.wait_ge(kv_turned, 8)
            for g in range(4):
                dve.tensor_copy(v_row[:, g], psg[:, 2 * g + 1]).then_inc(v_rows, 1)
            dve.wait_ge(decays_ready, 4)
            for g in range(4):
                dve.wait_ge(kk_done, g + 1)
                for j in range(4):
                    h = 4 * (g % 2) + j
                    e = dve.scalar_tensor_tensor(a_mat[:, g, j], psg[:, g, j], gcol[:, g // 2, 32 + h:33 + h],
                                                 expo_a[:, g, j], ALU.mult, ALU.mult)
                e.then_inc(kk_used, 1)
            dve.wait_ge(ret_done, 2)
            for g in range(4):
                dve.wait_ge(att_done, g + 1)
                dve.tensor_tensor(att[:, g], psg[:, 4 + g], expo_d[:, g], ALU.mult).then_inc(att_used, 1)
            with dve.Fori(0, LEVELS) as level:
                for g in range(4):
                    dve.wait_ge(outer_done, 4 * level + g + 1)
                    dve.tensor_tensor(inv[:, g], inv[:, g], psg[:, 4 + 2 * (g % 2)], ALU.subtract)
                    dve.tensor_tensor(inv_t[:, g], inv_t[:, g], psg[:, 5 + 2 * (g % 2)],
                                      ALU.subtract).then_inc(inv_updated, 1)
            for g in range(2):
                for j in range(4):
                    e = dve.tensor_scalar(rhs[:, g, j], v_row[:, g, j], gcol[:, 0, 32 + 4 * g + j:33 + 4 * g + j], None,
                                          ALU.mult)
                e.then_inc(rhs_ready, 1)
            for g in range(2):
                for j in range(4):
                    h = 4 * g + j
                    dve.tensor_scalar(v_row[:, 2 + g, j], v_row[:, 2 + g, j], gcol[:, 1, 32 + h:33 + h], None, ALU.mult)
            for g in range(2):
                dve.wait_ge(new_done, g + 1)
                dve.tensor_copy(v_new[:, g], psg[:, g]).then_inc(new_copied, 1)
            for g in range(2):
                dve.wait_ge(o_done, g + 1)
                dve.tensor_copy(o_rows(g), psg[:, 6 + g]).then_inc(o_copied, 1)
            for g in range(2):
                dve.wait_ge(from_state, g + 1)
                for j in range(4):
                    h = 4 * g + j
                    e = dve.scalar_tensor_tensor(rhs[:, 2 + g, j], psg[:, g, j], neg_beta_exp[:, h:h + 1],
                                                 v_row[:, 2 + g, j], ALU.mult, ALU.add)
                e.then_inc(rhs_ready, 1)
            for g in range(2):
                dve.wait_ge(new_done, g + 3)
                dve.tensor_copy(v_new[:, 2 + g], psg[:, 4 + g]).then_inc(new_copied, 1)
            for g in range(2):
                dve.wait_ge(q_state_copied, g + 1)
                dve.wait_ge(o_done, g + 3)
                dve.tensor_tensor(o_rows(2 + g), psg[:, g], q_out[:, g], ALU.add)
            dve.drain()
            for g in range(4):
                dve.tensor_tensor(o_sq[:, g], o_rows(g), o_rows(g), ALU.mult)
            dve.drain()
            dve.tensor_reduce(o_stat[:, 0], o_sq.rearrange("p g j n -> p (g j) n"), AX_X, ALU.add)
            dve.drain()
            dve.tensor_scalar(o_stat[:, 1], o_stat[:, 0], 1.0 / DK, EPS, ALU.mult, ALU.add).then_inc(o_mean, 1)
            dve.wait_ge(o_root, 1)
            dve.reciprocal(o_stat[:, 0], o_stat[:, 2])
            dve.wait_ge(z_weighted, 1)
            dve.drain()
            for g in range(4):
                for j in range(4):
                    dve.scalar_tensor_tensor(o_rows(g)[:, j], o_rows(g)[:, j], o_stat[:, 0, 4 * g + j:4 * g + j + 1],
                                             rows[:, g % 2, g // 2, j * P:(j + 1) * P], ALU.mult, ALU.mult)
            meet(dve, 2)
            dve_turn(dve, 1, None)
            meet(dve, 3)

            def take_out(g, parity):
                dve.wait_ge(lo_used, T_OUT + 8 * g + 8)
                dve.tensor_tensor(xh[:, :, ds(512 * g, 512)], ps[:, 2 - 2 * parity:4 - 2 * parity, :],
                                  xn[:, :, ds(512 * g, 512)], ALU.add).then_inc(taken, 1)

            dve.wait_ge(x_again, 16)
            group_round(T_OUT, 0, take_out, first=True)
            with dve.Fori(1, 2) as i:
                group_round(T_OUT, i, take_out)
            take_out(3, 1)
            dve.drain().then_inc(h_ready, 1)
            dve_norm(dve, 1, xh)
            dve_turn(dve, 2, 1)
            meet(dve, 4)

            def take_query(c, parity):
                dve.wait_ge(lo_used, T_PQ + 2 * c + 2)
                dve.tensor_scalar(query_t[:, ds(c, 1), :], ps[:, parity:parity + 1, 0:SEQ], 1.0, None,
                                  ALU.mult).then_inc(taken, 1)

            chunk_round(T_PQ, 0, lambda i, c: c and take_query(0, 0))
            with dve.Fori(1, PQ_CHUNKS // 2) as i:
                chunk_round(T_PQ, i, lambda i, c: take_query(2 * i + c - 1, 1 - c))
            take_query(PQ_CHUNKS - 1, 1)

            dve.wait_ge(scores_ready, 8)
            with dve.Fori(0, PK_HEADS * TB // 2) as i:
                for half in range(2):
                    unit = 2 * i + half

                    def tile(k):
                        rest_tile(dve, *tile_at(T_U, i, 12, 6 * half + k)[:3])

                    def sixteen(values, work, tops, index):
                        for v, t in zip(values, tops):
                            dve.max(t[:, 0:8], v)
                        dve.drain()
                        for v, w, t, x in zip(values, work, tops, index):
                            dve.max_index(x[:, 0:8], t[:, 0:8], v)
                            dve.match_replace(w, t[:, 0:8], v, LOWEST)
                        dve.drain()
                        yield
                        for w, t in zip(work, tops):
                            dve.max(t[:, 8:16], w)
                        dve.drain()
                        for w, t, x in zip(work, tops, index):
                            dve.max_index(x[:, 8:16], t[:, 8:16], w)
                        dve.drain()

                    tile(0)
                    dve.tensor_copy(key_in, scores[:, ds(unit, 1)].rearrange("p a k n -> p (a k) n"))
                    dve.drain()
                    for _ in sixteen([key_in[:, k] for k in range(2)], [key_work[:, k] for k in range(2)],
                                     [key_top[:, k] for k in range(2)], [key_index[:, k] for k in range(2)]):
                        tile(1)
                    tile(2)
                    dve.tensor_copy(key_index_f, key_index)
                    dve.tensor_tensor(cand, key_top[:, 0].unsqueeze(2).broadcast_to([P, TOPK, TOPK]),
                                      key_top[:, 1].unsqueeze(1).broadcast_to([P, TOPK, TOPK]), ALU.add)
                    dve.drain()
                    cand_row = cand.rearrange("p a b -> p (a b)")
                    for _ in sixteen([cand_row], [cand_work], [best], [best_index]):
                        tile(3)
                    tile(4)
                    dve.tensor_copy(best_all[:, ds(unit, 1), :], best.unsqueeze(1))
                    dve.tensor_scalar(ranks[:, 0], best_index, 4, None, ALU.logical_shift_right)
                    dve.tensor_scalar(ranks[:, 1], best_index, TOPK - 1, None, ALU.bitwise_and)
                    dve.drain()
                    dve.tensor_copy(ranks_f, ranks)
                    dve.drain()
                    dve.tensor_tensor(picked, iota[:, 0:TOPK].unsqueeze(1).unsqueeze(1).broadcast_to([P, 2, TOPK, TOPK]),
                                      ranks_f.unsqueeze(3).broadcast_to([P, 2, TOPK, TOPK]), ALU.is_equal)
                    dve.drain()
                    tile(5)
                    dve.tensor_tensor(picked, picked, key_index_f.unsqueeze(2).broadcast_to([P, 2, TOPK, TOPK]), ALU.mult)
                    dve.drain()
                    for k in range(2):
                        dve.tensor_reduce(picks_all[:, k, ds(unit, 1), :], picked[:, k], AX_X, ALU.add)
                    dve.drain()

            def plain(start, stop):
                with dve.Fori(start // 2, stop // 2) as i:
                    for k in range(4):
                        rest_tile(dve, *tile_at(T_U, i, 4, k)[:3])

            top_first = best_all[:, :, 0:1].broadcast_to([P, 16, TOPK])
            dve.tensor_tensor(gates3, best_all, top_first, ALU.subtract).then_inc(gates_in, 1)
            plain(TOPK_CHUNKS, TOPK_CHUNKS + 2)
            dve.wait_ge(gates_exp, 1)
            dve.tensor_reduce(gate_sum, gates3, AX_X, ALU.add)
            dve.drain()
            dve.reciprocal(gate_sum, gate_sum)
            dve.drain()
            dve.tensor_tensor(gates3, gates3, gate_sum.unsqueeze(2).broadcast_to([P, 16, TOPK]),
                              ALU.mult).then_inc(gates_ready, 1)
            plain(TOPK_CHUNKS + 2, TOPK_CHUNKS + 8)
            dve.wait_ge(sel_turned, 1)
            dve.tensor_copy(sel1_t[:], ps[:, 6, 0:SEQ])
            dve.tensor_copy(sel2_t[:], ps[:, 6, SEQ:2 * SEQ])
            dve.tensor_copy(gate_t[:], ps[:, 7, 0:SEQ])
            dve.drain().then_inc(sel_ready, 1)
            for part in range(3):
                dve.tensor_copy(gate_parts[:, part], gate_t[:])
                dve.drain()
                if part < 2:
                    dve.tensor_tensor(gate_t[:], gate_t[:], gate_parts[:, part], ALU.subtract)
                    dve.drain()
            plain(TOPK_CHUNKS + 8, CHUNKS // 2)

            def second_keys(q, slot, half):
                dve.drain()
                dve.wait_ge(gates_summed, q + GROUPS * half + 1)
                dve.tensor_tensor(equal2, iota[:, half * HALF_KEYS:(half + 1) * HALF_KEYS].unsqueeze(1)
                                  .broadcast_to([P, 4, HALF_KEYS]),
                                  sel2_t[:, ds(4 * q, 4)].unsqueeze(2).broadcast_to([P, 4, HALF_KEYS]), ALU.is_equal)
                dve.drain()
                dve.tensor_tensor(onehot2[:, slot], equal2.unsqueeze(2).broadcast_to([P, 4, 3, HALF_KEYS]),
                                  gate_parts[:, :, ds(4 * q, 4)].rearrange("p s t -> p t s").unsqueeze(3)
                                  .broadcast_to([P, 4, 3, HALF_KEYS]), ALU.mult).then_inc(onehot2_ready, 1)

            def apply_gates(q, slot, half):
                dve.wait_ge(gates_summed, q + GROUPS * half + 3)
                a = experts[:, half * HALF_KEYS:(half + 1) * HALF_KEYS, ds(4 * q, 4)]
                g = ps[:, 4 + slot, 0:4 * HALF_KEYS].rearrange("p (t c) -> p c t", t=4)
                dve.tensor_tensor(a, a, g, ALU.mult).then_inc(gates_applied, 1)

            dve.sem_inc(gates_applied, 2)
            dve.wait_ge(expert_bank, CHUNKS // 2 + 2)
            second_keys(0, 0, 0)
            for c in range(2):
                for k in range(2):
                    rest_tile(dve, *tile_at(T_U, CHUNKS // 4, 4, 2 * c + k)[:3])
                if c == 0:
                    second_keys(1, 1, 0)
                apply_gates(c, c, 0)
            with dve.Fori(CHUNKS // 4 + 1, CHUNKS // 2) as i:
                for c in range(2):
                    q = 2 * i + c - CHUNKS // 2
                    rest_tile(dve, *tile_at(T_U, i, 4, 2 * c)[:3])
                    second_keys(q, c, 0)
                    rest_tile(dve, *tile_at(T_U, i, 4, 2 * c + 1)[:3])
                    apply_gates(q, c, 0)

            def value_tile(half, i, c):
                v = CHUNKS * half + 4 * i + c
                dve.wait_ge(stage_hi_ready, v + 1)
                dve.tensor_tensor(stage_lo[:, c % 2:c % 2 + 1, :], experts[:, ds(4 * i + c, 1), :],
                                  stage_hi[:, c % 2:c % 2 + 1, :].bitcast(F32), ALU.subtract).then_inc(stage_lo_ready, 1)
                rest_tile(dve, T_V + v, c % RAW, c % SPLIT)

            with dve.Fori(0, CHUNKS // 8) as i:
                for c in range(4):
                    second_keys(4 * i + c, c % 2, 1)
                    value_tile(0, i, c)
                    apply_gates(4 * i + c, c % 2, 1)
            with dve.Fori(CHUNKS // 8, CHUNKS // 4) as i:
                for c in range(4):
                    value_tile(0, i, c)
            with dve.Fori(0, CHUNKS // 4) as i:
                for c in range(4):
                    value_tile(1, i, c)
            dve.wait_ge(stage_hi_ready, 2 * CHUNKS + 1)
            dve.tensor_tensor(stage_lo[:], p_rows, stage_hi[:].bitcast(F32), ALU.subtract).then_inc(stage_lo_ready, 1)
            for k in range(2):
                rest_tile(dve, *tile_at(T_PLE, 0, 4, k)[:3])
            dve.wait_ge(h_back, 16)
            dve.wait_ge(lo_used, T_PLE)
            for half in range(2):
                for tb in range(TB):
                    dst = xh[:, tb, half * 1024:(half + 1) * 1024].rearrange("p (b n) -> p b n", b=2)
                    dve.tensor_tensor(dst, ps[:, 4 * half + 2 * tb:4 * half + 2 * tb + 2, :], dst,
                                      ALU.add).then_inc(taken, 1)
            for k in range(4):
                if k >= 2:
                    rest_tile(dve, *tile_at(T_PLE, 0, 4, k)[:3])
                if k >= 1:
                    take_ple(dve, k - 1)
            take_ple(dve, 3)
            dve_norm(dve, 2, xh)
            dve_turn(dve, 3, 2)
            meet(dve, 5)

            def take_gate(g, parity):
                dve.wait_ge(sigmoid_ready, g + 1)
                s = gate_sig[:, parity]
                dve.tensor_tensor(s, s, ple[:, :, ds(512 * g, 512)], ALU.mult)
                dve.drain()
                dst = xh[:, :, ds(512 * g, 512)]
                dve.tensor_tensor(dst, dst, s, ALU.add).then_inc(taken, 1)

            group_round(T_GATE, 0, take_gate, first=True)
            group_round(T_GATE, 1, take_gate)
            take_gate(3, 1)
            dve.wait_ge(squares_summed, 8)
            dve.tensor_scalar(stat[:, 2:4], stat[:, 0:2], 1.0 / D, EPS, ALU.mult, ALU.add).then_inc(mean_ready, 1)
            dve.wait_ge(root_ready, 4)
            dve.reciprocal(stat[:, 6:8], stat[:, 4:6])
            dve.drain()
            dve.wait_ge(final_landed, 16)
            for tb in range(TB):
                dve.scalar_tensor_tensor(final[:, tb], xh[:, tb], stat[:, 6 + tb:7 + tb], final_w, ALU.mult,
                                         ALU.mult).then_inc(out_ready, 1)

        @block.gpsimd
        def _(pool):
            pool.wait_ge(consts_landed, ALL_CONSTS)
            pool.wait_ge(normed, 2)
            pool.wait_ge(turned, 8)
            pool.tensor_copy(angle, pos_i)
            pool.drain()
            pool.tensor_scalar(angle, angle, keep[:, C_INVF:C_INVF + 1], 1.0, ALU.mult, ALU.mult)
            pool.drain()
            for out_ap, quarter in ((turns, 0.25), (angle, 0.0)):
                k = trig_k
                pool.tensor_scalar(k, angle, 1.0 / TWO_PI, quarter, ALU.mult, ALU.add)
                pool.drain()
                pool.tensor_scalar(k, k, ROUNDER, 0.0, ALU.add, ALU.add)
                pool.drain()
                pool.tensor_scalar(k, k, -ROUNDER, 0.0, ALU.add, ALU.add)
                pool.drain()
                src = angle
                for part in TWO_PI_PARTS:
                    pool.tensor_scalar(trig_p, k, part, 1.0, ALU.mult, ALU.mult)
                    pool.drain()
                    pool.tensor_tensor(out_ap, src, trig_p, ALU.subtract)
                    pool.drain()
                    src = out_ap
                pool.tensor_scalar(out_ap, out_ap, quarter * TWO_PI, 0.0, ALU.add, ALU.add)
                pool.drain()
                pool.tensor_scalar(out_ap, out_ap, PI_BELOW, -PI_BELOW, ALU.min, ALU.max).then_inc(angles_ready, 1)
                pool.drain()
            meet(pool, 0)
            meet(pool, 1)
            pool.wait_ge(trig_ready, 2)
            rotate(pool, 2).then_inc(k_rotated, 1)
            pool.wait_ge(rows_silu, 2)
            z = rows[:, 0:2].rearrange("p g b c -> p (g b c)").rearrange("p (n d) -> p n d", d=P)
            pool.tensor_tensor(z, z, dn_w.unsqueeze(1).broadcast_to([P, 16, P]), ALU.mult).then_inc(z_weighted, 1)
            for tb in range(TB):
                pool.wait_ge(ret_scaled, tb + 1)
                r = mixed[:, tb, 1024:2048]
                pool.tensor_tensor(r, r, mixed[:, 0, 0:1024], ALU.mult)
                pool.drain()
                pool.tensor_tensor(r, r, mixed[:, 1, 0:1024], ALU.add)
                pool.drain()
                r2 = r.rearrange("p (g c) -> p g c", g=2)
                pool.tensor_tensor(r2, r2, rows[:, 4:6, tb, :], ALU.mult).then_inc(ret_done, 1)
            pool.wait_ge(kk_used, 4)
            with pool.Fori(0, LEVELS) as level:
                for g in range(4):
                    hold(pool, "pool", inv_updated, 4 * level + g + 1)
                    pool.tensor_tensor(blocks[:, g], a_mat[:, g], level_mask[:, ds(level, 1)].broadcast_to([P, 4, P]),
                                       ALU.mult).then_inc(blocks_ready, 1)
            meet(pool, 2)
            meet(pool, 3)
            meet(pool, 4)

            def first_keys(half, i):
                for slot in range(2):
                    q = 2 * i + slot
                    hold(pool, "pool", gates_summed, q + GROUPS * half + 1)
                    pool.tensor_copy(sel4[:, slot], sel1_t[:, ds(4 * q, 4)])
                    pool.drain()
                    for t in range(4):
                        e = pool.tensor_scalar(onehot1[:, slot, t], iota, sel4[:, slot, t:t + 1], None, ALU.is_equal)
                    e.then_inc(onehot1_ready, 1)

            pool.wait_ge(sel_ready, 1)
            for half in range(2):
                with pool.Fori(0, GROUPS // 2) as i:
                    first_keys(half, i)
            meet(pool, 5)

        @block.tensor
        def _(pe):
            pe.wait_ge(consts_landed, ALL_CONSTS)
            pe.wait_ge(normed, 2)
            pe_turn(pe, xn)
            meet(pe, 0)

            def column_chunk(base, i, c, signal=None):
                for k in range(2):
                    n, _, use, _ = tile_at(base, i, 4, 2 * c + k)
                    column_tile(pe, n, use, k, ps[:, c, 0:SEQ])

            for c in range(2):
                column_chunk(0, 0, c)
            with pe.Fori(1, IN_CHUNKS // 2) as i:
                for c in range(2):
                    pe.wait_ge(taken, 2 * i + c - 1)
                    column_chunk(0, i, c)
            for d in range(DC):
                pe.matmul(ps[0:64, 4, 0:SEQ], ab_w[:, d, :], act_hi[:, d, :].bitcast(F32), start=(d == 0), stop=False)
                pe.matmul(ps[0:64, 4, 0:SEQ], ab_w[:, d, :], act_lo[:, d, :].bitcast(F32), start=False,
                          stop=(d == DC - 1))

            def row_groups(base, count, taken_before):
                with pe.Fori(0, count // 2) as i:
                    for g in range(2):
                        pe.wait_ge(taken, taken_before - 1 + 2 * i + g)
                        for k in range(8):
                            n, _, use, _ = tile_at(base, i, 16, 8 * g + k)
                            row_tile(pe, n, use, k, [ps[:, 2 - 2 * g + tb, :] for tb in range(TB)])

            row_groups(T_ROW, ROW_GROUPS, IN_CHUNKS)
            meet(pe, 1)

            pe.wait_ge(ab_copied, 1)
            for p in range(8):
                pe.wait_ge(qk_squared, p + 1)
                if p >= 2:
                    pe.wait_ge(qk_root, p - 1)
                pe.matmul(ps[:, p % 2, :], ones_m, squares[:, p % 2], start=True, stop=True).then_inc(qk_summed, 1)
            pe.wait_ge(qk_root, 8)
            pe.wait_ge(q_rotated, 1)
            pe.wait_ge(k_rotated, 1)
            for h in range(RET_HEADS):
                g, rowsl = h // 4, slice(HALF * (h % 4), HALF * (h % 4 + 1))
                for m, (c0, c1), at in ((0, (0, SEQ), 0), (1, (P, SEQ), SEQ)):
                    for x12 in range(2):
                        mm = pe.matmul(ps[:, h, at:at + c1 - c0], rot[rowsl, 2 + x12, g, m * P:(m + 1) * P],
                                       rot[rowsl, x12, g, c0:c1], start=(x12 == 0), stop=(x12 == 1))
                mm.then_inc(ret_scores, 1)
            pe.wait_ge(ret_masked, 8)
            for tb in range(TB):
                for h in range(RET_HEADS):
                    o = ps[:, 2 * tb + h // 4, (h % 4) * P:(h % 4 + 1) * P]
                    for m in range(tb + 1):
                        mm = pe.matmul(o, att_ret[:, h, (tb + m) * P:(tb + m + 1) * P],
                                       rows[:, 2 + h // 4, m, (h % 4) * P:(h % 4 + 1) * P],
                                       start=(m == 0), stop=(m == tb))
                mm.then_inc(ret_out, 1)
            pe.wait_ge(decay_row, 1)
            pe.wait_ge(selector_ready, 1)
            for h in range(DN_HEADS):
                mm = pe.matmul(spread[:, h, :], selector[:, h, :], gb[0:8, :], start=True, stop=True)
            mm.then_inc(decay_spread, 1)
            pe.wait_ge(ret_copied, 2)
            for b in range(TB):
                mm = pe.transpose(ps[:, 0, 40 * b:40 * b + 40], gb[0:40, b * P:(b + 1) * P], ident[0:40, 0:40])
            mm.then_inc(decay_col, 1)
            pe.wait_ge(qk_normed, 8)
            pe.wait_ge(expo_ready, 8)
            for g in range(4):
                for kv in range(2):
                    for j in range(4):
                        mm = pe.transpose(psg[:, 2 * g + kv, j], channel(1 + kv, g, j), ident)
                    mm.then_inc(kv_turned, 1)
            pe.wait_ge(k_rows, 4)
            pe.wait_ge(v_rows, 4)
            for g in range(4):
                for j in range(4):
                    mm = pe.matmul(psg[:, g, j], channel(1, g, j), channel(1, g, j), start=True, stop=True)
                mm.then_inc(kk_done, 1)
            for g in range(4):
                for j in range(4):
                    mm = pe.matmul(psg[:, 4 + g, j], channel(1, g, j), channel(0, g, j), start=True, stop=True)
                mm.then_inc(att_done, 1)
            pe.wait_ge(att_used, 4)
            with pe.Fori(0, LEVELS) as level:
                def inner_products(g):
                    pe.wait_ge(blocks_ready, 4 * level + g + 1)
                    for j in range(4):
                        mm = pe.matmul(psg[:, g, j], blocks[:, g, j], inv_t[:, g, j], start=True, stop=True)
                    mm.then_inc(inner_done, 1)

                def outer_products(g):
                    pe.wait_ge(inner_copied, 4 * level + g + 1)
                    pe.wait_ge(inv_updated, 4 * level + g + 3)
                    for j in range(4):
                        pe.matmul(psg[:, 4 + 2 * (g % 2), j], inner[:, g, j], inv[:, g, j], start=True, stop=True)
                    for j in range(4):
                        mm = pe.matmul(psg[:, 5 + 2 * (g % 2), j], inv[:, g, j], inner[:, g, j], start=True, stop=True)
                    mm.then_inc(outer_done, 1)

                inner_products(0)
                inner_products(1)
                outer_products(0)
                inner_products(2)
                outer_products(1)
                inner_products(3)
                outer_products(2)
                outer_products(3)
            pe.wait_ge(inv_updated, 4 * LEVELS + 4)
            for g in range(2):
                pe.wait_ge(rhs_ready, g + 1)
                for j in range(4):
                    mm = pe.matmul(psg[:, g, j], inv_t[:, g, j], rhs[:, g, j], start=True, stop=True)
                mm.then_inc(new_done, 1)
            pe.wait_ge(kd_ready, 1)
            for g in range(2):
                pe.wait_ge(new_copied, g + 1)
                for j in range(4):
                    mm = pe.matmul(psg[:, 4 + g, j], k_dec[:, g, j], v_new[:, g, j], start=True, stop=True)
                mm.then_inc(state_done, 1)
            for g in range(2):
                for j in range(4):
                    mm = pe.matmul(psg[:, 6 + g, j], att[:, g, j], v_new[:, g, j], start=True, stop=True)
                mm.then_inc(o_done, 1)
            for g in range(2):
                pe.wait_ge(state_copied, g + 1)
                for j in range(4):
                    mm = pe.matmul(psg[:, g, j], channel(1, 2 + g, j), state[:, g, j], start=True, stop=True)
                mm.then_inc(from_state, 1)
            for g in range(2):
                for j in range(4):
                    mm = pe.matmul(psg[:, 2 + g, j], channel(0, 2 + g, j), state[:, g, j], start=True, stop=True)
                mm.then_inc(q_state, 1)
            for g in range(2):
                pe.wait_ge(rhs_ready, g + 3)
                for j in range(4):
                    mm = pe.matmul(psg[:, 4 + g, j], inv_t[:, 2 + g, j], rhs[:, 2 + g, j], start=True, stop=True)
                mm.then_inc(new_done, 1)
            for g in range(2):
                pe.wait_ge(new_copied, g + 3)
                for j in range(4):
                    mm = pe.matmul(psg[:, g, j], att[:, 2 + g, j], v_new[:, 2 + g, j], start=True, stop=True)
                mm.then_inc(o_done, 1)
            meet(pe, 2)
            pe_turn(pe, mixed)
            meet(pe, 3)
            row_groups(T_OUT, D // 512, IN_CHUNKS + ROW_GROUPS)
            pe.wait_ge(normed, 4)
            pe_turn(pe, xn_of[1])
            meet(pe, 4)
            with pe.Fori(0, PQ_CHUNKS // 2) as i:
                for c in range(2):
                    pe.wait_ge(taken, TAKEN_OUT - 1 + 2 * i + c)
                    column_chunk(T_PQ, i, c)
            pe.wait_ge(taken, TAKEN_OUT + PQ_CHUNKS)
            pe.wait_ge(keys_landed, 16)
            for b in range(8):
                for k in range(4):
                    hp = 4 * (b % 4) + k
                    mm = pe.matmul(ps[:, b, k * P:(k + 1) * P], query_t[:, hp, (b // 4) * P:(b // 4 + 1) * P],
                                   keys_t[:, hp, :], start=True, stop=True)
                mm.then_inc(scores_done, 1)

            def expert_chunks(start, stop, and_then=None):
                with pe.Fori(start // 2, stop // 2) as i:
                    for c in range(2):
                        pe.wait_ge(expert_bank, 2 * i + c + 1)
                        column_chunk(T_U, i, c)
                        if and_then:
                            and_then(i, c)

            def sum_gates(n, slot):
                pe.wait_ge(onehot1_ready, n + 1)
                pe.wait_ge(onehot2_ready, n + 1)
                pe.wait_ge(gates_applied, n + 1)
                for t in range(4):
                    o = ps[:, 4 + slot, t * HALF_KEYS:(t + 1) * HALF_KEYS]
                    for part in range(3):
                        mm = pe.matmul(o, onehot1[:, slot, t], onehot2[:, slot, t, part], start=(part == 0),
                                       stop=(part == 2))
                mm.then_inc(gates_summed, 1)

            pe.sem_inc(gates_summed, 2)
            expert_chunks(0, TOPK_CHUNKS + 4)
            pe.wait_ge(gates_ready, 1)
            for tb in range(TB):
                for k in range(2):
                    pe.transpose(ps[:, 6, (2 * k + tb) * P:(2 * k + tb + 1) * P],
                                 picks_all[:, k, 8 * tb:8 * tb + 8].rearrange("p u r -> p (u r)"), ident)
                mm = pe.transpose(ps[:, 7, tb * P:(tb + 1) * P],
                                  gates3[:, 8 * tb:8 * tb + 8].rearrange("p u r -> p (u r)"), ident)
            mm.then_inc(sel_turned, 1)
            expert_chunks(TOPK_CHUNKS + 4, CHUNKS // 2)
            expert_chunks(CHUNKS // 2, CHUNKS, lambda i, c: sum_gates(2 * i + c - CHUNKS // 2, c))

            def value_round(half, i, and_then=None, first=False):
                for c in range(4):
                    v, use = CHUNKS * half + 4 * i + c, c % SPLIT
                    pe.wait_ge(hi_ready, T_V + v + 1)
                    pe.wait_ge(stage_lo_ready, v + 1)
                    for k, a in enumerate((stage_hi, stage_lo)):
                        for tb in range(TB):
                            for b in range(2):
                                mm = pe.matmul(ps[:, 4 * half + 2 * tb + b, :], a[:, use, tb * P:(tb + 1) * P],
                                               hi[:, use, b * 512:(b + 1) * 512], start=(first and c == 0 and k == 0),
                                               stop=False, skip_group_check=True)
                    mm.then_inc(hi_used, 1)
                    pe.wait_ge(lo_ready, T_V + v + 1)
                    for tb in range(TB):
                        for b in range(2):
                            mm = pe.matmul(ps[:, 4 * half + 2 * tb + b, :], stage_hi[:, use, tb * P:(tb + 1) * P],
                                           lo[:, use, b * 512:(b + 1) * 512], start=False, stop=False,
                                           skip_group_check=True)
                    mm.then_inc(lo_used, 1)
                    if and_then:
                        and_then(4 * i + c, c % 2)

            def gates_too(v, slot):
                sum_gates(v + GROUPS, slot)

            pe.wait_ge(expert_bank, CHUNKS + 2)
            value_round(0, 0, gates_too, first=True)
            with pe.Fori(1, CHUNKS // 8) as i:
                value_round(0, i, gates_too)
            with pe.Fori(CHUNKS // 8, CHUNKS // 4) as i:
                value_round(0, i)
            pe.wait_ge(gates_applied, 2 * GROUPS + 2)
            value_round(1, 0, first=True)
            with pe.Fori(1, CHUNKS // 4) as i:
                value_round(1, i)
            for g, before in enumerate((TAKEN_H, TAKEN_H, TAKEN_H + 1, TAKEN_H + 2)):
                n, _, use, _ = tile_at(T_PLE, 0, 4, g)
                pe.wait_ge(taken, before)
                pe.wait_ge(stage_lo_ready, 2 * CHUNKS + 1)
                row_tile(pe, n, use, 0, [ps[:, 2 - 2 * (g % 2) + tb, :] for tb in range(TB)], stage_hi, stage_lo, last=0)
            pe.wait_ge(taken, TAKEN_PLE)
            pe.wait_ge(normed, 6)
            pe_turn(pe, xn_of[2])
            meet(pe, 5)
            row_groups(T_GATE, D // 512, TAKEN_PLE)


_OUTS = [((1, SEQ, D), "float32")]


def kernel(**inputs):
    import numpy as _np
    import concourse.bacc as _bacc
    from concourse import mybir as _mybir
    from concourse.bass_utils import run_bass_kernel_spmd as _run

    a = {k: _np.asarray(v) for k, v in inputs.items()}

    def column_tiles(w):
        n = w.shape[1] // P
        return _np.ascontiguousarray(w.reshape(2, 8, P, n, P).transpose(3, 0, 2, 1, 4).reshape(2 * n, P, TILE))

    def row_tiles(w):
        k, n = w.shape[0] // 256, w.shape[1] // 512
        return _np.ascontiguousarray(w.reshape(k, 2, P, n, 512).transpose(3, 0, 2, 1, 4).reshape(n * k, P, TILE))

    def by_column(v):
        return v.reshape(-1, P).T

    w_in = a["w_in"][0]
    at = _np.cumsum([0, CONV_CH, 1024, 8, 8, 512, 512, 1024, 1024])
    conv, z, ga, gb, rq, rk, rv, rg = (w_in[:, at[i]:at[i + 1]] for i in range(8))
    halves = [r.reshape(D, RET_HEADS, 2, HALF).transpose(0, 2, 1, 3).reshape(D, 512) for r in (rq, rk)]
    w_ab = _np.zeros((P, DC, 64), _np.float32)
    w_ab[:, :, 0:8] = ga.reshape(DC, P, 8).transpose(1, 0, 2)
    w_ab[:, :, 32:40] = gb.reshape(DC, P, 8).transpose(1, 0, 2)
    keep_c, mix_c = shape_consts()
    u = a["expert_u"][0].reshape(N_KEYS, N_KEYS, 2, 8, P)
    v = a["expert_v"][0].reshape(N_KEYS, N_KEYS, 2, TILE)
    arrays = {
        "x": a["x"][0],
        "w_in_cols": column_tiles(_np.concatenate([conv] + halves, axis=1)),
        "w_in_rows": row_tiles(_np.concatenate([z, rv, rg], axis=1)),
        "w_ab": w_ab,
        "w_out": row_tiles(a["w_out"][0]),
        "w_pq": column_tiles(a["w_pq"][0]),
        "expert_u": u.transpose(1, 2, 4, 3, 0).reshape(2 * CHUNKS, P, TILE),
        "expert_v": v.transpose(2, 1, 0, 3).reshape(2 * CHUNKS, P, TILE),
        "w_gate": row_tiles(a["w_ple_gate"][0]),
        "w_ple": row_tiles(a["w_ple_proj"][0]),
        "p_t": a["p"][0, 0].reshape(SEQ, 2, P).transpose(2, 1, 0),
        "positions": a["positions"][0],
        "keep_c": keep_c,
        "mix_c": mix_c,
        "norm_cols": _np.stack([by_column(a[k][0]) for k in ("norm_mix", "norm_ffn", "norm_ple")], axis=1),
        "conv_cols": a["conv_w"][0].reshape(CONV_CHUNKS, P, CONV_W).transpose(1, 0, 2).reshape(P, -1),
        "sub_keys_t": a["sub_keys"][0].reshape(2 * PK_HEADS, N_KEYS, P).transpose(2, 0, 1),
        "ab_cols": _np.stack([a["a_log"][0], a["dt_bias"][0]], axis=1),
        "dn_norm": a["dn_norm"][0],
        "ret_gn_w": a["ret_gn_w"][0],
        "ret_gn_b": a["ret_gn_b"][0],
        "norm_final": a["norm_final"],
    }
    arrays = {"in_" + k: _np.ascontiguousarray(v) for k, v in arrays.items()}
    nc = _bacc.Bacc("TRN2", target_bir_lowering=False, num_devices=1)
    args = [nc.dram_tensor(k, v.shape, _mybir.dt.from_np(v.dtype), kind="ExternalInput").ap()
            for k, v in arrays.items()]
    args.append(nc.dram_tensor("out_0", (SEQ, D), F32, kind="ExternalOutput").ap())
    args.append(nc.dram_tensor("h_spill", (SEQ, D), F32, kind="Internal").ap())
    build(nc, *args)
    r = _run(nc, [arrays], core_ids=[0])
    return r.results[0]["out_0"].reshape(1, SEQ, D)
```

```python
from contextlib import ExitStack

import numpy as np

import concourse.bass as bass
from concourse import mybir

F32 = mybir.dt.float32
F32R = mybir.dt.float32r
BF16 = mybir.dt.bfloat16
I32 = mybir.dt.int32
U32 = mybir.dt.uint32
ALU = mybir.AluOpType
ACT = mybir.ActivationFunctionType
AX_X = mybir.AxisListType.X
ds = bass.ds

P = 128
SEQ = 256
TB = SEQ // P
D = 2048
DC = D // P
DN_HEADS, DK = 8, 128
RET_HEADS, RET_DK, RET_DV = 8, 64, 128
HALF = RET_DK // 2
CONV_CH = 3 * DN_HEADS * DK
CONV_W = 4
N_KEYS = 128
PK_HEADS = 8
TOPK = 16
PLE = 256
ALL_CONSTS = 16 * 7
EPS = 1e-6
MASKED = -1e30
LOWEST = -3.0e38
TOPK_CHUNKS = 48
GROUPS = SEQ // 4
HALF_KEYS = N_KEYS // 2
TWO_PI = 6.283185307179586
TWO_PI_PARTS = (6.28125, 0.001934051513671875, 1.2556659146142806e-06)
PI_BELOW = 3.1415925
ROUNDER = 12582912.0
LEVELS = 7

TILE = 1024
RAW = 4
SPLIT = 2
CONV_CHUNKS = CONV_CH // P
RQK_CHUNKS = 2 * RET_HEADS * RET_DK // P
IN_CHUNKS = CONV_CHUNKS + RQK_CHUNKS
ROW_GROUPS = 6
T_ROW = 2 * IN_CHUNKS
T_OUT = T_ROW + 8 * ROW_GROUPS
T_PQ = T_OUT + 8 * D // 512
PQ_CHUNKS = PK_HEADS * 2
T_U = T_PQ + 2 * PQ_CHUNKS
CHUNKS = N_KEYS
T_V = T_U + 2 * CHUNKS
PLE_CHUNK = CHUNKS * 3 // 4
T_PLE = T_V + CHUNKS + PLE_CHUNK
T_GATE = T_V + 2 * CHUNKS + 4
T_END = T_GATE + 8 * D // 512

TAKEN_OUT = IN_CHUNKS + ROW_GROUPS + D // 512
TAKEN_H0 = TAKEN_OUT + PQ_CHUNKS + TB
TAKEN_PLE = TAKEN_H0 + 4
TAKEN_H = TAKEN_PLE + TB

C_IDENT, C_IOTA, C_INVF = 0, 128, 256
C_KEEP = 257
C_LEVEL = 0
C_NEGA = C_LEVEL + LEVELS * P
C_NEGD = C_NEGA + P
C_RETD = C_NEGD + P
C_MIX = C_RETD + RET_HEADS * 3 * P


def shape_consts():
    i = np.arange(P)
    keep = np.zeros((P, C_KEEP), np.float32)
    keep[:, C_IDENT:C_IDENT + P] = np.eye(P)
    keep[:, C_IOTA:C_IOTA + P] = i[None, :]
    half = np.arange(HALF, dtype=np.float32)
    inv_freq = np.float32(10000.0) ** (-half / np.float32(HALF))
    keep[:, C_INVF] = inv_freq[i % HALF]
    mix = np.zeros((P, C_MIX), np.float32)
    for level in range(LEVELS):
        a, b = i[:, None] >> level, i[None, :] >> level
        mix[:, C_LEVEL + level * P:C_LEVEL + (level + 1) * P] = (a == b + 1) & (b % 2 == 0)
    mix[:, C_NEGA:C_NEGA + P] = np.where(i[:, None] > i[None, :], 0.0, MASKED)
    mix[:, C_NEGD:C_NEGD + P] = np.where(i[None, :] >= i[:, None], 0.0, MASKED)
    log_gamma = np.log1p(-np.exp2(-5.0 - np.arange(RET_HEADS)))
    rel = (i[None, :] - i[:, None]).astype(np.float64)
    for h in range(RET_HEADS):
        near = np.where(rel >= 0, np.exp(np.maximum(rel, 0) * log_gamma[h]), 0.0)
        far = np.exp((rel + P) * log_gamma[h])
        d = np.concatenate([near, far, near], axis=1) * RET_DK ** -0.5
        mix[:, C_RETD + h * 3 * P:C_RETD + (h + 1) * 3 * P] = d
    return keep, mix


def build(nc, x, w_in_cols, w_in_rows, w_ab, w_out, w_pq, expert_u, expert_v, w_gate, w_ple, p_t,
          positions, keep_c, mix_c, norm_cols, conv_cols, sub_keys_t, ab_cols, dn_norm, ret_gn_w,
          ret_gn_b, norm_final, out, h_spill):
    with ExitStack() as ctx:
        def sb(name, shape, dt=F32):
            return ctx.enter_context(nc.sbuf_tensor(name, shape, dt))

        def sem(name):
            return ctx.enter_context(nc.semaphore(name))

        arena = sb("arena", [P, CHUNKS * SEQ])
        raw = sb("raw", [P, RAW, TILE])
        hi = sb("hi", [P, SPLIT, TILE], F32R)
        lo = sb("lo", [P, SPLIT, TILE], F32R)
        act_hi = sb("act_hi", [P, DC, SEQ], F32R)
        act_lo = sb("act_lo", [P, DC, SEQ], F32R)
        stage_hi = sb("stage_hi", [P, 2, SEQ], F32R)
        stage_lo = sb("stage_lo", [P, 2, SEQ], F32R)
        keep = sb("keep", [P, C_KEEP])
        ncol = sb("ncol", [P, 3, DC])
        sel1_t = sb("sel1_t", [P, SEQ])
        sel2_t = sb("sel2_t", [P, SEQ])
        gate_t = sb("gate_t", [P, SEQ])
        ab_col = sb("ab_col", [8, 4])
        gate_parts = sb("gate_parts", [P, 3, SEQ], BF16)
        onehot1 = sb("onehot1", [P, 2, 4, N_KEYS], BF16)
        onehot2 = sb("onehot2", [P, 2, 4, 3, HALF_KEYS], BF16)
        equal2_t = sb("equal2", [P, 4 * HALF_KEYS], BF16)
        sel4 = sb("sel4", [P, 2, 4])
        stat = sb("stat", [P, 16])
        one = sb("one", [P, 2])
        ps = ctx.enter_context(nc.psum_tensor("ps", [P, 8, 512], F32))
        ident = keep[:, C_IDENT:C_IDENT + P]
        iota = keep[:, C_IOTA:C_IOTA + P]

        mixer_small = onehot1[:].rearrange("p a b c -> p (a b c)").bitcast(F32)
        dn_w, ones_m = mixer_small[:, 0:P], mixer_small[:, P:2 * P]
        diag = onehot2[:].rearrange("p a b c d -> p (a b c d)").bitcast(F32)[:, 0:TB * P].rearrange(
            "p (b n) -> p b n", b=TB)

        def region(start, *shape):
            n = int(np.prod(shape))
            v = arena[:, start:start + n]
            if len(shape) == 1:
                return v
            names = "abcd"[:len(shape)]
            return v.rearrange("p (" + " ".join(names) + ") -> p " + " ".join(names),
                               **dict(zip(names[1:], shape[1:])))

        xh = region(0, TB, D)
        xn = region(4096, TB, D)
        qkv = region(8192, 24, SEQ)
        rqk = region(14336, 8, SEQ)
        rows = region(16384, ROW_GROUPS, TB, 512)
        conv_in = region(0, 2, SEQ)
        conv_y = region(22528, 2, SEQ)
        squares = region(22528, 512)
        roots = region(23552, 512)
        ab_w = region(23040, DC, 64)
        conv_w = region(24064, CONV_CHUNKS * CONV_W)
        pos_i = region(24160, SEQ).bitcast(I32)
        mixc = region(24448, C_MIX)
        mixed = region(28672, TB, D)

        weights_landed = [sem(f"weights_landed{i}") for i in range(RAW)]
        hi_ready, lo_ready = sem("hi_ready"), sem("lo_ready")
        hi_used, lo_used = sem("hi_used"), sem("lo_used")
        held = {e: sem(f"held_{e}") for e in ("act", "dve", "pool")}
        x_landed, keep_landed, conv_landed, consts_landed = ([sem(f"x_landed{b}") for b in range(TB)], sem("keep_landed"),
                                                             sem("conv_landed"), sem("consts_landed"))
        ones_ready = sem("ones_ready")

        def hold(eng, name, s, value):
            eng.wait_ge(s, value)
            eng.sem_inc(held[name], 1)

        def load_tile(sp, n, slot, src, first=False):
            if not first:
                sp.wait_ge(lo_ready, n - RAW + 1)
            sp.dma_start(raw[:, slot, :], src).then_inc(weights_landed[slot], 16)

        def round_tile(act, n, slot, use, turn, first=False):
            act.wait_ge(weights_landed[slot], 16 * turn + 16)
            if not first:
                act.wait_ge(hi_used, n - SPLIT + 1)
                act.wait_ge(lo_ready, n - SPLIT + 1)
            act.activation(hi[:, use, :], raw[:, slot, :], ACT.Copy).then_inc(hi_ready, 1)

        def rest_tile(dve, n, slot, use, first=False):
            dve.wait_ge(hi_ready, n + 1)
            if not first:
                dve.wait_ge(lo_used, n - SPLIT + 1)
            dve.tensor_tensor(lo[:, use, :], raw[:, slot, :], hi[:, use, :].bitcast(F32),
                              ALU.subtract).then_inc(lo_ready, 1)

        def tile_at(base, i, per, k):
            assert base % RAW == 0 and per % RAW == 0
            return (base + k + per * i, (base + k) % RAW, (base + k) % SPLIT,
                    (base + k) // RAW + (per // RAW) * i)

        def column_tile(pe, n, use, k, out_ap, turn=None):
            pe.wait_ge(hi_ready, n + 1)
            for d8 in range(8):
                w, d = hi[:, use, d8 * P:(d8 + 1) * P], 8 * k + d8
                if turn is not None:
                    wait_turned(pe, turn, d, 1)
                pe.matmul(out_ap, w, act_hi[:, d, :], start=(d == 0), stop=False)
                mm = pe.matmul(out_ap, w, act_lo[:, d, :], start=False, stop=False)
            mm.then_inc(hi_used, 1)
            pe.wait_ge(lo_ready, n + 1)
            for d8 in range(8):
                mm = pe.matmul(out_ap, lo[:, use, d8 * P:(d8 + 1) * P], act_hi[:, 8 * k + d8, :],
                               start=False, stop=(k == 1 and d8 == 7))
            mm.then_inc(lo_used, 1)

        def row_tile(pe, n, use, k, outs, a_hi=None, a_lo=None, last=7, turn=None):
            a_hi = act_hi if a_hi is None else a_hi
            a_lo = act_lo if a_lo is None else a_lo
            pe.wait_ge(hi_ready, n + 1)
            for tb in range(TB):
                for k2 in range(2):
                    if turn is not None and tb == 0:
                        wait_turned(pe, turn, 2 * k + k2, 4)
                    w, d, t = hi[:, use, k2 * 512:(k2 + 1) * 512], 2 * k + k2, slice(tb * P, tb * P + P)
                    pe.matmul(outs[tb], a_hi[:, d, t], w, start=(d == 0), stop=False)
                    mm = pe.matmul(outs[tb], a_lo[:, d, t], w, start=False, stop=False)
            mm.then_inc(hi_used, 1)
            pe.wait_ge(lo_ready, n + 1)
            for tb in range(TB):
                for k2 in range(2):
                    mm = pe.matmul(outs[tb], a_hi[:, 2 * k + k2, tb * P:tb * P + P],
                                   lo[:, use, k2 * 512:(k2 + 1) * 512], start=False,
                                   stop=(k == last and k2 == 1))
            mm.then_inc(lo_used, 1)

        met = [sem(f"phase_done{i}") for i in range(3)]

        def meet(eng, i):
            eng.drain().then_inc(met[i], 1)
            eng.wait_ge(met[i], 4)

        squares_summed, mean_ready, root_ready = sem("squares_summed"), sem("mean_ready"), sem("root_ready")
        diag_ready, turned, act_hi_ready, act_lo_ready = (sem("diag_ready"), sem("turned"), sem("act_hi_ready"),
                                                          sem("act_lo_ready"))

        def square(act, h, tb, part, parts):
            n = D // parts
            c = slice(part * n, (part + 1) * n)
            act.activation(squares_out[:, tb, c], h[:, tb, c], ACT.Square,
                           accum_out=stat[:, tb * parts + part:tb * parts + part + 1]).then_inc(squares_summed, 1)

        def act_root(act, n):
            act.wait_ge(mean_ready, n + 1)
            act.activation(stat[:, 12:14], stat[:, 10:12], ACT.Sqrt).then_inc(root_ready, 1)

        def dve_scale(dve, n, parts, summed):
            dve.wait_ge(squares_summed, summed)
            sums = stat[:, 0:2]
            if parts > 1:
                sums = stat[:, 8:10]
                dve.tensor_reduce(sums, stat[:, 0:2 * parts].rearrange("p (b c) -> p b c", b=2), AX_X, ALU.add)
                dve.drain()
            dve.tensor_scalar(stat[:, 10:12], sums, 1.0 / D, EPS, ALU.mult, ALU.add).then_inc(mean_ready, 1)
            dve.wait_ge(root_ready, n + 1)
            dve.reciprocal(stat[:, 14:16], stat[:, 12:14])
            dve.drain()

        def dve_norm(dve, n, parts, summed):
            dve_scale(dve, n, parts, summed)
            for tb in range(TB):
                e = dve.tensor_scalar(diag[:, tb], ident, stat[:, 14 + tb:15 + tb], None, ALU.mult)
            e.then_inc(diag_ready, 1)

        def pe_turn(pe, rows_ap, scaled=True):
            for b in range(8):
                for k in range(4):
                    d, tb = 2 * b + k // 2, k % 2
                    o, r = ps[:, b, k * P:(k + 1) * P], rows_ap[:, tb, d * P:(d + 1) * P]
                    if scaled:
                        mm = pe.matmul(o, r, diag[:, tb], start=True, stop=True)
                    else:
                        mm = pe.transpose(o, r, ident)
                mm.then_inc(turned, 1)

        def act_turn(act, turn, w):
            for d in range(DC):
                act.wait_ge(turned, 8 * turn + d // 2 + 1)
                src = ps[:, d // 2, (d % 2) * SEQ:(d % 2 + 1) * SEQ]
                act.activation(act_hi[:, d, :], src, ACT.Copy,
                               scale=1.0 if w is None else ncol[:, w, d:d + 1]).then_inc(act_hi_ready, 1)

        def dve_turn(dve, turn, w):
            for d in range(DC):
                dve.wait_ge(act_hi_ready, DC * turn + 2 * (d // 2) + 2)
                src = ps[:, d // 2, (d % 2) * SEQ:(d % 2 + 1) * SEQ]
                dve.scalar_tensor_tensor(act_lo[:, d, :], src, 1.0 if w is None else ncol[:, w, d:d + 1],
                                         act_hi[:, d, :].bitcast(F32), ALU.mult, ALU.subtract).then_inc(act_lo_ready, 1)

        def wait_turned(pe, turn, d, banks):
            pe.wait_ge(act_lo_ready, DC * turn + max(d + 1, 2 * banks))

        squares_out = region(8192, TB, D)


        taken, ab_copied, selector_ready = sem("taken"), sem("ab_copied"), sem("selector_ready")
        convolved, silu_done = sem("convolved"), sem("silu_done")
        angles_ready, rows_out, rows_silu = sem("angles_ready"), sem("rows_out"), sem("rows_silu")
        trig_ready, q_rotated, k_rotated = sem("trig_ready"), sem("q_rotated"), sem("k_rotated")
        ret_scores, ret_masked, ret_out = sem("ret_scores"), sem("ret_masked"), sem("ret_out")
        ret_copied, ret_centered, ret_squared = sem("ret_copied"), sem("ret_centered"), sem("ret_squared")
        ret_var, ret_root, ret_scaled = sem("ret_var"), sem("ret_root"), sem("ret_scaled")
        ret_done = sem("ret_done")
        qk_squared, qk_summed, qk_root, qk_normed = (sem("qk_squared"), sem("qk_summed"), sem("qk_root"),
                                                     sem("qk_normed"))
        gate_in, gate_exp, gate_ln_in, gate_ln = sem("gate_in"), sem("gate_exp"), sem("gate_ln_in"), sem("gate_ln")
        decay_row, decay_col, decay_cols_ready = sem("decay_row"), sem("decay_col"), sem("decay_cols_ready")
        decay_exp = sem("decay_exp")
        decay_spread, expo_ready, decays_ready = sem("decay_spread"), sem("expo_ready"), sem("decays_ready")
        kv_turned, k_rows, v_rows = sem("kv_turned"), sem("k_rows"), sem("v_rows")
        kk_done, kk_used, att_done, att_used = sem("kk_done"), sem("kk_used"), sem("att_done"), sem("att_used")
        inv_init, blocks_ready = sem("inv_init"), sem("blocks_ready")
        inner_done, inner_copied, outer_done, inv_updated = (sem("inner_done"), sem("inner_copied"),
                                                             sem("outer_done"), sem("inv_updated"))
        rhs_ready, new_done, new_copied = sem("rhs_ready"), sem("new_done"), sem("new_copied")
        kd_ready, state_done, state_copied = sem("kd_ready"), sem("state_done"), sem("state_copied")
        from_state, q_state, q_state_copied = sem("from_state"), sem("q_state"), sem("q_state_copied")
        o_done, o_copied, o_squared, o_mean, o_root = (sem("o_done"), sem("o_copied"), sem("o_squared"),
                                                       sem("o_mean"), sem("o_root"))
        z_weighted = sem("z_weighted")
        mixed_ready, x_again, h_ready, h_spilled = sem("mixed_ready"), sem("x_again"), sem("h_ready"), sem("h_spilled")

        att_ret = region(0, RET_HEADS, 3 * P)
        sin_t, cos_t = region(3072, SEQ), region(3328, SEQ)
        angle, turns = region(3584, SEQ), region(3840, SEQ)
        rot = region(4096, 4, 2, SEQ)
        rot_tmp = region(6144, 4, 2, SEQ)
        ret_sq = region(0, TB, 1024)
        a_mat = region(0, 4, 4, P)
        inv = region(2048, 4, 4, P)
        inv_t = region(4096, 4, 4, P)
        blocks = region(6144, 4, 4, P)
        expo_a = region(6144, 4, 4, P)
        expo_d = region(18432, 4, 4, P)
        inner = region(18432, 4, 4, P)
        att = region(20480, 4, 4, P)
        k_row = region(14336, 4, 4, P)
        v_row = region(12288, 4, 4, P)
        rhs = region(6144, 4, 4, P)
        v_new = region(18432, 4, 4, P)
        state = region(0, 2, 4, P)
        k_dec = region(1024, 2, 4, P)
        q_out = region(2048, 2, 4, P)
        o_sq = region(4096, 4, 4, P)
        selector = region(22528, DN_HEADS, P)[0:8]
        gb = sel1_t
        tmp8 = sel2_t
        gcol = gate_t[:, 0:80].rearrange("p (b c) -> p b c", b=2)
        neg_g = gate_t[:, 80:96].rearrange("p (b c) -> p b c", b=2)
        exp_g = gate_t[:, 96:112].rearrange("p (b c) -> p b c", b=2)
        neg_beta_exp = gate_t[:, 112:120]
        end_dec = gate_t[:, 120:128]
        o_stat = gate_t[:, 128:176].rearrange("p (s g) -> p s g", s=3)
        ret_stat = gate_t[:, 176:176 + 64].rearrange("p (s b h) -> p s b h", s=4, b=2)
        g_end = gate_t[:, 240:248]

        query_t = region(12288, PQ_CHUNKS, SEQ)
        keys_t = region(26624 - 2048, PQ_CHUNKS, P)
        scores = region(28672, 16, 2, P)
        scores4 = region(28672, 8, 512)
        key_in, key_work = region(20480, 2, P), region(20736, 2, P)
        cand, cand_work = region(20992, TOPK, TOPK), region(21248, TOPK * TOPK)
        picked = region(21504, 2, TOPK, TOPK)
        key_top, key_index = region(22016, 2, TOPK), region(22048, 2, TOPK).bitcast(U32)
        key_index_f = region(22080, 2, TOPK)
        best, best_index = region(22112, TOPK), region(22128, TOPK).bitcast(U32)
        ranks, ranks_f = region(22144, 2, TOPK).bitcast(U32), region(22176, 2, TOPK)
        best_all = region(22528, 16, TOPK)
        picks_all = region(22784, 2, 16, TOPK)
        gates3, gates_all = region(23296, 16, TOPK), region(23296, 16 * TOPK)
        gate_sum = region(23552, 16)
        experts = region(0, CHUNKS, SEQ)
        equal2 = equal2_t[:].rearrange("p (t c) -> p t c", t=4)
        ple = region(12288, TB, D)
        p_rows = region(4096, 2, SEQ)
        gate_sig = region(17408, 2, TB, 512)
        final_w = region(20480, D)
        final = region(24576, TB, D)
        keys_landed, scores_done, scores_ready = sem("keys_landed"), sem("scores_done"), sem("scores_ready")
        expert_bank, gates_in, gates_exp, gates_ready = (sem("expert_bank"), sem("gates_in"), sem("gates_exp"),
                                                         sem("gates_ready"))
        sel_turned, sel_ready = sem("sel_turned"), sem("sel_ready")
        onehot1_ready, onehot2_ready = sem("onehot1_ready"), sem("onehot2_ready")
        gates_summed, gates_applied = sem("gates_summed"), sem("gates_applied")
        stage_hi_ready, stage_lo_ready = sem("stage_hi_ready"), sem("stage_lo_ready")
        h_back, p_landed, final_landed = sem("h_back"), sem("p_landed"), sem("final_landed")
        sigmoid_ready, out_ready, out_stored = (sem("sigmoid_ready"), [sem(f"out_ready{b}") for b in range(TB)],
                                                sem("out_stored"))
        p_hi_ready, p_lo_ready, weighted, scale_ready = (sem("p_hi_ready"), sem("p_lo_ready"), sem("weighted"),
                                                         sem("scale_ready"))

        psg = ps[:].rearrange("p b (j n) -> p b j n", j=4)
        ps2 = ps[:, 0:4, :].rearrange("p (b c) n -> p b (c n)", b=2)
        spread = ps[:, 4:8, :].rearrange("p b (c t) -> p (b c) t", c=2)
        qkv2 = region(8192, 8, 512)
        neg_a = mixc[:, C_NEGA:C_NEGA + P].unsqueeze(1)
        neg_d = mixc[:, C_NEGD:C_NEGD + P].unsqueeze(1)
        level_mask = mixc[:, 0:LEVELS * P].rearrange("p (l n) -> p l n", l=LEVELS)
        ret_decay = mixc[:, C_RETD:].rearrange("p (h n) -> p h n", h=RET_HEADS)
        eps_c = one[:, 1:2]
        trig_k, trig_p = region(6144, SEQ), region(6400, SEQ)

        def channel(what, g, j):
            b = g // 2
            return qkv[:, 8 * what + 4 * (g % 2) + j, b * P:(b + 1) * P]

        def o_rows(g):
            return mixed[:, g // 2, (g % 2) * 512:(g % 2 + 1) * 512].rearrange("p (j n) -> p j n", j=4)

        def rotate(eng, at, x):
            x1, x2 = rqk[:, 2 * at:2 * at + 2], rqk[:, 2 * at + 2:2 * at + 4]
            sin_b, cos_b = (t.unsqueeze(1).broadcast_to([P, 2, SEQ]) for t in (sin_t, cos_t))
            t1, t2 = rot_tmp[:, at], rot_tmp[:, at + 1]
            eng.drain()
            eng.tensor_tensor(t1, x1, sin_b if x else cos_b, ALU.mult)
            eng.tensor_tensor(t2, x2, cos_b if x else sin_b, ALU.mult)
            eng.drain()
            return eng.tensor_tensor(rot[:, at + x], t1, t2, ALU.add if x else ALU.subtract)

        def take_ple(dve, g):
            dve.wait_ge(lo_used, T_PLE + g + 1)
            dve.tensor_copy(ple[:, :, 512 * g:512 * (g + 1)],
                            ps[:, 2 - 2 * (g % 2):4 - 2 * (g % 2), :]).then_inc(taken, 1)

        def start_of_stream(base, i, c):
            return base == 0 and isinstance(i, int) and i == 0 and c == 0

        block = ctx.enter_context(nc.Block())

        @block.sync
        def _(sp):
            for tb in range(TB):
                sp.dma_start(xh[:, tb], x[tb * P:(tb + 1) * P, :]).then_inc(x_landed[tb], 16)
            sp.dma_start(keep[:], keep_c).then_inc(keep_landed, 16)
            sp.dma_start(ncol[:], norm_cols).then_inc(keep_landed, 16)
            for k in range(RAW):
                load_tile(sp, k, k, w_in_cols[k], first=True)
            sp.dma_start(conv_w, conv_cols).then_inc(conv_landed, 16)

            def stream(base, source, start, stop):
                with sp.Fori(start, stop) as i:
                    for k in range(RAW):
                        n, slot, _, _ = tile_at(base, i, RAW, k)
                        load_tile(sp, n, slot, source[ds(i * RAW + k, 1)].rearrange("a p f -> (a p) f"))

            stream(0, w_in_cols, 1, T_ROW // RAW)
            stream(T_ROW, w_in_rows, 0, (T_OUT - T_ROW) // RAW)
            stream(T_OUT, w_out, 0, (T_PQ - T_OUT) // RAW)
            stream(T_PQ, w_pq, 0, (T_U - T_PQ) // RAW)
            stream(T_U, expert_u, 0, (T_V - T_U) // RAW)
            stream(T_V, expert_v, 0, (T_PLE - T_V) // RAW)
            stream(T_PLE, w_ple, 0, 1)
            stream(T_V + 4, expert_v, (T_PLE - T_V) // RAW, 2 * CHUNKS // RAW)
            stream(T_GATE, w_gate, 0, (T_END - T_GATE) // RAW)
            for tb in (1, 0):
                sp.wait_ge(out_ready[tb], 1)
                sp.dma_start(out[tb * P:(tb + 1) * P, :], final[:, tb]).then_inc(out_stored, 16)
            sp.wait_ge(out_stored, 16 * TB)

        @block.scalar
        def _(act):
            for tb in range(TB):
                act.wait_ge(x_landed[tb], 16)
                square(act, xh, tb, 0, 1)
            act_root(act, 0)
            for k in range(2):
                round_tile(act, *tile_at(0, 0, 4, k), first=True)
            act.wait_ge(keep_landed, 32)
            act_turn(act, 0, 0)

            def copy_chunk(c, parity):
                act.wait_ge(lo_used, 2 * c + 2)
                act.activation(conv_in[:, parity, :], ps[:, parity, 0:SEQ], ACT.Copy).then_inc(taken, 1)

            def silu_chunk(c, parity):
                hold(act, "act", convolved, c + 1)
                act.activation(qkv[:, ds(c, 1), :], conv_y[:, parity:parity + 1, :], ACT.Silu).then_inc(silu_done, 1)

            def copy_rqk(c, parity):
                hold(act, "act", lo_used, 2 * c + 2)
                act.activation(rqk[:, ds(c - CONV_CHUNKS, 1), :], ps[:, parity:parity + 1, 0:SEQ],
                               ACT.Copy).then_inc(taken, 1)

            def chunk_round(base, i, after, skip=0):
                for c in range(2):
                    for k in range(2)[skip * (1 - c):]:
                        round_tile(act, *tile_at(base, i, 4, 2 * c + k), first=start_of_stream(base, i, c))
                    after(i, c)

            def copy_and_silu(i, c):
                copy_chunk(2 * i + c - 1, 1 - c)
                silu_chunk(2 * i + c - 2, c)

            def silu_and_rqk(i, c):
                if c == 0:
                    copy_and_silu(i, c)
                else:
                    copy_rqk(CONV_CHUNKS, 0)
                    silu_chunk(CONV_CHUNKS - 1, 1)

            chunk_round(0, 0, lambda i, c: c and copy_chunk(0, 0), skip=2)
            with act.Fori(1, CONV_CHUNKS // 4) as i:
                chunk_round(0, i, copy_and_silu)
            act.dma_start(ab_w, w_ab).then_inc(consts_landed, 16)
            act.dma_start(mixc, mix_c).then_inc(consts_landed, 16)
            act.dma_start(ab_col[:, 0:2], ab_cols).then_inc(consts_landed, 16)
            act.dma_start(dn_w, dn_norm.partition_broadcast(P)).then_inc(consts_landed, 16)
            act.dma_start(mixed[:, 0, 0:1024], ret_gn_w.partition_broadcast(P)).then_inc(consts_landed, 16)
            act.dma_start(mixed[:, 1, 0:1024], ret_gn_b.partition_broadcast(P)).then_inc(consts_landed, 16)
            act.dma_start(pos_i, positions.partition_broadcast(P)).then_inc(consts_landed, 16)
            with act.Fori(CONV_CHUNKS // 4, CONV_CHUNKS // 2) as i:
                chunk_round(0, i, copy_and_silu)
            chunk_round(0, CONV_CHUNKS // 2, silu_and_rqk)
            with act.Fori(CONV_CHUNKS // 2 + 1, IN_CHUNKS // 2) as i:
                chunk_round(0, i, lambda i, c: copy_rqk(2 * i + c - 1, 1 - c))
            for k in range(4):
                round_tile(act, *tile_at(T_ROW, 0, 4, k))
                if k == 1:
                    copy_rqk(IN_CHUNKS - 1, 1)
            act.wait_ge(angles_ready, 2)
            act.activation(sin_t, angle, ACT.Sin).then_inc(trig_ready, 1)
            act.activation(cos_t, turns, ACT.Sin).then_inc(trig_ready, 1)
            for k in range(4):
                round_tile(act, *tile_at(T_ROW + 4, 0, 4, k))
            act.wait_ge(gate_in, 1)
            act.activation(tmp8[0:8, :], tmp8[0:8, :], ACT.Exp).then_inc(gate_exp, 1)
            act.activation(tmp8[32:40, :], tmp8[32:40, :], ACT.Exp, scale=-1.0).then_inc(gate_exp, 1)
            act.activation(ab_col[:, 2:3], ab_col[:, 0:1], ACT.Exp).then_inc(gate_exp, 1)
            for k in range(4):
                round_tile(act, *tile_at(T_ROW + 8, 0, 4, k))
            act.wait_ge(gate_ln_in, 1)
            act.activation(tmp8[0:8, :], tmp8[0:8, :], ACT.Ln).then_inc(gate_ln, 1)
            for k in range(4):
                round_tile(act, *tile_at(T_ROW + 12, 0, 4, k))
            with act.Fori(0, 8) as p:
                for k in range(4):
                    round_tile(act, *tile_at(T_ROW + 16, p, 4, k))
                    if k == 0:
                        act.activation(squares, qkv2[:, ds(p, 1), :].rearrange("p a n -> p (a n)"),
                                       ACT.Square).then_inc(qk_squared, 1)
                    if k == 2:
                        act.wait_ge(qk_summed, p + 1)
                        act.activation(roots, ps[:, 5, :], ACT.Sqrt, bias=eps_c).then_inc(qk_root, 1)
            meet(act, 1)

            act.activation(rows[:, 0:2], rows[:, 0:2], ACT.Silu).then_inc(rows_silu, 1)
            act.activation(rows[:, 4:6], rows[:, 4:6], ACT.Silu).then_inc(rows_silu, 1)

            for tb in range(TB):
                act.wait_ge(ret_out, tb + 1)
                act.activation(mixed[:, tb, 1024:2048], ps2[:, tb], ACT.Copy).then_inc(ret_copied, 1)
            for tb in range(TB):
                act.wait_ge(ret_centered, tb + 1)
                act.activation(ret_sq[:, tb], mixed[:, tb, 1024:2048], ACT.Square).then_inc(ret_squared, 1)
            act.wait_ge(decay_cols_ready, 1)
            act.activation(exp_g, gcol[:, :, 0:8], ACT.Exp).then_inc(decay_exp, 1)
            act.wait_ge(decay_cols_ready, 2)
            act.activation(end_dec, end_dec, ACT.Exp).then_inc(decay_exp, 1)
            act.wait_ge(ret_var, 1)
            act.activation(ret_stat[:, 2], ret_stat[:, 1], ACT.Sqrt).then_inc(ret_root, 1)
            for g in range(4):
                act.wait_ge(expo_ready, 2 * g + 2)
                for j in range(4):
                    h = 4 * (g % 2) + j
                    act.activation(expo_a[:, g, j], expo_a[:, g, j], ACT.Exp, bias=gcol[:, g // 2, h:h + 1])
                    e = act.activation(expo_d[:, g, j], expo_d[:, g, j], ACT.Exp, bias=neg_g[:, g // 2, h:h + 1])
                e.then_inc(decays_ready, 1)
            for g in range(4):
                act.wait_ge(kv_turned, 2 * g + 1)
                act.activation(k_row[:, g], psg[:, 2 * g], ACT.Copy).then_inc(k_rows, 1)
            with act.Fori(0, LEVELS) as level:
                for g in range(4):
                    act.wait_ge(inner_done, 4 * level + g + 1)
                    act.activation(inner[:, g], psg[:, g], ACT.Copy).then_inc(inner_copied, 1)
            act.wait_ge(inv_updated, 4 * LEVELS + 4)
            for j in range(8):
                e = act.activation(k_dec[:, j // 4, j % 4], k_row[:, j // 4, j % 4], ACT.Copy, scale=end_dec[:, j:j + 1])
            e.then_inc(kd_ready, 1)
            for g in range(2):
                act.wait_ge(state_done, g + 1)
                act.activation(state[:, g], psg[:, 4 + g], ACT.Copy).then_inc(state_copied, 1)
            for g in range(2):
                act.wait_ge(q_state, g + 1)
                for j in range(4):
                    h = 4 * g + j
                    e = act.activation(q_out[:, g, j], psg[:, 2 + g, j], ACT.Copy, scale=exp_g[:, 1, h:h + 1])
                e.then_inc(q_state_copied, 1)
            act.wait_ge(o_mean, 1)
            act.activation(o_stat[:, 2], o_stat[:, 1], ACT.Sqrt).then_inc(o_root, 1)
            meet(act, 2)
            act.dma_start(xn, x.rearrange("(b p) d -> p b d", p=P)).then_inc(x_again, 16)
            for k in range(2):
                round_tile(act, *tile_at(T_OUT, 0, 4, k))
            act_turn(act, 1, None)
            act.dma_start(keys_t, sub_keys_t).then_inc(keys_landed, 16)

            def group_rounds(base, after):
                for n in range(4 * 8):
                    if n >= 2:
                        round_tile(act, *tile_at(base + n // 4 * 4, 0, 4, n % 4))
                    if n % 8 == 3 and n > 8:
                        after(n // 8 - 1)

            def square_group(g, before):
                act.wait_ge(taken, before + g + 1)
                for tb in range(TB):
                    square(act, xh, tb, g, 4)

            group_rounds(T_OUT, lambda g: square_group(g, TAKEN_OUT - 4))
            for k in range(2):
                round_tile(act, *tile_at(T_PQ, 0, 4, k))
            square_group(3, TAKEN_OUT - 4)
            act.wait_ge(h_ready, 1)
            act.dma_start(h_spill.rearrange("(b p) d -> p b d", p=P), xh).then_inc(h_spilled, 16)
            act_root(act, 1)
            act_turn(act, 2, 1)
            for k in range(2, 4):
                round_tile(act, *tile_at(T_PQ, 0, 4, k))
            with act.Fori(1, PQ_CHUNKS // 2) as i:
                for k in range(4):
                    round_tile(act, *tile_at(T_PQ, i, 4, k))
            for b in range(8):
                act.wait_ge(scores_done, b + 1)
                e = act.activation(scores4[:, b], ps[:, b, :], ACT.Copy).then_inc(scores_ready, 1)
            act.wait_ge(h_spilled, 16)
            act.wait_ge(scores_ready, 8)
            act.sem_inc(expert_bank, 2)

            def gelu_chunk(c, parity):
                hold(act, "act", lo_used, T_U + 2 * c + 2)
                act.activation(experts[:, ds(c, 1), :], ps[:, parity:parity + 1, 0:SEQ], ACT.Gelu).then_inc(expert_bank, 1)

            def expert_round(i, first=False):
                for c in range(2):
                    for k in range(2):
                        round_tile(act, *tile_at(T_U, i, 4, 2 * c + k))
                    if not (first and c == 0):
                        gelu_chunk(2 * i + c - 1, 1 - c)

            expert_round(0, first=True)
            with act.Fori(1, TOPK_CHUNKS // 2) as i:
                expert_round(i)
            act.wait_ge(gates_in, 1)
            act.activation(gates_all, gates_all, ACT.Exp).then_inc(gates_exp, 1)
            with act.Fori(TOPK_CHUNKS // 2, CHUNKS // 2) as i:
                expert_round(i)
            gelu_chunk(CHUNKS - 1, 1)

            def value_round(half, i, late=0):
                for c in range(4):
                    v = CHUNKS * half + 4 * i + c
                    hold(act, "act", lo_used, T_V + v + late - 1)
                    act.activation(stage_hi[:, c % 2:c % 2 + 1, :], experts[:, ds(4 * i + c, 1), :],
                                   ACT.Copy).then_inc(stage_hi_ready, 1)
                    round_tile(act, T_V + v + late, c % RAW, c % SPLIT, (T_V + late) // RAW + CHUNKS // RAW * half + i)

            act.wait_ge(gates_applied, GROUPS + 2)
            with act.Fori(0, CHUNKS // 8) as i:
                value_round(0, i)
            act.wait_ge(gates_applied, 2 * GROUPS + 2)
            with act.Fori(CHUNKS // 8, CHUNKS // 4) as i:
                value_round(0, i)
            with act.Fori(0, CHUNKS // 8) as i:
                value_round(1, i)
            act.wait_ge(stage_lo_ready, CHUNKS + CHUNKS // 2)
            act.dma_start(xh, h_spill.rearrange("(b p) d -> p b d", p=P)).then_inc(h_back, 16)
            act.dma_start(p_rows, p_t).then_inc(p_landed, 16)
            with act.Fori(CHUNKS // 8, PLE_CHUNK // 4) as i:
                value_round(1, i)
            act.wait_ge(p_landed, 16)
            act.activation(act_hi[:, 0:2, :], p_rows, ACT.Copy).then_inc(p_hi_ready, 1)
            for k in range(4):
                round_tile(act, *tile_at(T_PLE, 0, 4, k))
            act.wait_ge(taken, TAKEN_H0)
            for tb in range(TB):
                square(act, xh, tb, 0, 2)
            with act.Fori(PLE_CHUNK // 4, CHUNKS // 4) as i:
                value_round(1, i, late=4)
            act.wait_ge(stage_lo_ready, 2 * CHUNKS)
            act.dma_start(final_w, norm_final.partition_broadcast(P)).then_inc(final_landed, 16)
            for k in range(2):
                round_tile(act, *tile_at(T_GATE, 0, 4, k))
            for tb in range(TB):
                act.wait_ge(taken, TAKEN_H - TB + tb + 1)
                square(act, xh, tb, 1, 2)
            act_root(act, 2)
            act_turn(act, 3, 2)

            def sigmoid_group(g, parity):
                act.wait_ge(lo_used, T_GATE + 8 * g + 8)
                act.wait_ge(taken, TAKEN_H + g - 1)
                act.activation(gate_sig[:, parity], ps[:, 2 - 2 * parity:4 - 2 * parity, :],
                               ACT.Sigmoid).then_inc(sigmoid_ready, 1)

            def sigmoid_and_square(g):
                sigmoid_group(g, g % 2)
                if g >= 1:
                    square_group(g - 1, TAKEN_H)

            group_rounds(T_GATE, sigmoid_and_square)
            sigmoid_and_square(3)
            square_group(3, TAKEN_H)
            act_root(act, 3)
            act.wait_ge(weighted, 4)
            act.wait_ge(scale_ready, 1)
            act.activation(final[:, 0], final[:, 0], ACT.Copy, scale=stat[:, 14:15]).then_inc(out_ready[0], 1)

        @block.vector
        def _(dve):
            dve.memset(ones_m, 1.0)
            dve.memset(eps_c, EPS)
            dve.wait_ge(keep_landed, 32)
            dve_norm(dve, 0, 1, TB)
            for k in range(2):
                rest_tile(dve, *tile_at(0, 0, 4, k)[:3], first=True)
            dve_turn(dve, 0, 0)
            dve.wait_ge(conv_landed, 16)

            def convolve(c, parity):
                if not (isinstance(c, int) and c < 2):
                    dve.wait_ge(silu_done, c - 1)
                dve.wait_ge(taken, c + 1)
                y, src = conv_y[:, parity, :], conv_in[:, parity, :]
                dve.tensor_scalar(y, src, conv_w[:, ds(4 * c + 3, 1)], None, ALU.mult)
                for s in range(1, CONV_W):
                    dve.drain()
                    e = dve.scalar_tensor_tensor(y[:, s:], src[:, 0:SEQ - s], conv_w[:, ds(4 * c + 3 - s, 1)],
                                                 y[:, s:], ALU.mult, ALU.add)
                e.then_inc(convolved, 1)

            def chunk_round(base, i, after, skip=0):
                for c in range(2):
                    for k in range(2)[skip * (1 - c):]:
                        rest_tile(dve, *tile_at(base, i, 4, 2 * c + k)[:3], first=start_of_stream(base, i, c))
                    after(i, c)

            chunk_round(0, 0, lambda i, c: c and convolve(0, 0), skip=2)
            chunk_round(0, 1, lambda i, c: convolve(2 * i + c - 1, 1 - c))
            with dve.Fori(2, CONV_CHUNKS // 2) as i:
                chunk_round(0, i, lambda i, c: convolve(2 * i + c - 1, 1 - c))
            chunk_round(0, CONV_CHUNKS // 2, lambda i, c: None if c else convolve(CONV_CHUNKS - 1, 1))
            with dve.Fori(CONV_CHUNKS // 2 + 1, IN_CHUNKS // 2) as i:
                chunk_round(0, i, lambda i, c: None)

            def take_rows(g, parity):
                dve.wait_ge(lo_used, T_ROW + 8 * g + 8)
                dve.tensor_scalar(rows[:, ds(g, 1)].rearrange("p a b c -> p (a b) c"),
                                  ps[:, 2 - 2 * parity:4 - 2 * parity, :], 1.0, None, ALU.mult).then_inc(taken, 1)

            def group_round(base, i, take, first=False, skip=0, between={}):
                for g in range(2):
                    for k in range(8):
                        if 8 * g + k >= skip:
                            rest_tile(dve, *tile_at(base, i, 16, 8 * g + k)[:3])
                        if k == 1 and not (first and g == 0):
                            take(2 * i + g - 1, 1 - g)
                        if 8 * g + k in between:
                            between[8 * g + k]()

            x8, m8 = tmp8[0:8, :], gb[0:8, :]

            def gates_first():
                dve.tensor_copy(tmp8[0:64, :], ps[0:64, 4, 0:SEQ]).then_inc(ab_copied, 1)
                dve.memset(gb[0:64, :], 0.0)
                dve.drain()
                dve.tensor_scalar(x8, x8, ab_col[:, 1:2], None, ALU.add)
                dve.drain()
                dve.tensor_scalar(m8, x8, 0.0, None, ALU.max)
                dve.drain()
                dve.scalar_tensor_tensor(x8, m8, -2.0, x8, ALU.mult, ALU.add).then_inc(gate_in, 1)

            def gates_second():
                dve.wait_ge(gate_exp, 3)
                dve.tensor_scalar(x8, x8, 1.0, None, ALU.add).then_inc(gate_ln_in, 1)
                dve.tensor_scalar(tmp8[32:40, :], tmp8[32:40, :], 1.0, None, ALU.add)
                dve.tensor_scalar(ab_col[:, 3:4], ab_col[:, 2:3], -1.0, None, ALU.mult)
                dve.drain()
                dve.reciprocal(gb[32:40, :], tmp8[32:40, :])

            def gates_third():
                dve.wait_ge(gate_ln, 1)
                dve.tensor_tensor(x8, x8, m8, ALU.add)
                dve.drain()
                dve.tensor_scalar(x8, x8, ab_col[:, 3:4], None, ALU.mult)
                dve.drain()
                for b in range(TB):
                    e = dve.tensor_tensor_scan(gb[0:8, b * P:(b + 1) * P], ones_m[0:8, :], x8[:, b * P:(b + 1) * P], 0.0,
                                               ALU.mult, ALU.add)
                e.then_inc(decay_row, 1)

            def rotate_q(x):
                dve.wait_ge(taken, IN_CHUNKS)
                dve.wait_ge(trig_ready, 2)
                rotate(dve, 0, x).then_inc(q_rotated, 1)

            def normalise(p):
                dve.wait_ge(qk_root, p + 1)
                dve.reciprocal(roots, roots)
                dve.drain()
                dve.scalar_tensor_tensor(qkv2[:, p], qkv2[:, p], DK ** -0.5 if p < 4 else 1.0, roots,
                                         ALU.mult, ALU.mult).then_inc(qk_normed, 1)

            group_round(T_ROW, 0, take_rows, first=True, between={
                3: gates_first, 9: gates_second, 13: gates_third,
                11: lambda: rotate_q(0), 15: lambda: rotate_q(1)})
            for i in (1, 2):
                group_round(T_ROW, i, take_rows, between={
                    4 * u + 2: lambda p=4 * i - 4 + u: normalise(p) for u in range(4)})
            take_rows(ROW_GROUPS - 1, 1)
            meet(dve, 1)
            dve.wait_ge(qk_summed, 8)
            dve.drain()
            dve.tensor_copy(selector, ident[0:8, 0:8].unsqueeze(2).broadcast_to([8, 8, P])).then_inc(selector_ready, 1)
            for h in range(RET_HEADS):
                dve.wait_ge(ret_scores, h + 1)
                dve.tensor_tensor(att_ret[:, h], ps[:, h, 0:3 * P], ret_decay[:, h], ALU.mult).then_inc(ret_masked, 1)
            r4 = [mixed[:, tb, 1024:2048].rearrange("p (h d) -> p h d", h=RET_HEADS) for tb in range(TB)]
            s4 = [ret_sq[:, tb].rearrange("p (h d) -> p h d", h=RET_HEADS) for tb in range(TB)]

            def over_head(s, tb):
                return ret_stat[:, s, tb].unsqueeze(2).broadcast_to([P, RET_HEADS, RET_DV])

            for tb in range(TB):
                dve.wait_ge(ret_copied, tb + 1)
                dve.tensor_reduce(ret_stat[:, 0, tb], r4[tb], AX_X, ALU.add)
                dve.drain()
                dve.tensor_scalar(ret_stat[:, 0, tb], ret_stat[:, 0, tb], 1.0 / RET_DV, None, ALU.mult)
                dve.drain()
                dve.tensor_tensor(r4[tb], r4[tb], over_head(0, tb), ALU.subtract).then_inc(ret_centered, 1)
            dve.wait_ge(decay_col, 1)
            dve.tensor_copy(gcol, ps[:, 0, 0:80].rearrange("p (b c) -> p b c", b=2)).then_inc(decay_cols_ready, 1)
            dve.drain()
            dve.tensor_scalar(neg_g, gcol[:, :, 0:8], -1.0, None, ALU.mult)
            dve.wait_ge(decay_spread, 1)
            dve.tensor_copy(g_end, spread[:, :, P - 1])
            dve.drain()
            dve.tensor_tensor(end_dec, g_end, gcol[:, 0, 0:8], ALU.subtract).then_inc(decay_cols_ready, 1)
            for g in range(4):
                src = spread[:, 4 * (g % 2):4 * (g % 2) + 4, (g // 2) * P:(g // 2 + 1) * P]
                dve.scalar_tensor_tensor(expo_a[:, g], src, -1.0, neg_a.broadcast_to([P, 4, P]), ALU.mult,
                                         ALU.add).then_inc(expo_ready, 1)
                dve.tensor_tensor(expo_d[:, g], src, neg_d.broadcast_to([P, 4, P]), ALU.add).then_inc(expo_ready, 1)
            dve.wait_ge(decay_exp, 1)
            dve.scalar_tensor_tensor(neg_beta_exp, exp_g[:, 1], -1.0, gcol[:, 1, 32:40], ALU.mult, ALU.mult)
            for tb in range(TB):
                dve.wait_ge(ret_squared, tb + 1)
                dve.tensor_reduce(ret_stat[:, 1, tb], s4[tb], AX_X, ALU.add)
            dve.drain()
            dve.tensor_scalar(ret_stat[:, 1], ret_stat[:, 1], 1.0 / RET_DV, EPS, ALU.mult, ALU.add).then_inc(ret_var, 1)
            dve.wait_ge(ret_root, 1)
            dve.reciprocal(ret_stat[:, 3], ret_stat[:, 2])
            dve.drain()
            for tb in range(TB):
                dve.tensor_tensor(r4[tb], r4[tb], over_head(3, tb), ALU.mult).then_inc(ret_scaled, 1)
            dve.wait_ge(ret_out, 2)
            for t in (inv, inv_t):
                e = dve.tensor_copy(t.rearrange("p g j n -> p (g j) n"), ident.unsqueeze(1).broadcast_to([P, 16, P]))
            e.then_inc(inv_updated, 4)
            dve.wait_ge(kv_turned, 8)
            for g in range(4):
                dve.tensor_copy(v_row[:, g], psg[:, 2 * g + 1]).then_inc(v_rows, 1)
            dve.wait_ge(decays_ready, 4)
            for g in range(4):
                dve.wait_ge(kk_done, g + 1)
                for j in range(4):
                    h = 4 * (g % 2) + j
                    e = dve.scalar_tensor_tensor(a_mat[:, g, j], psg[:, g, j], gcol[:, g // 2, 32 + h:33 + h],
                                                 expo_a[:, g, j], ALU.mult, ALU.mult)
                e.then_inc(kk_used, 1)
            dve.wait_ge(ret_done, 2)
            for g in range(4):
                dve.wait_ge(att_done, g + 1)
                dve.tensor_tensor(att[:, g], psg[:, 4 + g], expo_d[:, g], ALU.mult).then_inc(att_used, 1)
            with dve.Fori(0, LEVELS) as level:
                for g in range(4):
                    dve.wait_ge(outer_done, 4 * level + g + 1)
                    dve.tensor_tensor(inv[:, g], inv[:, g], psg[:, 4 + 2 * (g % 2)], ALU.subtract)
                    dve.tensor_tensor(inv_t[:, g], inv_t[:, g], psg[:, 5 + 2 * (g % 2)],
                                      ALU.subtract).then_inc(inv_updated, 1)
            for g in range(2):
                for j in range(4):
                    e = dve.tensor_scalar(rhs[:, g, j], v_row[:, g, j], gcol[:, 0, 32 + 4 * g + j:33 + 4 * g + j], None,
                                          ALU.mult)
                e.then_inc(rhs_ready, 1)
            for g in range(2):
                for j in range(4):
                    h = 4 * g + j
                    dve.tensor_scalar(v_row[:, 2 + g, j], v_row[:, 2 + g, j], gcol[:, 1, 32 + h:33 + h], None, ALU.mult)
            for g in range(2):
                dve.wait_ge(new_done, g + 1)
                dve.tensor_copy(v_new[:, g], psg[:, g]).then_inc(new_copied, 1)
            for g in range(2):
                dve.wait_ge(o_done, g + 1)
                dve.tensor_copy(o_rows(g), psg[:, 6 + g]).then_inc(o_copied, 1)
            for g in range(2):
                dve.wait_ge(from_state, g + 1)
                for j in range(4):
                    h = 4 * g + j
                    e = dve.scalar_tensor_tensor(rhs[:, 2 + g, j], psg[:, g, j], neg_beta_exp[:, h:h + 1],
                                                 v_row[:, 2 + g, j], ALU.mult, ALU.add)
                e.then_inc(rhs_ready, 1)
            for g in range(2):
                dve.wait_ge(new_done, g + 3)
                dve.tensor_copy(v_new[:, 2 + g], psg[:, 4 + g]).then_inc(new_copied, 1)
            for g in range(2):
                dve.wait_ge(q_state_copied, g + 1)
                dve.wait_ge(o_done, g + 3)
                dve.tensor_tensor(o_rows(2 + g), psg[:, g], q_out[:, g], ALU.add)
            dve.drain()
            for g in range(4):
                dve.tensor_tensor(o_sq[:, g], o_rows(g), o_rows(g), ALU.mult)
            dve.drain()
            dve.tensor_reduce(o_stat[:, 0], o_sq.rearrange("p g j n -> p (g j) n"), AX_X, ALU.add)
            dve.drain()
            dve.tensor_scalar(o_stat[:, 1], o_stat[:, 0], 1.0 / DK, EPS, ALU.mult, ALU.add).then_inc(o_mean, 1)
            dve.wait_ge(o_root, 1)
            dve.reciprocal(o_stat[:, 0], o_stat[:, 2])
            dve.wait_ge(z_weighted, 1)
            dve.drain()
            for g in range(4):
                for j in range(4):
                    dve.scalar_tensor_tensor(o_rows(g)[:, j], o_rows(g)[:, j], o_stat[:, 0, 4 * g + j:4 * g + j + 1],
                                             rows[:, g % 2, g // 2, j * P:(j + 1) * P], ALU.mult, ALU.mult)
            meet(dve, 2)
            for k in range(2):
                rest_tile(dve, *tile_at(T_OUT, 0, 4, k)[:3])
            dve_turn(dve, 1, None)

            def take_out(g, parity):
                dve.wait_ge(lo_used, T_OUT + 8 * g + 8)
                dve.tensor_tensor(xh[:, :, ds(512 * g, 512)], ps[:, 2 - 2 * parity:4 - 2 * parity, :],
                                  xn[:, :, ds(512 * g, 512)], ALU.add).then_inc(taken, 1)

            dve.wait_ge(x_again, 16)
            group_round(T_OUT, 0, take_out, first=True, skip=2)
            with dve.Fori(1, 2) as i:
                group_round(T_OUT, i, take_out)
            take_out(3, 1)
            dve.drain().then_inc(h_ready, 1)
            for k in range(2):
                rest_tile(dve, *tile_at(T_PQ, 0, 4, k)[:3])
            dve_norm(dve, 1, 4, TB + 8)
            dve_turn(dve, 2, 1)

            def take_query(c, parity):
                dve.wait_ge(lo_used, T_PQ + 2 * c + 2)
                dve.tensor_scalar(query_t[:, ds(c, 1), :], ps[:, parity:parity + 1, 0:SEQ], 1.0, None,
                                  ALU.mult).then_inc(taken, 1)

            chunk_round(T_PQ, 0, lambda i, c: c and take_query(0, 0), skip=2)
            with dve.Fori(1, PQ_CHUNKS // 2) as i:
                chunk_round(T_PQ, i, lambda i, c: take_query(2 * i + c - 1, 1 - c))
            take_query(PQ_CHUNKS - 1, 1)

            dve.wait_ge(scores_ready, 8)
            with dve.Fori(0, PK_HEADS * TB // 2) as i:
                for half in range(2):
                    unit = 2 * i + half

                    def tile(k):
                        rest_tile(dve, *tile_at(T_U, i, 12, 6 * half + k)[:3])

                    def sixteen(values, work, tops, index):
                        for v, t in zip(values, tops):
                            dve.max(t[:, 0:8], v)
                        dve.drain()
                        for v, w, t, x in zip(values, work, tops, index):
                            dve.max_index(x[:, 0:8], t[:, 0:8], v)
                            dve.match_replace(w, t[:, 0:8], v, LOWEST)
                        dve.drain()
                        yield
                        for w, t in zip(work, tops):
                            dve.max(t[:, 8:16], w)
                        dve.drain()
                        for w, t, x in zip(work, tops, index):
                            dve.max_index(x[:, 8:16], t[:, 8:16], w)
                        dve.drain()

                    tile(0)
                    dve.tensor_copy(key_in, scores[:, ds(unit, 1)].rearrange("p a k n -> p (a k) n"))
                    dve.drain()
                    for _ in sixteen([key_in[:, k] for k in range(2)], [key_work[:, k] for k in range(2)],
                                     [key_top[:, k] for k in range(2)], [key_index[:, k] for k in range(2)]):
                        tile(1)
                    tile(2)
                    dve.tensor_copy(key_index_f, key_index)
                    dve.tensor_tensor(cand, key_top[:, 0].unsqueeze(2).broadcast_to([P, TOPK, TOPK]),
                                      key_top[:, 1].unsqueeze(1).broadcast_to([P, TOPK, TOPK]), ALU.add)
                    dve.drain()
                    cand_row = cand.rearrange("p a b -> p (a b)")
                    for _ in sixteen([cand_row], [cand_work], [best], [best_index]):
                        tile(3)
                    tile(4)
                    dve.tensor_copy(best_all[:, ds(unit, 1), :], best.unsqueeze(1))
                    dve.tensor_scalar(ranks[:, 0], best_index, 4, None, ALU.logical_shift_right)
                    dve.tensor_scalar(ranks[:, 1], best_index, TOPK - 1, None, ALU.bitwise_and)
                    dve.drain()
                    dve.tensor_copy(ranks_f, ranks)
                    dve.drain()
                    dve.tensor_tensor(picked, iota[:, 0:TOPK].unsqueeze(1).unsqueeze(1).broadcast_to([P, 2, TOPK, TOPK]),
                                      ranks_f.unsqueeze(3).broadcast_to([P, 2, TOPK, TOPK]), ALU.is_equal)
                    dve.drain()
                    tile(5)
                    dve.tensor_tensor(picked, picked, key_index_f.unsqueeze(2).broadcast_to([P, 2, TOPK, TOPK]), ALU.mult)
                    dve.drain()
                    for k in range(2):
                        dve.tensor_reduce(picks_all[:, k, ds(unit, 1), :], picked[:, k], AX_X, ALU.add)
                    dve.drain()

            def plain(start, stop):
                with dve.Fori(start // 2, stop // 2) as i:
                    for k in range(4):
                        rest_tile(dve, *tile_at(T_U, i, 4, k)[:3])

            top_first = best_all[:, :, 0:1].broadcast_to([P, 16, TOPK])
            dve.tensor_tensor(gates3, best_all, top_first, ALU.subtract).then_inc(gates_in, 1)
            plain(TOPK_CHUNKS, TOPK_CHUNKS + 2)
            dve.wait_ge(gates_exp, 1)
            dve.tensor_reduce(gate_sum, gates3, AX_X, ALU.add)
            dve.drain()
            dve.reciprocal(gate_sum, gate_sum)
            dve.drain()
            dve.tensor_tensor(gates3, gates3, gate_sum.unsqueeze(2).broadcast_to([P, 16, TOPK]),
                              ALU.mult).then_inc(gates_ready, 1)
            plain(TOPK_CHUNKS + 2, TOPK_CHUNKS + 8)
            dve.wait_ge(sel_turned, 1)
            dve.tensor_copy(sel1_t[:], ps[:, 6, 0:SEQ])
            dve.tensor_copy(sel2_t[:], ps[:, 6, SEQ:2 * SEQ])
            dve.tensor_copy(gate_t[:], ps[:, 7, 0:SEQ])
            dve.drain().then_inc(sel_ready, 1)
            for part in range(3):
                dve.tensor_copy(gate_parts[:, part], gate_t[:])
                dve.drain()
                if part < 2:
                    dve.tensor_tensor(gate_t[:], gate_t[:], gate_parts[:, part], ALU.subtract)
                    dve.drain()
            plain(TOPK_CHUNKS + 8, CHUNKS // 2)

            def second_keys(q, slot, half):
                dve.drain()
                dve.wait_ge(gates_summed, q + GROUPS * half + 1)
                dve.tensor_tensor(equal2, iota[:, half * HALF_KEYS:(half + 1) * HALF_KEYS].unsqueeze(1)
                                  .broadcast_to([P, 4, HALF_KEYS]),
                                  sel2_t[:, ds(4 * q, 4)].unsqueeze(2).broadcast_to([P, 4, HALF_KEYS]), ALU.is_equal)
                dve.drain()
                dve.tensor_tensor(onehot2[:, slot], equal2.unsqueeze(2).broadcast_to([P, 4, 3, HALF_KEYS]),
                                  gate_parts[:, :, ds(4 * q, 4)].rearrange("p s t -> p t s").unsqueeze(3)
                                  .broadcast_to([P, 4, 3, HALF_KEYS]), ALU.mult).then_inc(onehot2_ready, 1)

            def apply_gates(q, slot, half):
                dve.wait_ge(gates_summed, q + GROUPS * half + 3)
                a = experts[:, half * HALF_KEYS:(half + 1) * HALF_KEYS, ds(4 * q, 4)]
                g = ps[:, 4 + slot, 0:4 * HALF_KEYS].rearrange("p (t c) -> p c t", t=4)
                dve.tensor_tensor(a, a, g, ALU.mult).then_inc(gates_applied, 1)

            dve.sem_inc(gates_applied, 2)
            dve.wait_ge(expert_bank, CHUNKS // 2 + 2)
            def expert_tiles(i, first=False):
                for c in range(2):
                    q = 2 * i + c - CHUNKS // 2
                    rest_tile(dve, *tile_at(T_U, i, 4, 2 * c)[:3])
                    second_keys(q, c, 0)
                    rest_tile(dve, *tile_at(T_U, i, 4, 2 * c + 1)[:3])
                    if not first:
                        apply_gates(q - 2, c, 0)

            expert_tiles(CHUNKS // 4, first=True)
            with dve.Fori(CHUNKS // 4 + 1, CHUNKS // 2) as i:
                expert_tiles(i)
            apply_gates(GROUPS - 2, 0, 0)
            apply_gates(GROUPS - 1, 1, 0)

            def value_tile(half, i, c, late=0):
                v = CHUNKS * half + 4 * i + c
                dve.wait_ge(stage_hi_ready, v + 1)
                dve.tensor_tensor(stage_lo[:, c % 2:c % 2 + 1, :], experts[:, ds(4 * i + c, 1), :],
                                  stage_hi[:, c % 2:c % 2 + 1, :].bitcast(F32), ALU.subtract).then_inc(stage_lo_ready, 1)
                rest_tile(dve, T_V + v + late, c % RAW, c % SPLIT)

            def gated_values(i, first=False):
                for c in range(4):
                    value_tile(0, i, c)
                    second_keys(4 * i + c, c % 2, 1)
                    if not (first and c < 2):
                        apply_gates(4 * i + c - 2, c % 2, 1)

            gated_values(0, first=True)
            with dve.Fori(1, CHUNKS // 8) as i:
                gated_values(i)
            apply_gates(GROUPS - 2, 0, 1)
            apply_gates(GROUPS - 1, 1, 1)
            with dve.Fori(CHUNKS // 8, CHUNKS // 4) as i:
                for c in range(4):
                    value_tile(0, i, c)
            with dve.Fori(0, PLE_CHUNK // 4 - 4) as i:
                for c in range(4):
                    value_tile(1, i, c)

            def add_experts(half):
                for tb in range(TB):
                    dst = xh[:, tb, half * 1024:(half + 1) * 1024].rearrange("p (b n) -> p b n", b=2)
                    dve.tensor_tensor(dst, ps[:, 4 * half + 2 * tb:4 * half + 2 * tb + 2, :], dst,
                                      ALU.add).then_inc(taken, 1)

            dve.wait_ge(h_back, 16)
            add_experts(0)
            with dve.Fori(PLE_CHUNK // 4 - 4, PLE_CHUNK // 4) as i:
                for c in range(4):
                    value_tile(1, i, c)
            dve.wait_ge(p_hi_ready, 1)
            dve.tensor_tensor(act_lo[:, 0:2, :], p_rows, act_hi[:, 0:2, :].bitcast(F32),
                              ALU.subtract).then_inc(p_lo_ready, 1)
            for k in range(4):
                rest_tile(dve, *tile_at(T_PLE, 0, 4, k)[:3])
                if k >= 1:
                    take_ple(dve, k - 1)
            with dve.Fori(PLE_CHUNK // 4, PLE_CHUNK // 4 + 1) as i:
                for c in range(4):
                    value_tile(1, i, c, late=4)
                    if c == 0:
                        take_ple(dve, 3)
            with dve.Fori(PLE_CHUNK // 4 + 1, CHUNKS // 4) as i:
                for c in range(4):
                    value_tile(1, i, c, late=4)
            dve.wait_ge(lo_used, T_GATE)
            add_experts(1)
            for k in range(2):
                rest_tile(dve, *tile_at(T_GATE, 0, 4, k)[:3])
            dve_norm(dve, 2, 2, TB + 8 + 4)
            dve_turn(dve, 3, 2)

            def take_gate(g, parity):
                dve.wait_ge(sigmoid_ready, g + 1)
                s = gate_sig[:, parity]
                dve.tensor_tensor(s, s, ple[:, :, ds(512 * g, 512)], ALU.mult)
                dve.drain()
                dst = xh[:, :, ds(512 * g, 512)]
                dve.tensor_tensor(dst, dst, s, ALU.add).then_inc(taken, 1)

            group_round(T_GATE, 0, take_gate, first=True, skip=2)
            group_round(T_GATE, 1, take_gate)
            take_gate(3, 1)
            dve_scale(dve, 3, 4, TB + 8 + 4 + 8)
            dve.sem_inc(scale_ready, 1)
            dve.wait_ge(weighted, 4)
            dve.tensor_scalar(final[:, 1], final[:, 1], stat[:, 15:16], None, ALU.mult).then_inc(out_ready[1], 1)

        @block.gpsimd
        def _(pool):
            pool.wait_ge(keep_landed, 32)
            pool.wait_ge(consts_landed, ALL_CONSTS)
            pool.wait_ge(turned, 8)
            pool.tensor_copy(angle, pos_i)
            pool.drain()
            pool.tensor_scalar(angle, angle, keep[:, C_INVF:C_INVF + 1], 1.0, ALU.mult, ALU.mult)
            pool.drain()
            for out_ap, quarter in ((turns, 0.25), (angle, 0.0)):
                k = trig_k
                pool.tensor_scalar(k, angle, 1.0 / TWO_PI, quarter, ALU.mult, ALU.add)
                pool.drain()
                pool.tensor_scalar(k, k, ROUNDER, 0.0, ALU.add, ALU.add)
                pool.drain()
                pool.tensor_scalar(k, k, -ROUNDER, 0.0, ALU.add, ALU.add)
                pool.drain()
                src = angle
                for part in TWO_PI_PARTS:
                    pool.tensor_scalar(trig_p, k, part, 1.0, ALU.mult, ALU.mult)
                    pool.drain()
                    pool.tensor_tensor(out_ap, src, trig_p, ALU.subtract)
                    pool.drain()
                    src = out_ap
                pool.tensor_scalar(out_ap, out_ap, quarter * TWO_PI, 0.0, ALU.add, ALU.add)
                pool.drain()
                pool.tensor_scalar(out_ap, out_ap, PI_BELOW, -PI_BELOW, ALU.min, ALU.max).then_inc(angles_ready, 1)
                pool.drain()
            pool.wait_ge(taken, IN_CHUNKS)
            pool.wait_ge(trig_ready, 2)
            for x in range(2):
                rotate(pool, 2, x).then_inc(k_rotated, 1)
            meet(pool, 1)
            pool.wait_ge(rows_silu, 2)
            z = rows[:, 0:2].rearrange("p g b c -> p (g b c)").rearrange("p (n d) -> p n d", d=P)
            pool.tensor_tensor(z, z, dn_w.unsqueeze(1).broadcast_to([P, 16, P]), ALU.mult).then_inc(z_weighted, 1)
            for tb in range(TB):
                pool.wait_ge(ret_scaled, tb + 1)
                r = mixed[:, tb, 1024:2048]
                pool.tensor_tensor(r, r, mixed[:, 0, 0:1024], ALU.mult)
                pool.drain()
                pool.tensor_tensor(r, r, mixed[:, 1, 0:1024], ALU.add)
                pool.drain()
                r2 = r.rearrange("p (g c) -> p g c", g=2)
                pool.tensor_tensor(r2, r2, rows[:, 4:6, tb, :], ALU.mult).then_inc(ret_done, 1)
            pool.wait_ge(kk_used, 4)
            with pool.Fori(0, LEVELS) as level:
                for g in range(4):
                    hold(pool, "pool", inv_updated, 4 * level + g + 1)
                    pool.tensor_tensor(blocks[:, g], a_mat[:, g], level_mask[:, ds(level, 1)].broadcast_to([P, 4, P]),
                                       ALU.mult).then_inc(blocks_ready, 1)
            meet(pool, 2)

            def first_keys(half, i):
                for slot in range(2):
                    q = 2 * i + slot
                    hold(pool, "pool", gates_summed, q + GROUPS * half + 1)
                    pool.tensor_copy(sel4[:, slot], sel1_t[:, ds(4 * q, 4)])
                    pool.drain()
                    for t in range(4):
                        e = pool.tensor_scalar(onehot1[:, slot, t], iota, sel4[:, slot, t:t + 1], None, ALU.is_equal)
                    e.then_inc(onehot1_ready, 1)

            pool.wait_ge(sel_ready, 1)
            for half in range(2):
                with pool.Fori(0, GROUPS // 2) as i:
                    first_keys(half, i)
            pool.wait_ge(final_landed, 16)
            for g in range(4):
                pool.wait_ge(taken, TAKEN_H + g + 1)
                c = slice(512 * g, 512 * (g + 1))
                pool.tensor_tensor(final[:, :, c], xh[:, :, c], final_w[:, c].unsqueeze(1).broadcast_to([P, TB, 512]),
                                   ALU.mult).then_inc(weighted, 1)

        @block.tensor
        def _(pe):
            pe.wait_ge(x_landed[0], 16)
            pe.wait_ge(x_landed[1], 16)
            pe.wait_ge(diag_ready, 1)
            pe_turn(pe, xh)

            def column_chunk(base, i, c, turn=None):
                for k in range(2):
                    n, _, use, _ = tile_at(base, i, 4, 2 * c + k)
                    column_tile(pe, n, use, k, ps[:, c, 0:SEQ], turn=turn)

            column_chunk(0, 0, 0, turn=0)
            column_chunk(0, 0, 1)
            with pe.Fori(1, IN_CHUNKS // 2) as i:
                for c in range(2):
                    pe.wait_ge(taken, 2 * i + c - 1)
                    column_chunk(0, i, c)
            pe.wait_ge(consts_landed, ALL_CONSTS)
            for d in range(DC):
                pe.matmul(ps[0:64, 4, 0:SEQ], ab_w[:, d, :], act_hi[:, d, :].bitcast(F32), start=(d == 0), stop=False)
                pe.matmul(ps[0:64, 4, 0:SEQ], ab_w[:, d, :], act_lo[:, d, :].bitcast(F32), start=False,
                          stop=(d == DC - 1))

            def row_groups(base, count, taken_before, turn=None, between=None):
                def row_round(i, turn):
                    for g in range(2):
                        pe.wait_ge(taken, taken_before - 1 + 2 * i + g)
                        for k in range(8):
                            n, _, use, _ = tile_at(base, i, 16, 8 * g + k)
                            row_tile(pe, n, use, k, [ps[:, 2 - 2 * g + tb, :] for tb in range(TB)],
                                     turn=turn if g == 0 else None)
                            if between:
                                between(i, 8 * g + k)

                row_round(0, turn)
                with pe.Fori(1, count // 2) as i:
                    row_round(i, None)

            def sum_squares(i, k):
                if not (isinstance(i, int) and i == 0) and k % 4 == 1:
                    p = 4 * i - 4 + k // 4
                    pe.wait_ge(qk_squared, p + 1)
                    pe.matmul(ps[:, 5, :], ones_m, squares, start=True, stop=True).then_inc(qk_summed, 1)

            row_groups(T_ROW, ROW_GROUPS, IN_CHUNKS, between=sum_squares)
            meet(pe, 1)

            pe.wait_ge(q_rotated, 2)
            pe.wait_ge(k_rotated, 2)
            for h in range(RET_HEADS):
                g, rowsl = h // 4, slice(HALF * (h % 4), HALF * (h % 4 + 1))
                for m, (c0, c1), at in ((0, (0, SEQ), 0), (1, (P, SEQ), SEQ)):
                    for x12 in range(2):
                        mm = pe.matmul(ps[:, h, at:at + c1 - c0], rot[rowsl, 2 + x12, g, m * P:(m + 1) * P],
                                       rot[rowsl, x12, g, c0:c1], start=(x12 == 0), stop=(x12 == 1))
                mm.then_inc(ret_scores, 1)
            pe.wait_ge(ret_masked, 8)
            for tb in range(TB):
                for h in range(RET_HEADS):
                    o = ps[:, 2 * tb + h // 4, (h % 4) * P:(h % 4 + 1) * P]
                    for m in range(tb + 1):
                        mm = pe.matmul(o, att_ret[:, h, (tb + m) * P:(tb + m + 1) * P],
                                       rows[:, 2 + h // 4, m, (h % 4) * P:(h % 4 + 1) * P],
                                       start=(m == 0), stop=(m == tb))
                mm.then_inc(ret_out, 1)
            pe.wait_ge(decay_row, 1)
            pe.wait_ge(selector_ready, 1)
            for h in range(DN_HEADS):
                mm = pe.matmul(spread[:, h, :], selector[:, h, :], gb[0:8, :], start=True, stop=True)
            mm.then_inc(decay_spread, 1)
            pe.wait_ge(ret_copied, 2)
            for b in range(TB):
                mm = pe.transpose(ps[:, 0, 40 * b:40 * b + 40], gb[0:40, b * P:(b + 1) * P], ident[0:40, 0:40])
            mm.then_inc(decay_col, 1)
            pe.wait_ge(qk_normed, 8)
            pe.wait_ge(expo_ready, 8)
            for g in range(4):
                for kv in range(2):
                    for j in range(4):
                        mm = pe.transpose(psg[:, 2 * g + kv, j], channel(1 + kv, g, j), ident)
                    mm.then_inc(kv_turned, 1)
            pe.wait_ge(k_rows, 4)
            pe.wait_ge(v_rows, 4)
            for g in range(4):
                for j in range(4):
                    mm = pe.matmul(psg[:, g, j], channel(1, g, j), channel(1, g, j), start=True, stop=True)
                mm.then_inc(kk_done, 1)
            for g in range(4):
                for j in range(4):
                    mm = pe.matmul(psg[:, 4 + g, j], channel(1, g, j), channel(0, g, j), start=True, stop=True)
                mm.then_inc(att_done, 1)
            pe.wait_ge(att_used, 4)
            with pe.Fori(0, LEVELS) as level:
                def inner_products(g):
                    pe.wait_ge(blocks_ready, 4 * level + g + 1)
                    for j in range(4):
                        mm = pe.matmul(psg[:, g, j], blocks[:, g, j], inv_t[:, g, j], start=True, stop=True)
                    mm.then_inc(inner_done, 1)

                def outer_products(g):
                    pe.wait_ge(inner_copied, 4 * level + g + 1)
                    pe.wait_ge(inv_updated, 4 * level + g + 3)
                    for j in range(4):
                        pe.matmul(psg[:, 4 + 2 * (g % 2), j], inner[:, g, j], inv[:, g, j], start=True, stop=True)
                    for j in range(4):
                        mm = pe.matmul(psg[:, 5 + 2 * (g % 2), j], inv[:, g, j], inner[:, g, j], start=True, stop=True)
                    mm.then_inc(outer_done, 1)

                inner_products(0)
                inner_products(1)
                outer_products(0)
                inner_products(2)
                outer_products(1)
                inner_products(3)
                outer_products(2)
                outer_products(3)
            pe.wait_ge(inv_updated, 4 * LEVELS + 4)
            for g in range(2):
                pe.wait_ge(rhs_ready, g + 1)
                for j in range(4):
                    mm = pe.matmul(psg[:, g, j], inv_t[:, g, j], rhs[:, g, j], start=True, stop=True)
                mm.then_inc(new_done, 1)
            pe.wait_ge(kd_ready, 1)
            for g in range(2):
                pe.wait_ge(new_copied, g + 1)
                for j in range(4):
                    mm = pe.matmul(psg[:, 4 + g, j], k_dec[:, g, j], v_new[:, g, j], start=True, stop=True)
                mm.then_inc(state_done, 1)
            for g in range(2):
                for j in range(4):
                    mm = pe.matmul(psg[:, 6 + g, j], att[:, g, j], v_new[:, g, j], start=True, stop=True)
                mm.then_inc(o_done, 1)
            for g in range(2):
                pe.wait_ge(state_copied, g + 1)
                for j in range(4):
                    mm = pe.matmul(psg[:, g, j], channel(1, 2 + g, j), state[:, g, j], start=True, stop=True)
                mm.then_inc(from_state, 1)
            for g in range(2):
                for j in range(4):
                    mm = pe.matmul(psg[:, 2 + g, j], channel(0, 2 + g, j), state[:, g, j], start=True, stop=True)
                mm.then_inc(q_state, 1)
            for g in range(2):
                pe.wait_ge(rhs_ready, g + 3)
                for j in range(4):
                    mm = pe.matmul(psg[:, 4 + g, j], inv_t[:, 2 + g, j], rhs[:, 2 + g, j], start=True, stop=True)
                mm.then_inc(new_done, 1)
            for g in range(2):
                pe.wait_ge(new_copied, g + 3)
                for j in range(4):
                    mm = pe.matmul(psg[:, g, j], att[:, 2 + g, j], v_new[:, 2 + g, j], start=True, stop=True)
                mm.then_inc(o_done, 1)
            meet(pe, 2)
            pe_turn(pe, mixed, scaled=False)
            row_groups(T_OUT, D // 512, IN_CHUNKS + ROW_GROUPS, turn=1)
            pe.wait_ge(diag_ready, 2)
            pe_turn(pe, xh)
            column_chunk(T_PQ, 0, 0, turn=2)
            column_chunk(T_PQ, 0, 1)
            with pe.Fori(1, PQ_CHUNKS // 2) as i:
                for c in range(2):
                    pe.wait_ge(taken, TAKEN_OUT - 1 + 2 * i + c)
                    column_chunk(T_PQ, i, c)
            pe.wait_ge(taken, TAKEN_OUT + PQ_CHUNKS)
            pe.wait_ge(keys_landed, 16)
            for b in range(8):
                for k in range(4):
                    hp = 4 * (b % 4) + k
                    mm = pe.matmul(ps[:, b, k * P:(k + 1) * P], query_t[:, hp, (b // 4) * P:(b // 4 + 1) * P],
                                   keys_t[:, hp, :], start=True, stop=True)
                mm.then_inc(scores_done, 1)

            def expert_round(i, and_then=None):
                for c in range(2):
                    pe.wait_ge(expert_bank, 2 * i + c + 1)
                    column_chunk(T_U, i, c)
                    if and_then:
                        and_then(i, c)

            def expert_chunks(start, stop, and_then=None):
                with pe.Fori(start // 2, stop // 2) as i:
                    expert_round(i, and_then)

            def sum_gates(n, slot):
                pe.wait_ge(onehot1_ready, n + 1)
                pe.wait_ge(onehot2_ready, n + 1)
                pe.wait_ge(gates_applied, n + 1)
                for t in range(4):
                    o = ps[:, 4 + slot, t * HALF_KEYS:(t + 1) * HALF_KEYS]
                    for part in range(3):
                        mm = pe.matmul(o, onehot1[:, slot, t], onehot2[:, slot, t, part], start=(part == 0),
                                       stop=(part == 2))
                mm.then_inc(gates_summed, 1)

            pe.sem_inc(gates_summed, 2)
            expert_chunks(0, TOPK_CHUNKS + 4)
            pe.wait_ge(gates_ready, 1)
            for tb in range(TB):
                for k in range(2):
                    pe.transpose(ps[:, 6, (2 * k + tb) * P:(2 * k + tb + 1) * P],
                                 picks_all[:, k, 8 * tb:8 * tb + 8].rearrange("p u r -> p (u r)"), ident)
                mm = pe.transpose(ps[:, 7, tb * P:(tb + 1) * P],
                                  gates3[:, 8 * tb:8 * tb + 8].rearrange("p u r -> p (u r)"), ident)
            mm.then_inc(sel_turned, 1)
            expert_chunks(TOPK_CHUNKS + 4, CHUNKS // 2)
            expert_round(CHUNKS // 4, lambda i, c: c and sum_gates(0, 0))
            expert_chunks(CHUNKS // 2 + 2, CHUNKS, lambda i, c: sum_gates(2 * i + c - CHUNKS // 2 - 1, 1 - c))
            sum_gates(GROUPS - 1, 1)

            def value_round(half, i, and_then=None, first=False, late=0):
                for c in range(4):
                    v, use = CHUNKS * half + 4 * i + c, c % SPLIT
                    pe.wait_ge(hi_ready, T_V + v + late + 1)
                    pe.wait_ge(stage_lo_ready, v + 1)
                    for k, a in enumerate((stage_hi, stage_lo)):
                        for tb in range(TB):
                            for b in range(2):
                                mm = pe.matmul(ps[:, 4 * half + 2 * tb + b, :], a[:, use, tb * P:(tb + 1) * P],
                                               hi[:, use, b * 512:(b + 1) * 512], start=(first and c == 0 and k == 0),
                                               stop=False, skip_group_check=True)
                    mm.then_inc(hi_used, 1)
                    pe.wait_ge(lo_ready, T_V + v + late + 1)
                    for tb in range(TB):
                        for b in range(2):
                            mm = pe.matmul(ps[:, 4 * half + 2 * tb + b, :], stage_hi[:, use, tb * P:(tb + 1) * P],
                                           lo[:, use, b * 512:(b + 1) * 512], start=False, stop=False,
                                           skip_group_check=True)
                    mm.then_inc(lo_used, 1)
                    if and_then and not (first and c == 0):
                        and_then(4 * i + c - 1, (c - 1) % 2)

            def gates_too(v, slot):
                sum_gates(v + GROUPS, slot)

            pe.wait_ge(expert_bank, CHUNKS + 2)
            value_round(0, 0, gates_too, first=True)
            with pe.Fori(1, CHUNKS // 8) as i:
                value_round(0, i, gates_too)
            gates_too(GROUPS - 1, 1)
            with pe.Fori(CHUNKS // 8, CHUNKS // 4) as i:
                value_round(0, i)
            pe.wait_ge(gates_applied, 2 * GROUPS + 2)
            value_round(1, 0, first=True)
            with pe.Fori(1, PLE_CHUNK // 4) as i:
                value_round(1, i)
            pe.wait_ge(p_lo_ready, 1)
            for g, before in enumerate((TAKEN_H0, TAKEN_H0, TAKEN_H0 + 1, TAKEN_H0 + 2)):
                n, _, use, _ = tile_at(T_PLE, 0, 4, g)
                pe.wait_ge(taken, before)
                row_tile(pe, n, use, 0, [ps[:, 2 - 2 * (g % 2) + tb, :] for tb in range(TB)], last=0)
            with pe.Fori(PLE_CHUNK // 4, CHUNKS // 4) as i:
                value_round(1, i, late=4)
            pe.wait_ge(taken, TAKEN_H)
            pe.wait_ge(diag_ready, 3)
            pe_turn(pe, xh)
            row_groups(T_GATE, D // 512, TAKEN_H, turn=3)


_OUTS = [((1, SEQ, D), "float32")]


def kernel(**inputs):
    import numpy as _np
    import concourse.bacc as _bacc
    from concourse import mybir as _mybir
    from concourse.bass_utils import run_bass_kernel_spmd as _run

    a = {k: _np.asarray(v) for k, v in inputs.items()}

    def column_tiles(w):
        n = w.shape[1] // P
        return _np.ascontiguousarray(w.reshape(2, 8, P, n, P).transpose(3, 0, 2, 1, 4).reshape(2 * n, P, TILE))

    def row_tiles(w):
        k, n = w.shape[0] // 256, w.shape[1] // 512
        return _np.ascontiguousarray(w.reshape(k, 2, P, n, 512).transpose(3, 0, 2, 1, 4).reshape(n * k, P, TILE))

    def by_column(v):
        return v.reshape(-1, P).T

    w_in = a["w_in"][0]
    at = _np.cumsum([0, CONV_CH, 1024, 8, 8, 512, 512, 1024, 1024])
    conv, z, ga, gb, rq, rk, rv, rg = (w_in[:, at[i]:at[i + 1]] for i in range(8))
    halves = [r.reshape(D, RET_HEADS, 2, HALF).transpose(0, 2, 1, 3).reshape(D, 512) for r in (rq, rk)]
    w_ab = _np.zeros((P, DC, 64), _np.float32)
    w_ab[:, :, 0:8] = ga.reshape(DC, P, 8).transpose(1, 0, 2)
    w_ab[:, :, 32:40] = gb.reshape(DC, P, 8).transpose(1, 0, 2)
    keep_c, mix_c = shape_consts()
    u = a["expert_u"][0].reshape(N_KEYS, N_KEYS, 2, 8, P)
    v = a["expert_v"][0].reshape(N_KEYS, N_KEYS, 2, TILE)
    arrays = {
        "x": a["x"][0],
        "w_in_cols": column_tiles(_np.concatenate([conv] + halves, axis=1)),
        "w_in_rows": row_tiles(_np.concatenate([z, rv, rg], axis=1)),
        "w_ab": w_ab,
        "w_out": row_tiles(a["w_out"][0]),
        "w_pq": column_tiles(a["w_pq"][0]),
        "expert_u": u.transpose(1, 2, 4, 3, 0).reshape(2 * CHUNKS, P, TILE),
        "expert_v": v.transpose(2, 1, 0, 3).reshape(2 * CHUNKS, P, TILE),
        "w_gate": row_tiles(a["w_ple_gate"][0]),
        "w_ple": row_tiles(a["w_ple_proj"][0]),
        "p_t": a["p"][0, 0].reshape(SEQ, 2, P).transpose(2, 1, 0),
        "positions": a["positions"][0],
        "keep_c": keep_c,
        "mix_c": mix_c,
        "norm_cols": _np.stack([by_column(a[k][0]) for k in ("norm_mix", "norm_ffn", "norm_ple")], axis=1),
        "conv_cols": a["conv_w"][0].reshape(CONV_CHUNKS, P, CONV_W).transpose(1, 0, 2).reshape(P, -1),
        "sub_keys_t": a["sub_keys"][0].reshape(2 * PK_HEADS, N_KEYS, P).transpose(2, 0, 1),
        "ab_cols": _np.stack([a["a_log"][0], a["dt_bias"][0]], axis=1),
        "dn_norm": a["dn_norm"][0],
        "ret_gn_w": a["ret_gn_w"][0],
        "ret_gn_b": a["ret_gn_b"][0],
        "norm_final": a["norm_final"],
    }
    arrays = {"in_" + k: _np.ascontiguousarray(v) for k, v in arrays.items()}
    nc = _bacc.Bacc("TRN2", target_bir_lowering=False, num_devices=1)
    args = [nc.dram_tensor(k, v.shape, _mybir.dt.from_np(v.dtype), kind="ExternalInput").ap()
            for k, v in arrays.items()]
    args.append(nc.dram_tensor("out_0", (SEQ, D), F32, kind="ExternalOutput").ap())
    args.append(nc.dram_tensor("h_spill", (SEQ, D), F32, kind="Internal").ap())
    build(nc, *args)
    r = _run(nc, [arrays], core_ids=[0])
    return r.results[0]["out_0"].reshape(1, SEQ, D)
```

```python
from contextlib import ExitStack

import numpy as np

import concourse.bass as bass
from concourse import mybir

F32 = mybir.dt.float32
F32R = mybir.dt.float32r
BF16 = mybir.dt.bfloat16
I32 = mybir.dt.int32
U32 = mybir.dt.uint32
ALU = mybir.AluOpType
ACT = mybir.ActivationFunctionType
AX_X = mybir.AxisListType.X
ds = bass.ds

P = 128
SEQ = 256
TB = SEQ // P
D = 2048
DC = D // P
DN_HEADS, DK = 8, 128
RET_HEADS, RET_DK, RET_DV = 8, 64, 128
HALF = RET_DK // 2
CONV_CH = 3 * DN_HEADS * DK
CONV_W = 4
N_KEYS = 128
PK_HEADS = 8
TOPK = 16
PLE = 256
ALL_CONSTS = 16 * 7
EPS = 1e-6
MASKED = -1e30
LOWEST = -3.0e38
TOPK_CHUNKS = 56
GROUPS = SEQ // 4
HALF_KEYS = N_KEYS // 2
TWO_PI = 6.283185307179586
TWO_PI_PARTS = (6.28125, 0.001934051513671875, 1.2556659146142806e-06)
PI_BELOW = 3.1415925
ROUNDER = 12582912.0
LEVELS = 7

TILE = 1024
RAW = 4
SPLIT = 2
CONV_CHUNKS = CONV_CH // P
RQK_CHUNKS = 2 * RET_HEADS * RET_DK // P
IN_CHUNKS = CONV_CHUNKS + RQK_CHUNKS
ROW_GROUPS = 6
T_ROW = 2 * IN_CHUNKS
AB_ROUND = IN_CHUNKS // 2 - 2
T_OUT = T_ROW + 8 * ROW_GROUPS
T_PQ = T_OUT + 8 * D // 512
PQ_CHUNKS = PK_HEADS * 2
T_U = T_PQ + 2 * PQ_CHUNKS
CHUNKS = N_KEYS
T_V = T_U + 2 * CHUNKS
PLE_CHUNK = CHUNKS * 3 // 4
T_PLE = T_V + CHUNKS + PLE_CHUNK
T_GATE = T_V + 2 * CHUNKS + 4
T_END = T_GATE + 8 * D // 512

TAKEN_OUT = IN_CHUNKS + ROW_GROUPS + D // 512
TAKEN_H0 = TAKEN_OUT + PQ_CHUNKS + TB
TAKEN_PLE = TAKEN_H0 + 4
TAKEN_H = TAKEN_PLE + TB

C_IDENT, C_IOTA, C_INVF = 0, 128, 256
C_KEEP = 257
C_LEVEL = 0
C_NEGA = C_LEVEL + LEVELS * P
C_NEGD = C_NEGA + P
C_RETD = C_NEGD + P
C_MIX = C_RETD + RET_HEADS * 3 * P


def shape_consts():
    i = np.arange(P)
    keep = np.zeros((P, C_KEEP), np.float32)
    keep[:, C_IDENT:C_IDENT + P] = np.eye(P)
    keep[:, C_IOTA:C_IOTA + P] = i[None, :]
    half = np.arange(HALF, dtype=np.float32)
    inv_freq = np.float32(10000.0) ** (-half / np.float32(HALF))
    keep[:, C_INVF] = inv_freq[i % HALF]
    mix = np.zeros((P, C_MIX), np.float32)
    for level in range(LEVELS):
        a, b = i[:, None] >> level, i[None, :] >> level
        mix[:, C_LEVEL + level * P:C_LEVEL + (level + 1) * P] = (a == b + 1) & (b % 2 == 0)
    mix[:, C_NEGA:C_NEGA + P] = np.where(i[:, None] > i[None, :], 0.0, MASKED)
    mix[:, C_NEGD:C_NEGD + P] = np.where(i[None, :] >= i[:, None], 0.0, MASKED)
    log_gamma = np.log1p(-np.exp2(-5.0 - np.arange(RET_HEADS)))
    rel = (i[None, :] - i[:, None]).astype(np.float64)
    for h in range(RET_HEADS):
        near = np.where(rel >= 0, np.exp(np.maximum(rel, 0) * log_gamma[h]), 0.0)
        far = np.exp((rel + P) * log_gamma[h])
        d = np.concatenate([near, far, near], axis=1) * RET_DK ** -0.5
        mix[:, C_RETD + h * 3 * P:C_RETD + (h + 1) * 3 * P] = d
    return keep, mix


def build(nc, x, w_in_cols, w_in_rows, w_ab, w_out, w_pq, expert_u, expert_v, w_gate, w_ple, p_t,
          positions, keep_c, mix_c, norm_cols, conv_cols, sub_keys_t, ab_cols, dn_norm, ret_gn_w,
          ret_gn_b, norm_final, out, h_spill):
    with ExitStack() as ctx:
        def sb(name, shape, dt=F32):
            return ctx.enter_context(nc.sbuf_tensor(name, shape, dt))

        def sem(name):
            return ctx.enter_context(nc.semaphore(name))

        arena = sb("arena", [P, CHUNKS * SEQ])
        raw = sb("raw", [P, RAW, TILE])
        hi = sb("hi", [P, SPLIT, TILE], F32R)
        lo = sb("lo", [P, SPLIT, TILE], F32R)
        act_hi = sb("act_hi", [P, DC, SEQ], F32R)
        act_lo = sb("act_lo", [P, DC, SEQ], F32R)
        stage_hi = sb("stage_hi", [P, 2, SEQ], F32R)
        stage_lo = sb("stage_lo", [P, 2, SEQ], F32R)
        keep = sb("keep", [P, C_KEEP])
        ncol = sb("ncol", [P, 3, DC])
        sel1_t = sb("sel1_t", [P, SEQ])
        sel2_t = sb("sel2_t", [P, SEQ])
        gate_t = sb("gate_t", [P, SEQ])
        ab_col = sb("ab_col", [8, 4])
        gate_parts = sb("gate_parts", [P, 3, SEQ], BF16)
        onehot1 = sb("onehot1", [P, 2, 4, N_KEYS], BF16)
        onehot2 = sb("onehot2", [P, 2, 4, 3, HALF_KEYS], BF16)
        equal2_t = sb("equal2", [P, 4 * HALF_KEYS], BF16)
        sel4 = sb("sel4", [P, 2, 4])
        stat = sb("stat", [P, 16])
        warm = sb("warm", [P, 1])
        one = sb("one", [P, 2])
        ps = ctx.enter_context(nc.psum_tensor("ps", [P, 8, 512], F32))
        ident = keep[:, C_IDENT:C_IDENT + P]
        iota = keep[:, C_IOTA:C_IOTA + P]

        mixer_small = onehot1[:].rearrange("p a b c -> p (a b c)").bitcast(F32)
        dn_w, ones_m = mixer_small[:, 0:P], mixer_small[:, P:2 * P]
        diag = onehot2[:].rearrange("p a b c d -> p (a b c d)").bitcast(F32)[:, 0:TB * P].rearrange(
            "p (b n) -> p b n", b=TB)

        def region(start, *shape):
            n = int(np.prod(shape))
            v = arena[:, start:start + n]
            if len(shape) == 1:
                return v
            names = "abcd"[:len(shape)]
            return v.rearrange("p (" + " ".join(names) + ") -> p " + " ".join(names),
                               **dict(zip(names[1:], shape[1:])))

        xh = region(0, TB, D)
        xn = region(4096, TB, D)
        qkv = region(8192, 24, SEQ)
        rqk = region(14336, 8, SEQ)
        rows = region(16384, ROW_GROUPS, TB, 512)
        conv_in = region(0, 2, SEQ)
        conv_y = region(22528, 2, SEQ)
        squares = region(22528, 512)
        roots = region(23552, 512)
        ab_w = region(23040, DC, 64)
        conv_w = region(24064, CONV_CHUNKS * CONV_W)
        pos_i = region(24160, SEQ).bitcast(I32)
        mixc = region(24448, C_MIX)
        mixed = region(28672, TB, D)

        weights_landed = [sem(f"weights_landed{i}") for i in range(RAW)]
        hi_ready, lo_ready = sem("hi_ready"), sem("lo_ready")
        hi_used, lo_used = sem("hi_used"), sem("lo_used")
        held = {e: sem(f"held_{e}") for e in ("act", "dve", "pool")}
        x_landed, keep_landed, conv_landed, consts_landed = ([sem(f"x_landed{b}") for b in range(TB)], sem("keep_landed"),
                                                             sem("conv_landed"), sem("consts_landed"))
        ones_ready = sem("ones_ready")

        def hold(eng, name, s, value):
            eng.wait_ge(s, value)
            eng.sem_inc(held[name], 1)

        def load_tile(sp, n, slot, src, first=False):
            if not first:
                sp.wait_ge(lo_ready, n - RAW + 1)
            sp.dma_start(raw[:, slot, :], src).then_inc(weights_landed[slot], 16)

        def round_tile(act, n, slot, use, turn, first=False):
            act.wait_ge(weights_landed[slot], 16 * turn + 16)
            if not first:
                act.wait_ge(hi_used, n - SPLIT + 1)
                act.wait_ge(lo_ready, n - SPLIT + 1)
            act.activation(hi[:, use, :], raw[:, slot, :], ACT.Copy).then_inc(hi_ready, 1)

        def rest_tile(dve, n, slot, use, first=False):
            dve.wait_ge(hi_ready, n + 1)
            if not first:
                dve.wait_ge(lo_used, n - SPLIT + 1)
            dve.tensor_tensor(lo[:, use, :], raw[:, slot, :], hi[:, use, :].bitcast(F32),
                              ALU.subtract).then_inc(lo_ready, 1)

        def tile_at(base, i, per, k):
            assert base % RAW == 0 and per % RAW == 0
            return (base + k + per * i, (base + k) % RAW, (base + k) % SPLIT,
                    (base + k) // RAW + (per // RAW) * i)

        def column_tile(pe, n, use, k, out_ap, turn=None):
            pe.wait_ge(hi_ready, n + 1)
            for d8 in range(8):
                w, d = hi[:, use, d8 * P:(d8 + 1) * P], 8 * k + d8
                if turn is not None:
                    wait_turned(pe, turn, d, 1)
                pe.matmul(out_ap, w, act_hi[:, d, :], start=(d == 0), stop=False)
                mm = pe.matmul(out_ap, w, act_lo[:, d, :], start=False, stop=False)
            mm.then_inc(hi_used, 1)
            pe.wait_ge(lo_ready, n + 1)
            for d8 in range(8):
                mm = pe.matmul(out_ap, lo[:, use, d8 * P:(d8 + 1) * P], act_hi[:, 8 * k + d8, :],
                               start=False, stop=(k == 1 and d8 == 7))
            mm.then_inc(lo_used, 1)

        def row_tile(pe, n, use, k, outs, last=7, turn=None):
            pe.wait_ge(hi_ready, n + 1)
            for tb in range(TB):
                for k2 in range(2):
                    if turn is not None and tb == 0:
                        wait_turned(pe, turn, 2 * k + k2, 4)
                    w, d, t = hi[:, use, k2 * 512:(k2 + 1) * 512], 2 * k + k2, slice(tb * P, tb * P + P)
                    pe.matmul(outs[tb], act_hi[:, d, t], w, start=(d == 0), stop=False)
                    mm = pe.matmul(outs[tb], act_lo[:, d, t], w, start=False, stop=False)
            mm.then_inc(hi_used, 1)
            pe.wait_ge(lo_ready, n + 1)
            for tb in range(TB):
                for k2 in range(2):
                    mm = pe.matmul(outs[tb], act_hi[:, 2 * k + k2, tb * P:tb * P + P],
                                   lo[:, use, k2 * 512:(k2 + 1) * 512], start=False,
                                   stop=(k == last and k2 == 1))
            mm.then_inc(lo_used, 1)

        mixer_done = sem("mixer_done")

        def meet(eng):
            eng.drain().then_inc(mixer_done, 1)
            eng.wait_ge(mixer_done, 4)

        squares_summed, mean_ready, root_ready = sem("squares_summed"), sem("mean_ready"), sem("root_ready")
        diag_ready, turned, act_hi_ready, act_lo_ready = (sem("diag_ready"), sem("turned"), sem("act_hi_ready"),
                                                          sem("act_lo_ready"))

        def square(act, h, tb, part, parts):
            n = D // parts
            c = slice(part * n, (part + 1) * n)
            act.activation(squares_out[:, tb, c], h[:, tb, c], ACT.Square,
                           accum_out=stat[:, tb * parts + part:tb * parts + part + 1]).then_inc(squares_summed, 1)

        def warm_root(act):
            act.activation(warm[:], one[:, 1:2], ACT.Sqrt)

        def act_root(act, n):
            act.wait_ge(mean_ready, n + 1)
            act.activation(stat[:, 12:14], stat[:, 10:12], ACT.Sqrt).then_inc(root_ready, 1)

        def dve_scale(dve, n, parts, summed):
            dve.wait_ge(squares_summed, summed)
            sums = stat[:, 0:2]
            if parts > 1:
                sums = stat[:, 8:10]
                dve.tensor_reduce(sums, stat[:, 0:2 * parts].rearrange("p (b c) -> p b c", b=2), AX_X, ALU.add)
                dve.drain()
            dve.tensor_scalar(stat[:, 10:12], sums, 1.0 / D, EPS, ALU.mult, ALU.add).then_inc(mean_ready, 1)
            dve.wait_ge(root_ready, n + 1)
            dve.reciprocal(stat[:, 14:16], stat[:, 12:14])
            dve.drain()

        def dve_norm(dve, n, parts, summed):
            dve_scale(dve, n, parts, summed)
            for tb in range(TB):
                e = dve.tensor_scalar(diag[:, tb], ident, stat[:, 14 + tb:15 + tb], None, ALU.mult)
            e.then_inc(diag_ready, 1)

        def pe_turn(pe, rows_ap, scaled=True):
            for b in range(8):
                for k in range(4):
                    d, tb = 2 * b + k // 2, k % 2
                    o, r = ps[:, b, k * P:(k + 1) * P], rows_ap[:, tb, d * P:(d + 1) * P]
                    if scaled:
                        mm = pe.matmul(o, r, diag[:, tb], start=True, stop=True)
                    else:
                        mm = pe.transpose(o, r, ident)
                mm.then_inc(turned, 1)

        def act_turn(act, turn, w):
            for d in range(DC):
                act.wait_ge(turned, 8 * turn + d // 2 + 1)
                src = ps[:, d // 2, (d % 2) * SEQ:(d % 2 + 1) * SEQ]
                act.activation(act_hi[:, d, :], src, ACT.Copy,
                               scale=1.0 if w is None else ncol[:, w, d:d + 1]).then_inc(act_hi_ready, 1)

        def dve_turn(dve, turn, w):
            for d in range(DC):
                dve.wait_ge(act_hi_ready, DC * turn + 2 * (d // 2) + 2)
                src = ps[:, d // 2, (d % 2) * SEQ:(d % 2 + 1) * SEQ]
                dve.scalar_tensor_tensor(act_lo[:, d, :], src, 1.0 if w is None else ncol[:, w, d:d + 1],
                                         act_hi[:, d, :].bitcast(F32), ALU.mult, ALU.subtract).then_inc(act_lo_ready, 1)

        def wait_turned(pe, turn, d, banks):
            pe.wait_ge(act_lo_ready, DC * turn + max(d + 1, 2 * banks))

        squares_out = region(8192, TB, D)


        taken, ab_copied, selector_ready = sem("taken"), sem("ab_copied"), sem("selector_ready")
        ab_hi_ready, ab_lo_ready, ab_used = sem("ab_hi_ready"), sem("ab_lo_ready"), sem("ab_used")
        convolved, silu_done = sem("convolved"), sem("silu_done")
        angles_ready, rows_silu = sem("angles_ready"), sem("rows_silu")
        trig_ready, q_rotated, k_rotated = sem("trig_ready"), sem("q_rotated"), sem("k_rotated")
        ret_scores, ret_masked, ret_out = sem("ret_scores"), sem("ret_masked"), sem("ret_out")
        ret_copied, ret_centered, ret_squared = sem("ret_copied"), sem("ret_centered"), sem("ret_squared")
        ret_var, ret_root, ret_scaled = sem("ret_var"), sem("ret_root"), sem("ret_scaled")
        ret_done = sem("ret_done")
        qk_squared, qk_summed, qk_root, qk_normed = (sem("qk_squared"), sem("qk_summed"), sem("qk_root"),
                                                     sem("qk_normed"))
        gate_in, gate_exp, gate_ln_in, gate_ln = sem("gate_in"), sem("gate_exp"), sem("gate_ln_in"), sem("gate_ln")
        decay_row, decay_col, decay_cols_ready = sem("decay_row"), sem("decay_col"), sem("decay_cols_ready")
        decay_exp = sem("decay_exp")
        decay_spread, expo_ready, decays_ready = sem("decay_spread"), sem("expo_ready"), sem("decays_ready")
        kv_turned, k_rows, v_rows = sem("kv_turned"), sem("k_rows"), sem("v_rows")
        kk_done, att_done, att_used = sem("kk_done"), sem("att_done"), sem("att_used")
        blocks_ready, blocks_turned = sem("blocks_ready"), sem("blocks_turned")
        inner_done, inner_copied, outer_done, inv_updated = (sem("inner_done"), sem("inner_copied"),
                                                             sem("outer_done"), sem("inv_updated"))
        rhs_ready, new_done, new_copied = sem("rhs_ready"), sem("new_done"), sem("new_copied")
        kd_ready, state_done, state_copied = sem("kd_ready"), sem("state_done"), sem("state_copied")
        from_state, q_state, q_state_copied = sem("from_state"), sem("q_state"), sem("q_state_copied")
        o_done, o_copied, o_mean, o_root = sem("o_done"), sem("o_copied"), sem("o_mean"), sem("o_root")
        z_weighted = sem("z_weighted")
        x_again, h_ready, h_spilled = sem("x_again"), sem("h_ready"), sem("h_spilled")

        att_ret = region(0, RET_HEADS, 3 * P)
        sin_t, cos_t = region(3072, SEQ), region(3328, SEQ)
        angle, turns = region(3584, SEQ), region(3840, SEQ)
        rot = region(4096, 4, 2, SEQ)
        rot_tmp = region(6144, 4, 2, SEQ)
        ret_sq = region(25600, TB, 1024)
        a_mat = region(0, 4, 4, P)
        inv = region(2048, 4, 4, P)
        inv_t = region(18432, 4, 4, P)
        blocks = region(6144, 4, 4, P)
        expo_a = region(6144, 4, 4, P)
        expo_d = region(14336, 4, 4, P)
        att = expo_d
        inner = region(25600, 4, 4, P)
        k_row = region(4096, 4, 4, P)
        v_row = [region(27648, 2, 4, P), region(13312, 2, 4, P)]
        rhs = region(6144, 4, 4, P)
        v_new = region(20480, 4, 4, P)
        state = region(0, 2, 4, P)
        k_dec = region(1024, 2, 4, P)
        q_out = region(2048, 2, 4, P)
        o_sq = region(25600, 4, 4, P)
        selector = region(1024, DN_HEADS, P)[0:8]
        gb = sel1_t
        tmp8 = sel2_t
        gcol = gate_t[:, 0:80].rearrange("p (b c) -> p b c", b=2)
        neg_g = gate_t[:, 80:96].rearrange("p (b c) -> p b c", b=2)
        exp_g = gate_t[:, 96:112].rearrange("p (b c) -> p b c", b=2)
        neg_beta_exp = gate_t[:, 112:120]
        end_dec = gate_t[:, 120:128]
        o_stat = gate_t[:, 128:176].rearrange("p (s g) -> p s g", s=3)
        ret_stat = gate_t[:, 176:176 + 64].rearrange("p (s b h) -> p s b h", s=4, b=2)
        g_end = gate_t[:, 240:248]

        query_t = region(12288, PQ_CHUNKS, SEQ)
        keys_t = region(26624 - 2048, PQ_CHUNKS, P)
        scores = region(28672, 16, 2, P)
        scores4 = region(28672, 8, 512)
        key_in, key_work = region(20480, 2, P), region(20736, 2, P)
        cand, cand_work = region(20992, TOPK, TOPK), region(21248, TOPK * TOPK)
        picked = region(21504, 2, TOPK, TOPK)
        key_top, key_index = region(22016, 2, TOPK), region(22048, 2, TOPK).bitcast(U32)
        key_index_f = region(22080, 2, TOPK)
        best, best_index = region(22112, TOPK), region(22128, TOPK).bitcast(U32)
        best_index_f, ranks_f = region(22144, TOPK), region(22176, 2, TOPK)
        best_all = region(22528, 16, TOPK)
        picks_all = region(22784, 2, 16, TOPK)
        gates3, gates_all = region(23296, 16, TOPK), region(23296, 16 * TOPK)
        gate_sum = region(23552, 16)
        experts = region(0, CHUNKS, SEQ)
        equal2 = equal2_t[:].rearrange("p (t c) -> p t c", t=4)
        ple = region(12288, TB, D)
        p_rows = region(4096, 2, SEQ)
        gate_sig = region(17408, 2, TB, 512)
        final_w = region(20480, D)
        final = region(24576, TB, D)
        keys_landed, scores_done, scores_ready = sem("keys_landed"), sem("scores_done"), sem("scores_ready")
        expert_bank, gates_in, gates_exp, gates_ready = (sem("expert_bank"), sem("gates_in"), sem("gates_exp"),
                                                         sem("gates_ready"))
        sel_turned, sel_ready = sem("sel_turned"), sem("sel_ready")
        onehot1_ready, onehot1_late, onehot2_ready = sem("onehot1_ready"), sem("onehot1_late"), sem("onehot2_ready")
        gates_summed, gates_applied = sem("gates_summed"), sem("gates_applied")
        stage_hi_ready, stage_lo_ready = sem("stage_hi_ready"), sem("stage_lo_ready")
        h_back, p_landed, final_landed = sem("h_back"), sem("p_landed"), sem("final_landed")
        sigmoid_ready, out_ready, out_stored = (sem("sigmoid_ready"), [sem(f"out_ready{b}") for b in range(TB)],
                                                sem("out_stored"))
        p_hi_ready, p_lo_ready, weighted, scale_ready = (sem("p_hi_ready"), sem("p_lo_ready"), sem("weighted"),
                                                         sem("scale_ready"))

        psg = ps[:].rearrange("p b (j n) -> p b j n", j=4)
        ps2 = ps[:].rearrange("p (b c) n -> p b (c n)", c=2)
        spread = ps[:, 4:8, :].rearrange("p b (c t) -> p (b c) t", c=2)
        qkv2 = region(8192, 8, 512)
        neg_a = mixc[:, C_NEGA:C_NEGA + P].unsqueeze(1)
        neg_d = mixc[:, C_NEGD:C_NEGD + P].unsqueeze(1)
        level_mask = mixc[:, 0:LEVELS * P].rearrange("p (l n) -> p l n", l=LEVELS)
        ret_decay = mixc[:, C_RETD:].rearrange("p (h n) -> p h n", h=RET_HEADS)
        one_c, eps_c = one[:, 0:1], one[:, 1:2]
        trig_k, trig_p = region(6144, SEQ), region(6400, SEQ)

        def channel(what, g, j):
            b = g // 2
            return qkv[:, 8 * what + 4 * (g % 2) + j, b * P:(b + 1) * P]

        def o_rows(g):
            return mixed[:, g // 2, (g % 2) * 512:(g % 2 + 1) * 512].rearrange("p (j n) -> p j n", j=4)

        def rotate(eng, at, x):
            x1, x2 = rqk[:, 2 * at:2 * at + 2], rqk[:, 2 * at + 2:2 * at + 4]
            sin_b, cos_b = (t.unsqueeze(1).broadcast_to([P, 2, SEQ]) for t in (sin_t, cos_t))
            t1, t2 = rot_tmp[:, at], rot_tmp[:, at + 1]
            eng.drain()
            eng.tensor_tensor(t1, x1, sin_b if x else cos_b, ALU.mult)
            eng.tensor_tensor(t2, x2, cos_b if x else sin_b, ALU.mult)
            eng.drain()
            return eng.tensor_tensor(rot[:, at + x], t1, t2, ALU.add if x else ALU.subtract)

        def ab_part(stage):
            return stage[:].rearrange("p a b -> p (a b)").rearrange("p (d n) -> p d n", d=8)

        def take_ple(dve, g):
            dve.wait_ge(lo_used, T_PLE + g + 1)
            dve.tensor_copy(ple[:, :, 512 * g:512 * (g + 1)],
                            ps[:, 2 - 2 * (g % 2):4 - 2 * (g % 2), :]).then_inc(taken, 1)

        def start_of_stream(base, i, c):
            return base == 0 and isinstance(i, int) and i == 0 and c == 0

        block = ctx.enter_context(nc.Block())

        @block.sync
        def _(sp):
            for tb in range(TB):
                sp.dma_start(xh[:, tb], x[tb * P:(tb + 1) * P, :]).then_inc(x_landed[tb], 16)
            sp.dma_start(keep[:], keep_c).then_inc(keep_landed, 16)
            sp.dma_start(ncol[:], norm_cols).then_inc(keep_landed, 16)
            for k in range(RAW):
                load_tile(sp, k, k, w_in_cols[k], first=True)
            sp.dma_start(conv_w, conv_cols).then_inc(conv_landed, 16)

            def stream(base, source, start, stop):
                with sp.Fori(start, stop) as i:
                    for k in range(RAW):
                        n, slot, _, _ = tile_at(base, i, RAW, k)
                        load_tile(sp, n, slot, source[ds(i * RAW + k, 1)].rearrange("a p f -> (a p) f"))

            stream(0, w_in_cols, 1, T_ROW // RAW)
            stream(T_ROW, w_in_rows, 0, (T_OUT - T_ROW) // RAW)
            stream(T_OUT, w_out, 0, (T_PQ - T_OUT) // RAW)
            stream(T_PQ, w_pq, 0, (T_U - T_PQ) // RAW)
            stream(T_U, expert_u, 0, (T_V - T_U) // RAW)
            stream(T_V, expert_v, 0, (T_PLE - T_V) // RAW)
            stream(T_PLE, w_ple, 0, 1)
            stream(T_V + 4, expert_v, (T_PLE - T_V) // RAW, 2 * CHUNKS // RAW)
            stream(T_GATE, w_gate, 0, (T_END - T_GATE) // RAW)
            for tb in (1, 0):
                sp.wait_ge(out_ready[tb], 2)
                sp.dma_start(out[tb * P:(tb + 1) * P, :], final[:, tb]).then_inc(out_stored, 16)
            sp.wait_ge(out_stored, 16 * TB)

        @block.scalar
        def _(act):
            act.wait_ge(ones_ready, 1)
            warm_root(act)
            for tb in range(TB):
                act.wait_ge(x_landed[tb], 16)
                square(act, xh, tb, 0, 1)
            act_root(act, 0)
            for k in range(2):
                round_tile(act, *tile_at(0, 0, 4, k), first=True)
            act.wait_ge(keep_landed, 32)
            act_turn(act, 0, 0)

            def copy_chunk(c, parity):
                act.wait_ge(lo_used, 2 * c + 2)
                act.activation(conv_in[:, parity, :], ps[:, parity, 0:SEQ], ACT.Copy).then_inc(taken, 1)

            def silu_chunk(c, parity):
                hold(act, "act", convolved, c + 1)
                act.activation(qkv[:, ds(c, 1), :], conv_y[:, parity:parity + 1, :], ACT.Silu).then_inc(silu_done, 1)

            def copy_rqk(c, parity):
                hold(act, "act", lo_used, 2 * c + 2)
                act.activation(rqk[:, ds(c - CONV_CHUNKS, 1), :], ps[:, parity:parity + 1, 0:SEQ],
                               ACT.Copy).then_inc(taken, 1)

            def chunk_round(base, i, after, skip=0):
                for c in range(2):
                    for k in range(2)[skip * (1 - c):]:
                        round_tile(act, *tile_at(base, i, 4, 2 * c + k), first=start_of_stream(base, i, c))
                    after(i, c)

            def copy_and_silu(i, c):
                copy_chunk(2 * i + c - 1, 1 - c)
                silu_chunk(2 * i + c - 2, c)

            def silu_and_rqk(i, c):
                if c == 0:
                    copy_and_silu(i, c)
                else:
                    copy_rqk(CONV_CHUNKS, 0)
                    silu_chunk(CONV_CHUNKS - 1, 1)

            chunk_round(0, 0, lambda i, c: c and copy_chunk(0, 0), skip=2)
            with act.Fori(1, CONV_CHUNKS // 4) as i:
                chunk_round(0, i, copy_and_silu)
            act.dma_start(ab_w, w_ab).then_inc(consts_landed, 16)
            act.dma_start(mixc, mix_c).then_inc(consts_landed, 16)
            act.dma_start(ab_col[:, 0:2], ab_cols).then_inc(consts_landed, 16)
            act.dma_start(dn_w, dn_norm.partition_broadcast(P)).then_inc(consts_landed, 16)
            act.dma_start(mixed[:, 0, 0:1024], ret_gn_w.partition_broadcast(P)).then_inc(consts_landed, 16)
            act.dma_start(mixed[:, 1, 0:1024], ret_gn_b.partition_broadcast(P)).then_inc(consts_landed, 16)
            act.dma_start(pos_i, positions.partition_broadcast(P)).then_inc(consts_landed, 16)
            with act.Fori(CONV_CHUNKS // 4, CONV_CHUNKS // 2) as i:
                chunk_round(0, i, copy_and_silu)
            chunk_round(0, CONV_CHUNKS // 2, silu_and_rqk)
            act.wait_ge(consts_landed, ALL_CONSTS)
            act.activation(ab_part(stage_hi), ab_w[:, 0:8], ACT.Copy).then_inc(ab_hi_ready, 1)
            with act.Fori(CONV_CHUNKS // 2 + 1, AB_ROUND + 1) as i:
                chunk_round(0, i, lambda i, c: copy_rqk(2 * i + c - 1, 1 - c))
            act.wait_ge(ab_used, 1)
            act.activation(ab_part(stage_hi), ab_w[:, 8:16], ACT.Copy).then_inc(ab_hi_ready, 1)
            with act.Fori(AB_ROUND + 1, IN_CHUNKS // 2) as i:
                chunk_round(0, i, lambda i, c: copy_rqk(2 * i + c - 1, 1 - c))
            for k in range(4):
                round_tile(act, *tile_at(T_ROW, 0, 4, k))
                if k == 1:
                    copy_rqk(IN_CHUNKS - 1, 1)
            act.wait_ge(angles_ready, 2)
            act.activation(sin_t, angle, ACT.Sin).then_inc(trig_ready, 1)
            act.activation(cos_t, turns, ACT.Sin).then_inc(trig_ready, 1)
            for k in range(4):
                round_tile(act, *tile_at(T_ROW + 4, 0, 4, k))
            act.wait_ge(gate_in, 1)
            act.activation(tmp8[0:8, :], tmp8[0:8, :], ACT.Exp).then_inc(gate_exp, 1)
            act.activation(tmp8[32:40, :], tmp8[32:40, :], ACT.Exp, scale=-1.0).then_inc(gate_exp, 1)
            act.activation(ab_col[:, 2:3], ab_col[:, 0:1], ACT.Exp).then_inc(gate_exp, 1)
            for k in range(4):
                round_tile(act, *tile_at(T_ROW + 8, 0, 4, k))
            act.wait_ge(gate_ln_in, 1)
            act.activation(tmp8[0:8, :], tmp8[0:8, :], ACT.Ln).then_inc(gate_ln, 1)
            for k in range(4):
                round_tile(act, *tile_at(T_ROW + 12, 0, 4, k))
            with act.Fori(0, 8) as p:
                for k in range(4):
                    round_tile(act, *tile_at(T_ROW + 16, p, 4, k))
                    if k == 0:
                        act.activation(squares, qkv2[:, ds(p, 1), :].rearrange("p a n -> p (a n)"),
                                       ACT.Square).then_inc(qk_squared, 1)
                    if k == 2:
                        act.wait_ge(qk_summed, p + 1)
                        act.activation(roots, ps[:, 5, :], ACT.Sqrt, bias=eps_c).then_inc(qk_root, 1)

            act.wait_ge(decay_cols_ready, 1)
            act.activation(exp_g, gcol[:, :, 0:8], ACT.Exp).then_inc(decay_exp, 1)
            act.wait_ge(decay_cols_ready, 2)
            act.activation(end_dec, end_dec, ACT.Exp).then_inc(decay_exp, 1)
            for g in range(4):
                act.wait_ge(expo_ready, 2 * g + 2)
                for j in range(4):
                    h = 4 * (g % 2) + j
                    act.activation(expo_a[:, g, j], expo_a[:, g, j], ACT.Exp, bias=gcol[:, g // 2, h:h + 1])
                    e = act.activation(expo_d[:, g, j], expo_d[:, g, j], ACT.Exp, bias=neg_g[:, g // 2, h:h + 1])
                e.then_inc(decays_ready, 1)
            act.wait_ge(taken, IN_CHUNKS + ROW_GROUPS)
            act.activation(rows[:, 0:2], rows[:, 0:2], ACT.Silu).then_inc(rows_silu, 1)
            act.activation(rows[:, 4:6], rows[:, 4:6], ACT.Silu).then_inc(rows_silu, 1)

            def k_to_rows(b):
                for g in range(2):
                    act.wait_ge(kv_turned, 4 * b + 2 * g + 1)
                    act.activation(k_row[:, 2 * b + g], psg[:, 2 * g], ACT.Copy).then_inc(k_rows, 1)

            k_to_rows(0)
            for tb in range(TB):
                act.wait_ge(ret_out, tb + 1)
                act.activation(mixed[:, tb, 1024:2048], ps2[:, 2 + tb], ACT.Copy).then_inc(ret_copied, 1)
            k_to_rows(1)
            for tb in range(TB):
                act.wait_ge(ret_centered, tb + 1)
                act.activation(ret_sq[:, tb], mixed[:, tb, 1024:2048], ACT.Square).then_inc(ret_squared, 1)
            def copy_inner(level):
                for g in range(4):
                    act.wait_ge(inner_done, 4 * level + g - 3)
                    act.activation(inner[:, g], psg[:, g], ACT.Copy).then_inc(inner_copied, 1)

            act.wait_ge(ret_var, 1)
            copy_inner(1)
            act.wait_ge(ret_var, 1)
            act.activation(ret_stat[:, 2], ret_stat[:, 1], ACT.Sqrt).then_inc(ret_root, 1)
            with act.Fori(2, LEVELS) as level:
                copy_inner(level)
            act.wait_ge(inv_updated, 4 * LEVELS)
            for j in range(8):
                e = act.activation(k_dec[:, j // 4, j % 4], k_row[:, j // 4, j % 4], ACT.Copy, scale=end_dec[:, j:j + 1])
            e.then_inc(kd_ready, 1)
            for g in range(2):
                act.wait_ge(state_done, g + 1)
                act.activation(state[:, g], psg[:, 4 + g], ACT.Copy).then_inc(state_copied, 1)
            for g in range(2):
                act.wait_ge(q_state, g + 1)
                for j in range(4):
                    h = 4 * g + j
                    e = act.activation(q_out[:, g, j], psg[:, 2 + g, j], ACT.Copy, scale=exp_g[:, 1, h:h + 1])
                e.then_inc(q_state_copied, 1)
            for b in range(TB):
                act.wait_ge(o_mean, b + 1)
                heads = slice(8 * b, 8 * b + 8)
                act.activation(o_stat[:, 2, heads], o_stat[:, 1, heads], ACT.Sqrt).then_inc(o_root, 1)
            meet(act)
            act.dma_start(xn, x.rearrange("(b p) d -> p b d", p=P)).then_inc(x_again, 16)
            for k in range(2):
                round_tile(act, *tile_at(T_OUT, 0, 4, k))
            act_turn(act, 1, None)
            act.dma_start(keys_t, sub_keys_t).then_inc(keys_landed, 16)

            def group_rounds(base, after):
                for n in range(4 * 8):
                    if n >= 2:
                        round_tile(act, *tile_at(base + n // 4 * 4, 0, 4, n % 4))
                    for k, step in after.items():
                        if n % 8 == k and n > 8:
                            step(n // 8 - 1)

            def square_group(g, before):
                act.wait_ge(taken, before + g + 1)
                for tb in range(TB):
                    square(act, xh, tb, g, 4)

            group_rounds(T_OUT, {3: lambda g: square_group(g, TAKEN_OUT - 4)})
            for k in range(2):
                round_tile(act, *tile_at(T_PQ, 0, 4, k))
            warm_root(act)
            square_group(3, TAKEN_OUT - 4)
            act.wait_ge(h_ready, 1)
            act.dma_start(h_spill.rearrange("(b p) d -> p b d", p=P), xh).then_inc(h_spilled, 16)
            act_root(act, 1)
            act_turn(act, 2, 1)
            for k in range(2, 4):
                round_tile(act, *tile_at(T_PQ, 0, 4, k))
            with act.Fori(1, PQ_CHUNKS // 2) as i:
                for k in range(4):
                    round_tile(act, *tile_at(T_PQ, i, 4, k))
            for b in range(8):
                act.wait_ge(scores_done, b + 1)
                e = act.activation(scores4[:, b], ps[:, b, :], ACT.Copy).then_inc(scores_ready, 1)
            act.wait_ge(h_spilled, 16)
            act.wait_ge(scores_ready, 8)
            act.sem_inc(expert_bank, 2)

            def gelu_chunk(c, parity):
                hold(act, "act", lo_used, T_U + 2 * c + 2)
                act.activation(experts[:, ds(c, 1), :], ps[:, parity:parity + 1, 0:SEQ], ACT.Gelu).then_inc(expert_bank, 1)

            def expert_round(i, first=False):
                for c in range(2):
                    for k in range(2):
                        round_tile(act, *tile_at(T_U, i, 4, 2 * c + k))
                    if not (first and c == 0):
                        gelu_chunk(2 * i + c - 1, 1 - c)

            expert_round(0, first=True)
            with act.Fori(1, TOPK_CHUNKS // 2) as i:
                expert_round(i)
            act.wait_ge(gates_in, 1)
            act.activation(gates_all, gates_all, ACT.Exp).then_inc(gates_exp, 1)
            with act.Fori(TOPK_CHUNKS // 2, CHUNKS // 2) as i:
                expert_round(i)
            gelu_chunk(CHUNKS - 1, 1)

            def first_keys(q, slot):
                hold(act, "act", gates_summed, q + GROUPS + 1)
                for t in (2, 3):
                    act.activation(onehot1[:, slot, t], iota, ACT.Square, scale=-1.0, bias=sel1_t[:, ds(4 * q + t, 1)])
                act.drain()
                act.activation(onehot1[:, slot, 2:4], onehot1[:, slot, 2:4], ACT.Relu, scale=-1.0,
                               bias=one_c).then_inc(onehot1_late, 1)

            def value_round(half, i, late=0, keys=False, first=False):
                for c in range(4):
                    v = CHUNKS * half + 4 * i + c
                    hold(act, "act", lo_used, T_V + v + late - 1)
                    act.activation(stage_hi[:, c % 2:c % 2 + 1, :], experts[:, ds(4 * i + c, 1), :],
                                   ACT.Copy).then_inc(stage_hi_ready, 1)
                    round_tile(act, T_V + v + late, c % RAW, c % SPLIT, (T_V + late) // RAW + CHUNKS // RAW * half + i)
                    if keys and not (first and c == 0):
                        first_keys(4 * i + c - 1, (c - 1) % 2)

            act.wait_ge(gates_applied, GROUPS + 2)
            value_round(0, 0, keys=True, first=True)
            with act.Fori(1, CHUNKS // 8) as i:
                value_round(0, i, keys=True)
            first_keys(GROUPS - 1, 1)
            act.wait_ge(gates_applied, 2 * GROUPS + 2)
            with act.Fori(CHUNKS // 8, CHUNKS // 4) as i:
                value_round(0, i)
            with act.Fori(0, CHUNKS // 8) as i:
                value_round(1, i)
            act.wait_ge(stage_lo_ready, CHUNKS + CHUNKS // 2)
            act.dma_start(xh, h_spill.rearrange("(b p) d -> p b d", p=P)).then_inc(h_back, 16)
            act.dma_start(p_rows, p_t).then_inc(p_landed, 16)
            with act.Fori(CHUNKS // 8, PLE_CHUNK // 4) as i:
                value_round(1, i)
            act.wait_ge(p_landed, 16)
            act.activation(act_hi[:, 0:2, :], p_rows, ACT.Copy).then_inc(p_hi_ready, 1)
            for k in range(4):
                round_tile(act, *tile_at(T_PLE, 0, 4, k))
            act.wait_ge(taken, TAKEN_H0)
            for tb in range(TB):
                square(act, xh, tb, 0, 2)
            with act.Fori(PLE_CHUNK // 4, CHUNKS // 4) as i:
                value_round(1, i, late=4)
            warm_root(act)
            act.wait_ge(stage_lo_ready, 2 * CHUNKS)
            act.dma_start(final_w, norm_final.partition_broadcast(P)).then_inc(final_landed, 16)
            for k in range(2):
                round_tile(act, *tile_at(T_GATE, 0, 4, k))
            for tb in range(TB):
                act.wait_ge(taken, TAKEN_H - TB + tb + 1)
                square(act, xh, tb, 1, 2)
            act_root(act, 2)
            act_turn(act, 3, 2)

            def sigmoid_group(g, parity):
                act.wait_ge(lo_used, T_GATE + 8 * g + 8)
                act.wait_ge(taken, TAKEN_H + g - 1)
                act.activation(gate_sig[:, parity], ps[:, 2 - 2 * parity:4 - 2 * parity, :],
                               ACT.Sigmoid).then_inc(sigmoid_ready, 1)

            group_rounds(T_GATE, {1: lambda g: sigmoid_group(g, g % 2), 6: lambda g: square_group(g, TAKEN_H)})
            sigmoid_group(3, 1)
            warm_root(act)
            square_group(3, TAKEN_H)
            act_root(act, 3)
            act.wait_ge(weighted, 3)
            act.wait_ge(scale_ready, 1)
            act.activation(final[:, 0, 0:1536], final[:, 0, 0:1536], ACT.Copy, scale=stat[:, 14:15]).then_inc(out_ready[0], 1)

        @block.vector
        def _(dve):
            dve.memset(ones_m, 1.0)
            dve.memset(one_c, 1.0)
            dve.memset(eps_c, EPS).then_inc(ones_ready, 1)
            dve.wait_ge(keep_landed, 32)
            dve_norm(dve, 0, 1, TB)
            for k in range(2):
                rest_tile(dve, *tile_at(0, 0, 4, k)[:3], first=True)
            dve_turn(dve, 0, 0)
            dve.wait_ge(conv_landed, 16)

            def convolve(c, parity):
                if not (isinstance(c, int) and c < 2):
                    dve.wait_ge(silu_done, c - 1)
                dve.wait_ge(taken, c + 1)
                y, src = conv_y[:, parity, :], conv_in[:, parity, :]
                dve.tensor_scalar(y, src, conv_w[:, ds(4 * c + 3, 1)], None, ALU.mult)
                for s in range(1, CONV_W):
                    dve.drain()
                    e = dve.scalar_tensor_tensor(y[:, s:], src[:, 0:SEQ - s], conv_w[:, ds(4 * c + 3 - s, 1)],
                                                 y[:, s:], ALU.mult, ALU.add)
                e.then_inc(convolved, 1)

            def chunk_round(base, i, after, skip=0):
                for c in range(2):
                    for k in range(2)[skip * (1 - c):]:
                        rest_tile(dve, *tile_at(base, i, 4, 2 * c + k)[:3], first=start_of_stream(base, i, c))
                    after(i, c)

            chunk_round(0, 0, lambda i, c: c and convolve(0, 0), skip=2)
            chunk_round(0, 1, lambda i, c: convolve(2 * i + c - 1, 1 - c))
            with dve.Fori(2, CONV_CHUNKS // 2) as i:
                chunk_round(0, i, lambda i, c: convolve(2 * i + c - 1, 1 - c))
            chunk_round(0, CONV_CHUNKS // 2, lambda i, c: None if c else convolve(CONV_CHUNKS - 1, 1))
            def ab_rest(half):
                dve.wait_ge(ab_hi_ready, half + 1)
                dve.tensor_tensor(ab_part(stage_lo), ab_w[:, 8 * half:8 * half + 8], ab_part(stage_hi).bitcast(F32),
                                  ALU.subtract).then_inc(ab_lo_ready, 1)

            ab_rest(0)
            with dve.Fori(CONV_CHUNKS // 2 + 1, AB_ROUND + 1) as i:
                chunk_round(0, i, lambda i, c: None)
            ab_rest(1)
            with dve.Fori(AB_ROUND + 1, IN_CHUNKS // 2) as i:
                chunk_round(0, i, lambda i, c: None)

            def take_rows(g, parity):
                dve.wait_ge(lo_used, T_ROW + 8 * g + 8)
                dve.tensor_scalar(rows[:, ds(g, 1)].rearrange("p a b c -> p (a b) c"),
                                  ps[:, 2 - 2 * parity:4 - 2 * parity, :], 1.0, None, ALU.mult).then_inc(taken, 1)

            def group_round(base, i, take, first=False, skip=0, between={}):
                for g in range(2):
                    for k in range(8):
                        if 8 * g + k >= skip:
                            rest_tile(dve, *tile_at(base, i, 16, 8 * g + k)[:3])
                        if take and k == 1 and not (first and g == 0):
                            take(2 * i + g - 1, 1 - g)
                        if 8 * g + k in between:
                            between[8 * g + k]()

            x8, m8 = tmp8[0:8, :], gb[0:8, :]

            def gates_first():
                dve.tensor_copy(selector, ident[0:8, 0:8].unsqueeze(2).broadcast_to([8, 8, P])).then_inc(selector_ready, 1)
                dve.tensor_copy(tmp8[0:64, :], ps[0:64, 4, 0:SEQ]).then_inc(ab_copied, 1)
                dve.memset(gb[0:64, :], 0.0)
                dve.drain()
                dve.tensor_scalar(x8, x8, ab_col[:, 1:2], None, ALU.add)
                dve.drain()
                dve.tensor_scalar(m8, x8, 0.0, None, ALU.max)
                dve.drain()
                dve.scalar_tensor_tensor(x8, m8, -2.0, x8, ALU.mult, ALU.add).then_inc(gate_in, 1)

            def gates_second():
                dve.wait_ge(gate_exp, 3)
                dve.tensor_scalar(x8, x8, 1.0, None, ALU.add).then_inc(gate_ln_in, 1)
                dve.tensor_scalar(tmp8[32:40, :], tmp8[32:40, :], 1.0, None, ALU.add)
                dve.tensor_scalar(ab_col[:, 3:4], ab_col[:, 2:3], -1.0, None, ALU.mult)
                dve.drain()
                dve.reciprocal(gb[32:40, :], tmp8[32:40, :])

            def gates_third():
                dve.wait_ge(gate_ln, 1)
                dve.tensor_tensor(x8, x8, m8, ALU.add)
                dve.drain()
                dve.tensor_scalar(x8, x8, ab_col[:, 3:4], None, ALU.mult)
                dve.drain()
                for b in range(TB):
                    e = dve.tensor_tensor_scan(gb[0:8, b * P:(b + 1) * P], ones_m[0:8, :], x8[:, b * P:(b + 1) * P], 0.0,
                                               ALU.mult, ALU.add)
                e.then_inc(decay_row, 1)

            def rotate_q(x):
                dve.wait_ge(taken, IN_CHUNKS)
                dve.wait_ge(trig_ready, 2)
                rotate(dve, 0, x).then_inc(q_rotated, 1)

            def invert_roots(p):
                dve.wait_ge(qk_root, p + 1)
                dve.reciprocal(roots[:, 0:SEQ], roots[:, 0:SEQ])

            def normalise(p):
                dve.reciprocal(roots[:, SEQ:], roots[:, SEQ:])
                dve.drain()
                dve.scalar_tensor_tensor(qkv2[:, p], qkv2[:, p], DK ** -0.5 if p < 4 else 1.0, roots,
                                         ALU.mult, ALU.mult).then_inc(qk_normed, 1)

            group_round(T_ROW, 0, take_rows, first=True, between={
                3: gates_first, 9: gates_second, 13: gates_third,
                11: lambda: rotate_q(0), 15: lambda: rotate_q(1)})
            for i in (1, 2):
                halves = {4 * u + 2: lambda p=4 * i - 4 + u: invert_roots(p) for u in range(4)}
                halves |= {4 * u + 3: lambda p=4 * i - 4 + u: normalise(p) for u in range(4)}
                group_round(T_ROW, i, take_rows, between=halves)
            take_rows(ROW_GROUPS - 1, 1)
            dve.wait_ge(decay_col, 1)
            dve.tensor_copy(gcol, ps[:, 3, 0:80].rearrange("p (b c) -> p b c", b=2)).then_inc(decay_cols_ready, 1)
            dve.drain()
            dve.tensor_scalar(neg_g, gcol[:, :, 0:8], -1.0, None, ALU.mult)
            dve.wait_ge(decay_spread, 1)
            dve.tensor_copy(g_end, spread[:, :, P - 1])
            dve.drain()
            dve.tensor_tensor(end_dec, g_end, gcol[:, 0, 0:8], ALU.subtract).then_inc(decay_cols_ready, 1)
            dve.wait_ge(k_rotated, 2)
            for g in range(4):
                src = spread[:, 4 * (g % 2):4 * (g % 2) + 4, (g // 2) * P:(g // 2 + 1) * P]
                dve.scalar_tensor_tensor(expo_a[:, g], src, -1.0, neg_a.broadcast_to([P, 4, P]), ALU.mult,
                                         ALU.add).then_inc(expo_ready, 1)
                dve.tensor_tensor(expo_d[:, g], src, neg_d.broadcast_to([P, 4, P]), ALU.add).then_inc(expo_ready, 1)
            for h in range(RET_HEADS):
                dve.wait_ge(ret_scores, h + 1)
                dve.tensor_tensor(att_ret[:, h], ps[:, h, 0:3 * P], ret_decay[:, h], ALU.mult).then_inc(ret_masked, 1)
            def v_to_rows(b):
                dve.drain()
                for g in range(2):
                    dve.wait_ge(kv_turned, 4 * b + 2 * g + 2)
                    beta = gcol[:, b, 32 + 4 * g:36 + 4 * g].unsqueeze(2).broadcast_to([P, 4, P])
                    dve.tensor_tensor(v_row[b][:, g], psg[:, 2 * g + 1], beta, ALU.mult).then_inc(v_rows, 1)

            v_to_rows(0)
            dve.wait_ge(decay_exp, 1)
            dve.scalar_tensor_tensor(neg_beta_exp, exp_g[:, 1], -1.0, gcol[:, 1, 32:40], ALU.mult, ALU.mult)
            r4 = [mixed[:, tb, 1024:2048].rearrange("p (h d) -> p h d", h=RET_HEADS) for tb in range(TB)]
            s4 = [ret_sq[:, tb].rearrange("p (h d) -> p h d", h=RET_HEADS) for tb in range(TB)]

            def over_head(s, tb):
                return ret_stat[:, s, tb].unsqueeze(2).broadcast_to([P, RET_HEADS, RET_DV])

            for tb in range(TB):
                dve.wait_ge(ret_copied, tb + 1)
                dve.tensor_reduce(ret_stat[:, 0, tb], r4[tb], AX_X, ALU.add)
                dve.drain()
                dve.tensor_scalar(ret_stat[:, 0, tb], ret_stat[:, 0, tb], 1.0 / RET_DV, None, ALU.mult)
                dve.drain()
                dve.tensor_tensor(r4[tb], r4[tb], over_head(0, tb), ALU.subtract).then_inc(ret_centered, 1)
            dve.wait_ge(kv_turned, 8)
            v_to_rows(1)
            for tb in range(TB):
                dve.wait_ge(ret_squared, tb + 1)
                dve.tensor_reduce(ret_stat[:, 1, tb], s4[tb], AX_X, ALU.add)
            dve.drain()
            dve.tensor_scalar(ret_stat[:, 1], ret_stat[:, 1], 1.0 / RET_DV, EPS, ALU.mult, ALU.add).then_inc(ret_var, 1)
            dve.wait_ge(decays_ready, 4)

            def mask_blocks(level, g):
                mask = level_mask[:, level:level + 1] if isinstance(level, int) else level_mask[:, ds(level, 1)]
                dve.tensor_tensor(blocks[:, g], a_mat[:, g], mask.broadcast_to([P, 4, P]), ALU.mult).then_inc(blocks_ready, 1)

            for g in range(4):
                dve.wait_ge(kk_done, g + 1)
                for j in range(4):
                    h = 4 * (g % 2) + j
                    e = dve.scalar_tensor_tensor(a_mat[:, g, j], psg[:, g, j], gcol[:, g // 2, 32 + h:33 + h],
                                                 expo_a[:, g, j], ALU.mult, ALU.mult)
                dve.drain()
                mask_blocks(0, g)
            for g in range(4):
                dve.wait_ge(att_done, g + 1)
                dve.tensor_tensor(att[:, g], psg[:, 4 + g], expo_d[:, g], ALU.mult).then_inc(att_used, 1)
            eye = ident.unsqueeze(1).broadcast_to([P, 4, P])
            for g in range(4):
                dve.tensor_tensor(inv[:, g], eye, blocks[:, g], ALU.subtract)
                dve.wait_ge(blocks_turned, g + 1)
                dve.tensor_tensor(inv_t[:, g], eye, psg[:, g], ALU.subtract).then_inc(inv_updated, 1)
                dve.drain()
                mask_blocks(1, g)
            def ret_scale(tb):
                if tb == 0:
                    dve.wait_ge(ret_root, 1)
                    dve.reciprocal(ret_stat[:, 3], ret_stat[:, 2])
                    dve.drain()
                dve.tensor_tensor(r4[tb], r4[tb], over_head(3, tb), ALU.mult).then_inc(ret_scaled, 1)

            def update_inverse(level, last=False, between={}):
                for g in range(4):
                    dve.wait_ge(outer_done, 4 * level + g - 3)
                    dve.tensor_tensor(inv[:, g], inv[:, g], psg[:, 4 + 2 * (g % 2)], ALU.subtract)
                    dve.tensor_tensor(inv_t[:, g], inv_t[:, g], psg[:, 5 + 2 * (g % 2)],
                                      ALU.subtract).then_inc(inv_updated, 1)
                    if not last:
                        mask_blocks(level + 1, g)
                    if g in between:
                        between[g]()

            update_inverse(1)
            update_inverse(2, between={1: lambda: ret_scale(0), 3: lambda: ret_scale(1)})
            with dve.Fori(3, LEVELS - 1) as level:
                update_inverse(level)
            update_inverse(LEVELS - 1, last=True)
            dve.wait_ge(ret_done, 2)
            for g in range(2):
                dve.wait_ge(new_done, g + 1)
                dve.tensor_copy(v_new[:, g], psg[:, g]).then_inc(new_copied, 1)
            for g in range(2):
                dve.wait_ge(o_done, g + 1)
                dve.tensor_copy(o_rows(g), psg[:, 6 + g]).then_inc(o_copied, 1)
            for g in range(2):
                dve.wait_ge(from_state, g + 1)
                for j in range(4):
                    h = 4 * g + j
                    e = dve.scalar_tensor_tensor(rhs[:, 2 + g, j], psg[:, g, j], neg_beta_exp[:, h:h + 1],
                                                 v_row[1][:, g, j], ALU.mult, ALU.add)
                e.then_inc(rhs_ready, 1)
            def o_mean_square(b):
                heads = slice(8 * b, 8 * b + 8)
                for g in range(2 * b, 2 * b + 2):
                    dve.tensor_tensor(o_sq[:, g], o_rows(g), o_rows(g), ALU.mult)
                dve.drain()
                dve.tensor_reduce(o_stat[:, 0, heads], o_sq[:, 2 * b:2 * b + 2].rearrange("p g j n -> p (g j) n"), AX_X,
                                  ALU.add)
                dve.drain()
                dve.tensor_scalar(o_stat[:, 1, heads], o_stat[:, 0, heads], 1.0 / DK, EPS, ALU.mult,
                                  ALU.add).then_inc(o_mean, 1)

            def o_scale(b):
                heads = slice(8 * b, 8 * b + 8)
                dve.wait_ge(o_root, b + 1)
                dve.reciprocal(o_stat[:, 0, heads], o_stat[:, 2, heads])
                dve.wait_ge(z_weighted, 1)
                dve.drain()
                for g in range(2 * b, 2 * b + 2):
                    for j in range(4):
                        dve.scalar_tensor_tensor(o_rows(g)[:, j], o_rows(g)[:, j],
                                                 o_stat[:, 0, 4 * g + j:4 * g + j + 1],
                                                 rows[:, g % 2, g // 2, j * P:(j + 1) * P], ALU.mult, ALU.mult)

            dve.drain()
            o_mean_square(0)
            for g in range(2):
                dve.wait_ge(new_done, g + 3)
                dve.tensor_copy(v_new[:, 2 + g], psg[:, 4 + g]).then_inc(new_copied, 1)
            o_scale(0)
            for g in range(2):
                dve.wait_ge(q_state_copied, g + 1)
                dve.wait_ge(o_done, g + 3)
                dve.tensor_tensor(o_rows(2 + g), psg[:, g], q_out[:, g], ALU.add)
            dve.drain()
            dve.drain()
            o_mean_square(1)
            o_scale(1)
            meet(dve)
            for k in range(2):
                rest_tile(dve, *tile_at(T_OUT, 0, 4, k)[:3])
            dve_turn(dve, 1, None)

            def take_out(g, parity):
                dve.wait_ge(lo_used, T_OUT + 8 * g + 8)
                dve.tensor_tensor(xh[:, :, ds(512 * g, 512)], ps[:, 2 - 2 * parity:4 - 2 * parity, :],
                                  xn[:, :, ds(512 * g, 512)], ALU.add).then_inc(taken, 1)

            dve.wait_ge(x_again, 16)
            group_round(T_OUT, 0, take_out, first=True, skip=2)
            with dve.Fori(1, 2) as i:
                group_round(T_OUT, i, take_out)
            take_out(3, 1)
            dve.drain().then_inc(h_ready, 1)
            rest_tile(dve, *tile_at(T_PQ, 0, 4, 0)[:3])
            dve_norm(dve, 1, 4, TB + 8)
            rest_tile(dve, *tile_at(T_PQ, 0, 4, 1)[:3])
            dve_turn(dve, 2, 1)

            def take_query(c, parity):
                dve.wait_ge(lo_used, T_PQ + 2 * c + 2)
                dve.tensor_scalar(query_t[:, ds(c, 1), :], ps[:, parity:parity + 1, 0:SEQ], 1.0, None,
                                  ALU.mult).then_inc(taken, 1)

            chunk_round(T_PQ, 0, lambda i, c: c and take_query(0, 0), skip=2)
            with dve.Fori(1, PQ_CHUNKS // 2) as i:
                chunk_round(T_PQ, i, lambda i, c: take_query(2 * i + c - 1, 1 - c))
            take_query(PQ_CHUNKS - 1, 1)

            dve.wait_ge(scores_ready, 8)
            with dve.Fori(0, PK_HEADS * TB // 4) as i:
                for u in range(4):
                    unit = 4 * i + u

                    def tile(k):
                        rest_tile(dve, *tile_at(T_U, i, 28, 7 * u + k)[:3])

                    def sixteen(values, work, tops, index):
                        for v, t in zip(values, tops):
                            dve.max(t[:, 0:8], v)
                        dve.drain()
                        for v, w, t, x in zip(values, work, tops, index):
                            dve.max_index(x[:, 0:8], t[:, 0:8], v)
                            dve.match_replace(w, t[:, 0:8], v, LOWEST)
                        dve.drain()
                        yield
                        for w, t in zip(work, tops):
                            dve.max(t[:, 8:16], w)
                        dve.drain()
                        for w, t, x in zip(work, tops, index):
                            dve.max_index(x[:, 8:16], t[:, 8:16], w)
                        dve.drain()

                    tile(0)
                    dve.tensor_copy(key_in, scores[:, ds(unit, 1)].rearrange("p a k n -> p (a k) n"))
                    dve.drain()
                    for _ in sixteen([key_in[:, k] for k in range(2)], [key_work[:, k] for k in range(2)],
                                     [key_top[:, k] for k in range(2)], [key_index[:, k] for k in range(2)]):
                        tile(1)
                    tile(2)
                    dve.tensor_copy(key_index_f, key_index)
                    dve.tensor_tensor(cand, key_top[:, 0].unsqueeze(2).broadcast_to([P, TOPK, TOPK]),
                                      key_top[:, 1].unsqueeze(1).broadcast_to([P, TOPK, TOPK]), ALU.add)
                    dve.drain()
                    cand_row = cand.rearrange("p a b -> p (a b)")
                    for _ in sixteen([cand_row], [cand_work], [best], [best_index]):
                        tile(3)
                    tile(4)
                    dve.tensor_copy(best_all[:, ds(unit, 1), :], best.unsqueeze(1))
                    dve.tensor_copy(best_index_f, best_index)
                    dve.drain()
                    dve.tensor_scalar(ranks_f[:, 0], best_index_f, 1.0 / TOPK, -(TOPK - 1) / (2 * TOPK), ALU.mult, ALU.add)
                    dve.drain()
                    dve.tensor_scalar(ranks_f[:, 0], ranks_f[:, 0], ROUNDER, None, ALU.add)
                    dve.drain()
                    dve.tensor_scalar(ranks_f[:, 0], ranks_f[:, 0], -ROUNDER, None, ALU.add)
                    dve.drain()
                    dve.scalar_tensor_tensor(ranks_f[:, 1], ranks_f[:, 0], -float(TOPK), best_index_f, ALU.mult, ALU.add)
                    dve.drain()
                    dve.tensor_tensor(picked, iota[:, 0:TOPK].unsqueeze(1).unsqueeze(1).broadcast_to([P, 2, TOPK, TOPK]),
                                      ranks_f.unsqueeze(3).broadcast_to([P, 2, TOPK, TOPK]), ALU.is_equal)
                    dve.drain()
                    tile(5)
                    dve.tensor_tensor(picked, picked, key_index_f.unsqueeze(2).broadcast_to([P, 2, TOPK, TOPK]), ALU.mult)
                    dve.drain()
                    for k in range(2):
                        dve.tensor_reduce(picks_all[:, k, ds(unit, 1), :], picked[:, k], AX_X, ALU.add)
                    dve.drain()
                    tile(6)

            def plain(start, stop):
                with dve.Fori(start // 2, stop // 2) as i:
                    for k in range(4):
                        rest_tile(dve, *tile_at(T_U, i, 4, k)[:3])

            top_first = best_all[:, :, 0:1].broadcast_to([P, 16, TOPK])
            dve.tensor_tensor(gates3, best_all, top_first, ALU.subtract).then_inc(gates_in, 1)
            plain(TOPK_CHUNKS, TOPK_CHUNKS + 2)
            dve.wait_ge(gates_exp, 1)
            dve.tensor_reduce(gate_sum, gates3, AX_X, ALU.add)
            dve.drain()
            dve.reciprocal(gate_sum, gate_sum)
            dve.drain()
            dve.tensor_tensor(gates3, gates3, gate_sum.unsqueeze(2).broadcast_to([P, 16, TOPK]),
                              ALU.mult).then_inc(gates_ready, 1)
            plain(TOPK_CHUNKS + 2, TOPK_CHUNKS + 6)
            dve.wait_ge(sel_turned, 1)
            dve.tensor_copy(sel1_t[:], ps[:, 6, 0:SEQ])
            dve.tensor_copy(sel2_t[:], ps[:, 6, SEQ:2 * SEQ])
            dve.tensor_copy(gate_t[:], ps[:, 7, 0:SEQ])
            dve.drain().then_inc(sel_ready, 1)
            for part in range(3):
                dve.tensor_copy(gate_parts[:, part], gate_t[:])
                dve.drain()
                if part < 2:
                    dve.tensor_tensor(gate_t[:], gate_t[:], gate_parts[:, part], ALU.subtract)
                    dve.drain()
            plain(TOPK_CHUNKS + 6, CHUNKS // 2)

            def second_keys(q, slot, half):
                dve.drain()
                dve.wait_ge(gates_summed, q + GROUPS * half + 1)
                dve.tensor_tensor(equal2, iota[:, half * HALF_KEYS:(half + 1) * HALF_KEYS].unsqueeze(1)
                                  .broadcast_to([P, 4, HALF_KEYS]),
                                  sel2_t[:, ds(4 * q, 4)].unsqueeze(2).broadcast_to([P, 4, HALF_KEYS]), ALU.is_equal)
                dve.drain()
                dve.tensor_tensor(onehot2[:, slot], equal2.unsqueeze(2).broadcast_to([P, 4, 3, HALF_KEYS]),
                                  gate_parts[:, :, ds(4 * q, 4)].rearrange("p s t -> p t s").unsqueeze(3)
                                  .broadcast_to([P, 4, 3, HALF_KEYS]), ALU.mult).then_inc(onehot2_ready, 1)

            def apply_gates(q, slot, half):
                dve.wait_ge(gates_summed, q + GROUPS * half + 3)
                a = experts[:, half * HALF_KEYS:(half + 1) * HALF_KEYS, ds(4 * q, 4)]
                g = ps[:, 4 + slot, 0:4 * HALF_KEYS].rearrange("p (t c) -> p c t", t=4)
                dve.tensor_tensor(a, a, g, ALU.mult).then_inc(gates_applied, 1)

            dve.sem_inc(gates_applied, 2)
            dve.wait_ge(expert_bank, CHUNKS // 2 + 2)
            def expert_tiles(i, first=False):
                for c in range(2):
                    q = 2 * i + c - CHUNKS // 2
                    rest_tile(dve, *tile_at(T_U, i, 4, 2 * c)[:3])
                    second_keys(q, c, 0)
                    rest_tile(dve, *tile_at(T_U, i, 4, 2 * c + 1)[:3])
                    if not first:
                        apply_gates(q - 2, c, 0)

            expert_tiles(CHUNKS // 4, first=True)
            with dve.Fori(CHUNKS // 4 + 1, CHUNKS // 2) as i:
                expert_tiles(i)
            apply_gates(GROUPS - 2, 0, 0)
            apply_gates(GROUPS - 1, 1, 0)

            def value_tile(half, i, c, late=0):
                v = CHUNKS * half + 4 * i + c
                dve.wait_ge(stage_hi_ready, v + 1)
                dve.tensor_tensor(stage_lo[:, c % 2:c % 2 + 1, :], experts[:, ds(4 * i + c, 1), :],
                                  stage_hi[:, c % 2:c % 2 + 1, :].bitcast(F32), ALU.subtract).then_inc(stage_lo_ready, 1)
                rest_tile(dve, T_V + v + late, c % RAW, c % SPLIT)

            def gated_values(i, first=False):
                for c in range(4):
                    rest_tile(dve, T_V + 4 * i + c, c % RAW, c % SPLIT)
                    second_keys(4 * i + c, c % 2, 1)
                    if not (first and c < 2):
                        apply_gates(4 * i + c - 2, c % 2, 1)

            gated_values(0, first=True)
            with dve.Fori(1, CHUNKS // 8) as i:
                gated_values(i)
            apply_gates(GROUPS - 2, 0, 1)
            apply_gates(GROUPS - 1, 1, 1)
            dve.wait_ge(stage_lo_ready, CHUNKS // 2)
            with dve.Fori(CHUNKS // 8, CHUNKS // 4) as i:
                for c in range(4):
                    value_tile(0, i, c)
            with dve.Fori(0, PLE_CHUNK // 4 - 4) as i:
                for c in range(4):
                    value_tile(1, i, c)

            def add_experts(half):
                for tb in range(TB):
                    dst = xh[:, tb, half * 1024:(half + 1) * 1024].rearrange("p (b n) -> p b n", b=2)
                    dve.tensor_tensor(dst, ps[:, 4 * half + 2 * tb:4 * half + 2 * tb + 2, :], dst,
                                      ALU.add).then_inc(taken, 1)

            dve.wait_ge(h_back, 16)
            add_experts(0)
            with dve.Fori(PLE_CHUNK // 4 - 4, PLE_CHUNK // 4) as i:
                for c in range(4):
                    value_tile(1, i, c)
            dve.wait_ge(p_hi_ready, 1)
            dve.tensor_tensor(act_lo[:, 0:2, :], p_rows, act_hi[:, 0:2, :].bitcast(F32),
                              ALU.subtract).then_inc(p_lo_ready, 1)
            for k in range(4):
                rest_tile(dve, *tile_at(T_PLE, 0, 4, k)[:3])
                if k >= 1:
                    take_ple(dve, k - 1)
            with dve.Fori(PLE_CHUNK // 4, PLE_CHUNK // 4 + 1) as i:
                for c in range(4):
                    value_tile(1, i, c, late=4)
                    if c == 0:
                        take_ple(dve, 3)
            with dve.Fori(PLE_CHUNK // 4 + 1, CHUNKS // 4) as i:
                for c in range(4):
                    value_tile(1, i, c, late=4)
            dve.wait_ge(lo_used, T_GATE)
            add_experts(1)
            rest_tile(dve, *tile_at(T_GATE, 0, 4, 0)[:3])
            dve_norm(dve, 2, 2, TB + 8 + 4)
            rest_tile(dve, *tile_at(T_GATE, 0, 4, 1)[:3])
            dve_turn(dve, 3, 2)

            def gate_ple(g):
                dve.wait_ge(sigmoid_ready, g + 1)
                s = gate_sig[:, g % 2]
                dve.tensor_tensor(s, s, ple[:, :, 512 * g:512 * (g + 1)], ALU.mult)

            def add_ple(g):
                dve.drain()
                dst = xh[:, :, 512 * g:512 * (g + 1)]
                dve.tensor_tensor(dst, dst, gate_sig[:, g % 2], ALU.add).then_inc(taken, 1)

            group_round(T_GATE, 0, None, skip=2, between={11: lambda: gate_ple(0), 12: lambda: add_ple(0)})
            group_round(T_GATE, 1, None, between={3: lambda: gate_ple(1), 4: lambda: add_ple(1),
                                                  11: lambda: gate_ple(2), 12: lambda: add_ple(2)})
            gate_ple(3)
            add_ple(3)
            dve.wait_ge(final_landed, 16)
            dve_scale(dve, 3, 4, TB + 8 + 4 + 8)
            dve.sem_inc(scale_ready, 1)
            for tb in (1, 0):
                dve.scalar_tensor_tensor(final[:, tb, 1536:], xh[:, tb, 1536:], stat[:, 14 + tb:15 + tb], final_w[:, 1536:],
                                         ALU.mult, ALU.mult).then_inc(out_ready[tb], 1)
                if tb == 1:
                    dve.wait_ge(weighted, 3)
                    dve.tensor_scalar(final[:, 1, 0:1536], final[:, 1, 0:1536], stat[:, 15:16], None,
                                      ALU.mult).then_inc(out_ready[1], 1)

        @block.gpsimd
        def _(pool):
            pool.wait_ge(keep_landed, 32)
            pool.wait_ge(consts_landed, ALL_CONSTS)
            pool.wait_ge(turned, 8)
            pool.tensor_copy(angle, pos_i)
            pool.drain()
            pool.tensor_scalar(angle, angle, keep[:, C_INVF:C_INVF + 1], 1.0, ALU.mult, ALU.mult)
            pool.drain()
            for out_ap, quarter in ((turns, 0.25), (angle, 0.0)):
                k = trig_k
                pool.tensor_scalar(k, angle, 1.0 / TWO_PI, quarter, ALU.mult, ALU.add)
                pool.drain()
                pool.tensor_scalar(k, k, ROUNDER, 0.0, ALU.add, ALU.add)
                pool.drain()
                pool.tensor_scalar(k, k, -ROUNDER, 0.0, ALU.add, ALU.add)
                pool.drain()
                src = angle
                for part in TWO_PI_PARTS:
                    pool.tensor_scalar(trig_p, k, part, 1.0, ALU.mult, ALU.mult)
                    pool.drain()
                    pool.tensor_tensor(out_ap, src, trig_p, ALU.subtract)
                    pool.drain()
                    src = out_ap
                pool.tensor_scalar(out_ap, out_ap, quarter * TWO_PI, 0.0, ALU.add, ALU.add)
                pool.drain()
                pool.tensor_scalar(out_ap, out_ap, PI_BELOW, -PI_BELOW, ALU.min, ALU.max).then_inc(angles_ready, 1)
                pool.drain()
            pool.wait_ge(taken, IN_CHUNKS)
            pool.wait_ge(trig_ready, 2)
            for x in range(2):
                rotate(pool, 2, x).then_inc(k_rotated, 1)
            pool.wait_ge(rows_silu, 2)
            z = rows[:, 0:2].rearrange("p g b c -> p (g b c)").rearrange("p (n d) -> p n d", d=P)
            pool.tensor_tensor(z, z, dn_w.unsqueeze(1).broadcast_to([P, 16, P]), ALU.mult).then_inc(z_weighted, 1)
            for tb in range(TB):
                pool.wait_ge(ret_scaled, tb + 1)
                r = mixed[:, tb, 1024:2048]
                pool.tensor_tensor(r, r, mixed[:, 0, 0:1024], ALU.mult)
                pool.drain()
                pool.tensor_tensor(r, r, mixed[:, 1, 0:1024], ALU.add)
                pool.drain()
                r2 = r.rearrange("p (g c) -> p g c", g=2)
                pool.tensor_tensor(r2, r2, rows[:, 4:6, tb, :], ALU.mult).then_inc(ret_done, 1)
            meet(pool)

            def first_keys(half, i):
                pool.drain()
                pool.tensor_copy(sel4[:].rearrange("p s t -> p (s t)"), sel1_t[:, ds(8 * i, 8)])
                pool.drain()
                for slot in range(2):
                    if half == 1:
                        v = 2 * i + slot
                        hold(pool, "pool", stage_hi_ready, v + 1)
                        pool.tensor_tensor(stage_lo[:, slot:slot + 1, :], experts[:, ds(v, 1), :],
                                           stage_hi[:, slot:slot + 1, :].bitcast(F32),
                                           ALU.subtract).then_inc(stage_lo_ready, 1)
                    hold(pool, "pool", gates_summed, 2 * i + slot + GROUPS * half + 1)
                    for t in range(2 if half == 1 else 4):
                        e = pool.tensor_scalar(onehot1[:, slot, t], iota, sel4[:, slot, t:t + 1], None, ALU.is_equal)
                    e.then_inc(onehot1_ready, 1)

            pool.wait_ge(sel_ready, 1)
            for half in range(2):
                with pool.Fori(0, GROUPS // 2) as i:
                    first_keys(half, i)
            pool.wait_ge(final_landed, 16)
            for g in range(3):
                pool.wait_ge(taken, TAKEN_H + g + 1)
                c = slice(512 * g, 512 * (g + 1))
                pool.tensor_tensor(final[:, :, c], xh[:, :, c], final_w[:, c].unsqueeze(1).broadcast_to([P, TB, 512]),
                                   ALU.mult).then_inc(weighted, 1)

        @block.tensor
        def _(pe):
            pe.wait_ge(x_landed[0], 16)
            pe.wait_ge(x_landed[1], 16)
            pe.wait_ge(diag_ready, 1)
            pe_turn(pe, xh)

            def column_chunk(base, i, c, turn=None):
                for k in range(2):
                    n, _, use, _ = tile_at(base, i, 4, 2 * c + k)
                    column_tile(pe, n, use, k, ps[:, c, 0:SEQ], turn=turn)

            column_chunk(0, 0, 0, turn=0)
            column_chunk(0, 0, 1)
            def ab_products(half):
                pe.wait_ge(ab_hi_ready, half + 1)
                pe.wait_ge(ab_lo_ready, half + 1)
                for d8 in range(8):
                    d, o = 8 * half + d8, ps[0:64, 4, 0:SEQ]
                    pe.matmul(o, ab_part(stage_hi)[:, d8], act_hi[:, d, :], start=(d == 0), stop=False)
                    pe.matmul(o, ab_part(stage_hi)[:, d8], act_lo[:, d, :], start=False, stop=False)
                    mm = pe.matmul(o, ab_part(stage_lo)[:, d8], act_hi[:, d, :], start=False, stop=(d == DC - 1))
                mm.then_inc(ab_used, 1)

            for start, stop in ((1, AB_ROUND), (AB_ROUND, IN_CHUNKS // 2)):
                with pe.Fori(start, stop) as i:
                    for c in range(2):
                        pe.wait_ge(taken, 2 * i + c - 1)
                        column_chunk(0, i, c)
                if start == 1:
                    ab_products(0)
            ab_products(1)

            def row_groups(base, count, taken_before, turn=None, between=None):
                def row_round(i, turn):
                    for g in range(2):
                        pe.wait_ge(taken, taken_before - 1 + 2 * i + g)
                        for k in range(8):
                            n, _, use, _ = tile_at(base, i, 16, 8 * g + k)
                            row_tile(pe, n, use, k, [ps[:, 2 - 2 * g + tb, :] for tb in range(TB)],
                                     turn=turn if g == 0 else None)
                            if between:
                                between(i, 8 * g + k)

                row_round(0, turn)
                with pe.Fori(1, count // 2) as i:
                    row_round(i, None)

            def sum_squares(i, k):
                if not (isinstance(i, int) and i == 0) and k % 4 == 1:
                    p = 4 * i - 4 + k // 4
                    pe.wait_ge(qk_squared, p + 1)
                    pe.matmul(ps[:, 5, :], ones_m, squares, start=True, stop=True).then_inc(qk_summed, 1)

            row_groups(T_ROW, ROW_GROUPS, IN_CHUNKS, between=sum_squares)

            pe.wait_ge(decay_row, 1)
            pe.wait_ge(taken, IN_CHUNKS + ROW_GROUPS - 1)
            for b in range(TB):
                mm = pe.transpose(ps[:, 3, 40 * b:40 * b + 40], gb[0:40, b * P:(b + 1) * P], ident[0:40, 0:40])
            mm.then_inc(decay_col, 1)
            pe.wait_ge(selector_ready, 1)
            pe.wait_ge(ab_copied, 1)
            pe.wait_ge(qk_root, 8)
            for h in range(DN_HEADS):
                mm = pe.matmul(spread[:, h, :], selector[:, h, :], gb[0:8, :], start=True, stop=True)
            mm.then_inc(decay_spread, 1)
            pe.wait_ge(q_rotated, 2)
            pe.wait_ge(k_rotated, 2)
            pe.wait_ge(taken, IN_CHUNKS + ROW_GROUPS)
            for h in range(RET_HEADS):
                if h == 3:
                    pe.wait_ge(decay_cols_ready, 1)
                if h == 4:
                    pe.wait_ge(expo_ready, 8)
                g, rowsl = h // 4, slice(HALF * (h % 4), HALF * (h % 4 + 1))
                for m, (c0, c1), at in ((0, (0, SEQ), 0), (1, (P, SEQ), SEQ)):
                    for x12 in range(2):
                        mm = pe.matmul(ps[:, h, at:at + c1 - c0], rot[rowsl, 2 + x12, g, m * P:(m + 1) * P],
                                       rot[rowsl, x12, g, c0:c1], start=(x12 == 0), stop=(x12 == 1))
                mm.then_inc(ret_scores, 1)

            def turn_kv(b):
                for g in range(2):
                    for kv in range(2):
                        for j in range(4):
                            mm = pe.transpose(psg[:, 2 * g + kv, j], channel(1 + kv, 2 * b + g, j), ident)
                        mm.then_inc(kv_turned, 1)

            pe.wait_ge(qk_normed, 8)
            pe.wait_ge(ret_masked, 4)
            turn_kv(0)
            pe.wait_ge(ret_masked, 8)
            for tb in range(TB):
                for h in range(RET_HEADS):
                    o = ps[:, 4 + 2 * tb + h // 4, (h % 4) * P:(h % 4 + 1) * P]
                    for m in range(tb + 1):
                        mm = pe.matmul(o, att_ret[:, h, (tb + m) * P:(tb + m + 1) * P],
                                       rows[:, 2 + h // 4, m, (h % 4) * P:(h % 4 + 1) * P],
                                       start=(m == 0), stop=(m == tb))
                mm.then_inc(ret_out, 1)
            pe.wait_ge(k_rows, 2)
            pe.wait_ge(v_rows, 2)
            turn_kv(1)
            pe.wait_ge(k_rows, 4)
            pe.wait_ge(v_rows, 4)
            for g in range(4):
                for j in range(4):
                    mm = pe.matmul(psg[:, g, j], channel(1, g, j), channel(1, g, j), start=True, stop=True)
                mm.then_inc(kk_done, 1)
            pe.wait_ge(ret_copied, 2)
            for g in range(4):
                for j in range(4):
                    mm = pe.matmul(psg[:, 4 + g, j], channel(1, g, j), channel(0, g, j), start=True, stop=True)
                mm.then_inc(att_done, 1)
            for g in range(4):
                pe.wait_ge(blocks_ready, g + 1)
                for j in range(4):
                    mm = pe.transpose(psg[:, g, j], blocks[:, g, j], ident)
                mm.then_inc(blocks_turned, 1)
            pe.wait_ge(att_used, 4)
            with pe.Fori(1, LEVELS) as level:
                def inner_products(g):
                    pe.wait_ge(blocks_ready, 4 * level + g + 1)
                    for j in range(4):
                        mm = pe.matmul(psg[:, g, j], blocks[:, g, j], inv_t[:, g, j], start=True, stop=True)
                    mm.then_inc(inner_done, 1)

                def outer_products(g):
                    pe.wait_ge(inner_copied, 4 * level + g - 3)
                    pe.wait_ge(inv_updated, 4 * level + g - 1)
                    for j in range(4):
                        pe.matmul(psg[:, 4 + 2 * (g % 2), j], inner[:, g, j], inv[:, g, j], start=True, stop=True)
                    for j in range(4):
                        mm = pe.matmul(psg[:, 5 + 2 * (g % 2), j], inv[:, g, j], inner[:, g, j], start=True, stop=True)
                    mm.then_inc(outer_done, 1)

                inner_products(0)
                inner_products(1)
                outer_products(0)
                inner_products(2)
                outer_products(1)
                inner_products(3)
                outer_products(2)
                outer_products(3)
            pe.wait_ge(inv_updated, 4 * LEVELS)
            for g in range(2):
                for j in range(4):
                    mm = pe.matmul(psg[:, g, j], inv_t[:, g, j], v_row[0][:, g, j], start=True, stop=True)
                mm.then_inc(new_done, 1)
            pe.wait_ge(kd_ready, 1)
            for g in range(2):
                pe.wait_ge(new_copied, g + 1)
                for j in range(4):
                    mm = pe.matmul(psg[:, 4 + g, j], k_dec[:, g, j], v_new[:, g, j], start=True, stop=True)
                mm.then_inc(state_done, 1)
            for g in range(2):
                for j in range(4):
                    mm = pe.matmul(psg[:, 6 + g, j], att[:, g, j], v_new[:, g, j], start=True, stop=True)
                mm.then_inc(o_done, 1)
            for g in range(2):
                pe.wait_ge(state_copied, g + 1)
                for j in range(4):
                    mm = pe.matmul(psg[:, g, j], channel(1, 2 + g, j), state[:, g, j], start=True, stop=True)
                mm.then_inc(from_state, 1)
            for g in range(2):
                for j in range(4):
                    mm = pe.matmul(psg[:, 2 + g, j], channel(0, 2 + g, j), state[:, g, j], start=True, stop=True)
                mm.then_inc(q_state, 1)
            for g in range(2):
                pe.wait_ge(rhs_ready, g + 1)
                for j in range(4):
                    mm = pe.matmul(psg[:, 4 + g, j], inv_t[:, 2 + g, j], rhs[:, 2 + g, j], start=True, stop=True)
                mm.then_inc(new_done, 1)
            for g in range(2):
                pe.wait_ge(new_copied, g + 3)
                for j in range(4):
                    mm = pe.matmul(psg[:, g, j], att[:, 2 + g, j], v_new[:, 2 + g, j], start=True, stop=True)
                mm.then_inc(o_done, 1)
            meet(pe)
            pe_turn(pe, mixed, scaled=False)
            row_groups(T_OUT, D // 512, IN_CHUNKS + ROW_GROUPS, turn=1)
            pe.wait_ge(diag_ready, 2)
            pe_turn(pe, xh)
            column_chunk(T_PQ, 0, 0, turn=2)
            column_chunk(T_PQ, 0, 1)
            with pe.Fori(1, PQ_CHUNKS // 2) as i:
                for c in range(2):
                    pe.wait_ge(taken, TAKEN_OUT - 1 + 2 * i + c)
                    column_chunk(T_PQ, i, c)
            pe.wait_ge(taken, TAKEN_OUT + PQ_CHUNKS)
            pe.wait_ge(keys_landed, 16)
            for b in range(8):
                for k in range(4):
                    hp = 4 * (b % 4) + k
                    mm = pe.matmul(ps[:, b, k * P:(k + 1) * P], query_t[:, hp, (b // 4) * P:(b // 4 + 1) * P],
                                   keys_t[:, hp, :], start=True, stop=True)
                mm.then_inc(scores_done, 1)

            def expert_round(i, and_then=None):
                for c in range(2):
                    pe.wait_ge(expert_bank, 2 * i + c + 1)
                    column_chunk(T_U, i, c)
                    if and_then:
                        and_then(i, c)

            def expert_chunks(start, stop, and_then=None):
                with pe.Fori(start // 2, stop // 2) as i:
                    expert_round(i, and_then)

            def sum_gates(n, slot, late=None):
                pe.wait_ge(onehot1_ready, n + 1)
                if late is not None:
                    pe.wait_ge(onehot1_late, late + 1)
                pe.wait_ge(onehot2_ready, n + 1)
                pe.wait_ge(gates_applied, n + 1)
                for t in range(4):
                    o = ps[:, 4 + slot, t * HALF_KEYS:(t + 1) * HALF_KEYS]
                    for part in range(3):
                        mm = pe.matmul(o, onehot1[:, slot, t], onehot2[:, slot, t, part], start=(part == 0),
                                       stop=(part == 2))
                mm.then_inc(gates_summed, 1)

            pe.sem_inc(gates_summed, 2)
            expert_chunks(0, TOPK_CHUNKS + 4)
            pe.wait_ge(gates_ready, 1)
            for tb in range(TB):
                for k in range(2):
                    pe.transpose(ps[:, 6, (2 * k + tb) * P:(2 * k + tb + 1) * P],
                                 picks_all[:, k, 8 * tb:8 * tb + 8].rearrange("p u r -> p (u r)"), ident)
                mm = pe.transpose(ps[:, 7, tb * P:(tb + 1) * P],
                                  gates3[:, 8 * tb:8 * tb + 8].rearrange("p u r -> p (u r)"), ident)
            mm.then_inc(sel_turned, 1)
            expert_chunks(TOPK_CHUNKS + 4, CHUNKS // 2)
            expert_round(CHUNKS // 4, lambda i, c: c and sum_gates(0, 0))
            expert_chunks(CHUNKS // 2 + 2, CHUNKS, lambda i, c: sum_gates(2 * i + c - CHUNKS // 2 - 1, 1 - c))
            sum_gates(GROUPS - 1, 1)

            def value_round(half, i, and_then=None, first=False, late=0):
                for c in range(4):
                    v, use = CHUNKS * half + 4 * i + c, c % SPLIT
                    pe.wait_ge(hi_ready, T_V + v + late + 1)
                    pe.wait_ge(stage_lo_ready, v + 1)
                    for k, a in enumerate((stage_hi, stage_lo)):
                        for tb in range(TB):
                            for b in range(2):
                                mm = pe.matmul(ps[:, 4 * half + 2 * tb + b, :], a[:, use, tb * P:(tb + 1) * P],
                                               hi[:, use, b * 512:(b + 1) * 512], start=(first and c == 0 and k == 0),
                                               stop=False, skip_group_check=True)
                    mm.then_inc(hi_used, 1)
                    pe.wait_ge(lo_ready, T_V + v + late + 1)
                    for tb in range(TB):
                        for b in range(2):
                            mm = pe.matmul(ps[:, 4 * half + 2 * tb + b, :], stage_hi[:, use, tb * P:(tb + 1) * P],
                                           lo[:, use, b * 512:(b + 1) * 512], start=False, stop=False,
                                           skip_group_check=True)
                    mm.then_inc(lo_used, 1)
                    if and_then and not (first and c == 0):
                        and_then(4 * i + c - 1, (c - 1) % 2)

            def gates_too(v, slot):
                sum_gates(v + GROUPS, slot, late=v)

            pe.wait_ge(expert_bank, CHUNKS + 2)
            value_round(0, 0, gates_too, first=True)
            with pe.Fori(1, CHUNKS // 8) as i:
                value_round(0, i, gates_too)
            gates_too(GROUPS - 1, 1)
            with pe.Fori(CHUNKS // 8, CHUNKS // 4) as i:
                value_round(0, i)
            pe.wait_ge(gates_applied, 2 * GROUPS + 2)
            value_round(1, 0, first=True)
            with pe.Fori(1, PLE_CHUNK // 4) as i:
                value_round(1, i)
            pe.wait_ge(p_lo_ready, 1)
            for g, before in enumerate((TAKEN_H0, TAKEN_H0, TAKEN_H0 + 1, TAKEN_H0 + 2)):
                n, _, use, _ = tile_at(T_PLE, 0, 4, g)
                pe.wait_ge(taken, before)
                row_tile(pe, n, use, 0, [ps[:, 2 - 2 * (g % 2) + tb, :] for tb in range(TB)], last=0)
            with pe.Fori(PLE_CHUNK // 4, CHUNKS // 4) as i:
                value_round(1, i, late=4)
            pe.wait_ge(taken, TAKEN_H)
            pe.wait_ge(diag_ready, 3)
            pe_turn(pe, xh)
            row_groups(T_GATE, D // 512, TAKEN_H, turn=3)


_OUTS = [((1, SEQ, D), "float32")]


def kernel(**inputs):
    import numpy as _np
    import concourse.bacc as _bacc
    from concourse import mybir as _mybir
    from concourse.bass_utils import run_bass_kernel_spmd as _run

    a = {k: _np.asarray(v) for k, v in inputs.items()}

    def column_tiles(w):
        n = w.shape[1] // P
        return _np.ascontiguousarray(w.reshape(2, 8, P, n, P).transpose(3, 0, 2, 1, 4).reshape(2 * n, P, TILE))

    def row_tiles(w):
        k, n = w.shape[0] // 256, w.shape[1] // 512
        return _np.ascontiguousarray(w.reshape(k, 2, P, n, 512).transpose(3, 0, 2, 1, 4).reshape(n * k, P, TILE))

    def by_column(v):
        return v.reshape(-1, P).T

    w_in = a["w_in"][0]
    at = _np.cumsum([0, CONV_CH, 1024, 8, 8, 512, 512, 1024, 1024])
    conv, z, ga, gb, rq, rk, rv, rg = (w_in[:, at[i]:at[i + 1]] for i in range(8))
    halves = [r.reshape(D, RET_HEADS, 2, HALF).transpose(0, 2, 1, 3).reshape(D, 512) for r in (rq, rk)]
    w_ab = _np.zeros((P, DC, 64), _np.float32)
    w_ab[:, :, 0:8] = ga.reshape(DC, P, 8).transpose(1, 0, 2)
    w_ab[:, :, 32:40] = gb.reshape(DC, P, 8).transpose(1, 0, 2)
    keep_c, mix_c = shape_consts()
    u = a["expert_u"][0].reshape(N_KEYS, N_KEYS, 2, 8, P)
    v = a["expert_v"][0].reshape(N_KEYS, N_KEYS, 2, TILE)
    arrays = {
        "x": a["x"][0],
        "w_in_cols": column_tiles(_np.concatenate([conv] + halves, axis=1)),
        "w_in_rows": row_tiles(_np.concatenate([z, rv, rg], axis=1)),
        "w_ab": w_ab,
        "w_out": row_tiles(a["w_out"][0]),
        "w_pq": column_tiles(a["w_pq"][0]),
        "expert_u": u.transpose(1, 2, 4, 3, 0).reshape(2 * CHUNKS, P, TILE),
        "expert_v": v.transpose(2, 1, 0, 3).reshape(2 * CHUNKS, P, TILE),
        "w_gate": row_tiles(a["w_ple_gate"][0]),
        "w_ple": row_tiles(a["w_ple_proj"][0]),
        "p_t": a["p"][0, 0].reshape(SEQ, 2, P).transpose(2, 1, 0),
        "positions": a["positions"][0],
        "keep_c": keep_c,
        "mix_c": mix_c,
        "norm_cols": _np.stack([by_column(a[k][0]) for k in ("norm_mix", "norm_ffn", "norm_ple")], axis=1),
        "conv_cols": a["conv_w"][0].reshape(CONV_CHUNKS, P, CONV_W).transpose(1, 0, 2).reshape(P, -1),
        "sub_keys_t": a["sub_keys"][0].reshape(2 * PK_HEADS, N_KEYS, P).transpose(2, 0, 1),
        "ab_cols": _np.stack([a["a_log"][0], a["dt_bias"][0]], axis=1),
        "dn_norm": a["dn_norm"][0],
        "ret_gn_w": a["ret_gn_w"][0],
        "ret_gn_b": a["ret_gn_b"][0],
        "norm_final": a["norm_final"],
    }
    arrays = {"in_" + k: _np.ascontiguousarray(v) for k, v in arrays.items()}
    nc = _bacc.Bacc("TRN2", target_bir_lowering=False, num_devices=1)
    args = [nc.dram_tensor(k, v.shape, _mybir.dt.from_np(v.dtype), kind="ExternalInput").ap()
            for k, v in arrays.items()]
    args.append(nc.dram_tensor("out_0", (SEQ, D), F32, kind="ExternalOutput").ap())
    args.append(nc.dram_tensor("h_spill", (SEQ, D), F32, kind="Internal").ap())
    build(nc, *args)
    r = _run(nc, [arrays], core_ids=[0])
    return r.results[0]["out_0"].reshape(1, SEQ, D)
```
